# Optimizing a Trainium2 kernel written in Bass

```python
import jax, jax.numpy as jnp
from jax import lax
import numpy as np

D_MODEL = 1024
BATCH = 1
SEQ = 512
DEPTH = 1

EPS = 1e-6
D_FF = 2816
N_MOD = 9
GLA_HEADS = 4
GLA_DK = D_MODEL // 2
GLA_DV = D_MODEL
GLA_HK = GLA_DK // GLA_HEADS
GLA_HV = GLA_DV // GLA_HEADS
GLA_RANK = 16
GLA_TAU = 16.0
GLA_CHUNK = 64
FOX_HEADS = 16
FOX_HD = D_MODEL // FOX_HEADS
FOX_W = FOX_HEADS * FOX_HD
Q_BLOCK = 128
SPLITS = (GLA_DK, GLA_DK, GLA_DV, GLA_RANK, GLA_DV, FOX_W, FOX_W, FOX_W, FOX_HEADS, D_MODEL, D_MODEL)
IN_COLS = 2 * GLA_DK + 2 * GLA_DV + GLA_RANK + 3 * FOX_W + FOX_HEADS + 2 * D_MODEL


def rmsnorm(x, g):
    xf = x.astype(jnp.float32)
    y = xf * lax.rsqrt(jnp.mean(xf * xf, axis=-1, keepdims=True) + EPS)
    return (y * g.astype(jnp.float32)).astype(x.dtype)

def swiglu(h, w_gu, w_dn):
    g, u = jnp.split(h @ w_gu, 2, axis=-1)
    return (jax.nn.silu(g) * u) @ w_dn

def gla_chunked(q, k, v, log_a):
    B, H, T, dk = q.shape
    dv = v.shape[-1]
    C = GLA_CHUNK
    N = T // C

    def to_chunks(a):
        return a.reshape(B, H, N, C, a.shape[-1]).transpose(2, 0, 1, 3, 4)

    qc, kc, vc, gc = to_chunks(q), to_chunks(k), to_chunks(v), to_chunks(log_a)
    causal = jnp.tril(jnp.ones((C, C), dtype=bool))[:, :, None]

    def step(S, inp):
        qi, ki, vi, gi = inp
        b = jnp.cumsum(gi, axis=2)
        o_inter = jnp.einsum('bhtd,bhde->bhte', qi * jnp.exp(b), S)
        diff = b[:, :, :, None, :] - b[:, :, None, :, :]
        decay = jnp.exp(jnp.where(causal, diff, -jnp.inf))
        A = jnp.einsum('bhtd,bhsd,bhtsd->bhts', qi, ki, decay)
        o = o_inter + jnp.einsum('bhts,bhse->bhte', A, vi)
        b_last = b[:, :, -1:, :]
        S_new = jnp.exp(b_last[:, :, 0, :, None]) * S + jnp.einsum(
            'bhsd,bhse->bhde', ki * jnp.exp(b_last - b), vi)
        return S_new, o

    S0 = jnp.zeros((B, H, dk, dv), jnp.float32)
    _, o = lax.scan(step, S0, (qc, kc, vc, gc))
    return o.transpose(1, 2, 0, 3, 4).reshape(B, H, T, dv)

def fox_attention(q, k, v, logf):
    B, H, T, hd = q.shape
    F = jnp.cumsum(logf, axis=-1)
    nb = T // Q_BLOCK
    qb = q.reshape(B, H, nb, Q_BLOCK, hd).transpose(2, 0, 1, 3, 4)
    Fb = F.reshape(B, H, nb, Q_BLOCK).transpose(2, 0, 1, 3)
    kpos = jnp.arange(T)
    scale = hd ** -0.5

    def block(args):
        qi, Fi, i = args
        s = jnp.einsum('bhqd,bhkd->bhqk', qi, k).astype(jnp.float32) * scale
        s = s + Fi[..., None] - F[:, :, None, :]
        qpos = i * Q_BLOCK + jnp.arange(Q_BLOCK)
        s = jnp.where(kpos[None, :] <= qpos[:, None], s, -jnp.inf)
        p = jax.nn.softmax(s, axis=-1)
        return jnp.einsum('bhqk,bhkd->bhqd', p.astype(v.dtype), v)

    o = lax.map(block, (qb, Fb, jnp.arange(nb)))
    return o.transpose(1, 2, 0, 3, 4).reshape(B, H, T, hd)

def token_mixer(h, w_in, w_a2, b_a, b_f, g_gla, w_pa, w_pb, w_out):
    B, T, _ = h.shape
    f32 = jnp.float32
    z = h @ w_in
    cuts = np.cumsum(SPLITS)[:-1].tolist()
    q_a, k_a, v_a, a_low, r_a, q_b, k_b, v_b, f_b, gate_a, gate_b = jnp.split(z, cuts, axis=-1)

    def heads(t, n):
        return t.reshape(B, T, n, -1).transpose(0, 2, 1, 3)

    log_a = jax.nn.log_sigmoid((a_low @ w_a2 + b_a).astype(f32)) / GLA_TAU
    o_a = gla_chunked(heads(q_a.astype(f32) * (GLA_HK ** -0.5), GLA_HEADS),
                      heads(k_a.astype(f32), GLA_HEADS),
                      heads(v_a.astype(f32), GLA_HEADS),
                      heads(log_a, GLA_HEADS))
    o_a = rmsnorm(o_a.transpose(0, 2, 1, 3), g_gla.reshape(GLA_HEADS, GLA_HV))
    o_a = o_a.astype(h.dtype).reshape(B, T, GLA_DV) * jax.nn.silu(r_a)

    logf = jax.nn.log_sigmoid((f_b + b_f).astype(f32)).transpose(0, 2, 1)
    o_b = fox_attention(heads(q_b, FOX_HEADS), heads(k_b, FOX_HEADS), heads(v_b, FOX_HEADS), logf)
    o_b = o_b.transpose(0, 2, 1, 3).reshape(B, T, FOX_W)

    merged = jax.nn.sigmoid(gate_a) * (o_a @ w_pa) + jax.nn.sigmoid(gate_b) * (o_b @ w_pb)
    return merged @ w_out

def first_inputs(seed: int = 0) -> dict:
    key = jax.random.key(seed)
    ks = jax.random.split(key, 20)
    L, D = DEPTH, D_MODEL
    nrm = jax.random.normal

    def w(k, shape, fan_in):
        return nrm(k, shape, jnp.float32) * fan_in ** -0.5

    return {
        "x": nrm(ks[0], (BATCH, SEQ, D), jnp.float32),
        "c": nrm(ks[1], (BATCH, D), jnp.float32),
        "w_ada": w(ks[2], (L, D, N_MOD * D), D) * 0.5,
        "b_ada": 0.02 * nrm(ks[3], (L, N_MOD * D), jnp.float32),
        "g_pre": 1.0 + 0.05 * nrm(ks[4], (L, 3, D), jnp.float32),
        "g_post": 1.0 + 0.05 * nrm(ks[5], (L, 3, D), jnp.float32),
        "w_gu1": w(ks[6], (L, D, 2 * D_FF), D),
        "w_dn1": w(ks[7], (L, D_FF, D), D_FF),
        "w_gu2": w(ks[8], (L, D, 2 * D_FF), D),
        "w_dn2": w(ks[9], (L, D_FF, D), D_FF),
        "w_in": w(ks[10], (L, D, IN_COLS), D),
        "w_a2": w(ks[11], (L, GLA_RANK, GLA_DK), GLA_RANK),
        "b_a": 0.1 * nrm(ks[12], (L, GLA_DK), jnp.float32),
        "b_f": 1.0 + 0.1 * nrm(ks[13], (L, FOX_HEADS), jnp.float32),
        "g_gla": 1.0 + 0.05 * nrm(ks[14], (L, GLA_DV), jnp.float32),
        "w_pa": w(ks[15], (L, GLA_DV, D), GLA_DV),
        "w_pb": w(ks[16], (L, FOX_W, D), FOX_W),
        "w_out": w(ks[17], (L, D, D), D),
    }

def first_block(x, c, w_ada, b_ada, g_pre, g_post, w_gu1, w_dn1, w_gu2, w_dn2,
              w_in, w_a2, b_a, b_f, g_gla, w_pa, w_pb, w_out):
    B = x.shape[0]
    for l in range(DEPTH):
        mods = (jax.nn.silu(c) @ w_ada[l] + b_ada[l]).reshape(B, N_MOD, 1, D_MODEL)
        sh1, sc1, gt1, sh2, sc2, gt2, sh3, sc3, gt3 = [mods[:, i] for i in range(N_MOD)]

        h = rmsnorm(x, g_pre[l, 0]) * (1 + sc1) + sh1
        x = x + 0.5 * gt1 * rmsnorm(swiglu(h, w_gu1[l], w_dn1[l]), g_post[l, 0])

        h = rmsnorm(x, g_pre[l, 1]) * (1 + sc2) + sh2
        y = token_mixer(h, w_in[l], w_a2[l], b_a[l], b_f[l], g_gla[l], w_pa[l], w_pb[l], w_out[l])
        x = x + gt2 * rmsnorm(y, g_post[l, 1])

        h = rmsnorm(x, g_pre[l, 2]) * (1 + sc3) + sh3
        x = x + 0.5 * gt3 * rmsnorm(swiglu(h, w_gu2[l], w_dn2[l]), g_post[l, 2])
    return x


NSA_HEADS = 8
NSA_GROUPS = 2
NSA_HPG = NSA_HEADS // NSA_GROUPS
NSA_DH = 64
CMP_STRIDE = 16
CMP_LEN = 2 * CMP_STRIDE
CMP_HIDDEN = 128
SEL_BLOCK = 64
SEL_TOPK = 16
WINDOW = 512
NSA_QBLOCK = 64
FORCE_BONUS = 1e4
RET_HEADS = 8
RET_DK = 64
RET_DV = 64
RET_CHUNK = 128
ROPE_BASE = 10000.0
NEG = -1e30

NSA_QW = NSA_HEADS * NSA_DH
NSA_KVW = NSA_GROUPS * NSA_DH
RET_QW = RET_HEADS * RET_DK
RET_VW = RET_HEADS * RET_DV
IN_WIDTHS = [NSA_QW, NSA_KVW, NSA_KVW, NSA_KVW, NSA_KVW, NSA_KVW, NSA_KVW, 3 * NSA_HEADS,
             RET_QW, RET_QW, RET_VW, RET_VW, D_MODEL, D_MODEL]
IN_W = sum(IN_WIDTHS)


def rmsnorm_2(x, w):
    xf = x.astype(jnp.float32)
    y = xf * lax.rsqrt(jnp.mean(xf * xf, axis=-1, keepdims=True) + EPS)
    return (y * w.astype(jnp.float32)).astype(x.dtype)

def modulate(h, shift, scale):
    return h * (1 + scale[:, None, :]) + shift[:, None, :]

def swiglu_2(h, w_in, w_out):
    a, b = jnp.split(h @ w_in, 2, axis=-1)
    return (jax.nn.silu(a) * b) @ w_out

def masked_softmax(s, mask):
    return jax.nn.softmax(jnp.where(mask, s.astype(jnp.float32), NEG), axis=-1)

def rope(x, pos):
    half = x.shape[-1] // 2
    inv = ROPE_BASE ** (-jnp.arange(half, dtype=jnp.float32) / half)
    ang = pos.astype(jnp.float32)[:, None] * inv[None, :]
    cos = jnp.cos(ang)[None, :, None, :]
    sin = jnp.sin(ang)[None, :, None, :]
    x1 = x[..., :half].astype(jnp.float32)
    x2 = x[..., half:].astype(jnp.float32)
    return jnp.concatenate([x1 * cos - x2 * sin, x1 * sin + x2 * cos], axis=-1).astype(x.dtype)

def compress(raw, pe, w1, w2):
    B, S, G, dh = raw.shape
    ch = raw.reshape(B, S // CMP_STRIDE, CMP_STRIDE, G, dh)
    blocks = jnp.concatenate([ch[:, :-1], ch[:, 1:]], axis=2)
    blocks = blocks + pe[None, None, :, None, :]
    nc = blocks.shape[1]
    flat = blocks.transpose(0, 1, 3, 2, 4).reshape(B, nc, G, CMP_LEN * dh)
    return jax.nn.silu(flat @ w1) @ w2

def nsa_attention(q, k_cmp, v_cmp, k_slc, v_slc, k_win, v_win, gates,
                  cmp_k_pe, cmp_k_w1, cmp_k_w2, cmp_v_pe, cmp_v_w1, cmp_v_w2):
    B, S = q.shape[:2]
    G, HPG, dh, QB = NSA_GROUPS, NSA_HPG, NSA_DH, NSA_QBLOCK
    kc = compress(k_cmp, cmp_k_pe, cmp_k_w1, cmp_k_w2)
    vc = compress(v_cmp, cmp_v_pe, cmp_v_w1, cmp_v_w2)
    nc = kc.shape[1]
    ns = S // SEL_BLOCK
    n_sel = min(SEL_TOPK, ns)
    cmp_end = jnp.arange(nc) * CMP_STRIDE + CMP_LEN - 1
    c_start = np.arange(nc) * CMP_STRIDE
    s_start = np.arange(ns) * SEL_BLOCK
    overlap = jnp.asarray((c_start[:, None] < s_start[None, :] + SEL_BLOCK) &
                          (c_start[:, None] + CMP_LEN > s_start[None, :]), dtype=jnp.float32)
    ks_blk = k_slc.reshape(B, ns, SEL_BLOCK, G, dh).transpose(0, 3, 1, 2, 4)
    vs_blk = v_slc.reshape(B, ns, SEL_BLOCK, G, dh).transpose(0, 3, 1, 2, 4)
    kw_pad = jnp.pad(k_win, ((0, 0), (WINDOW, 0), (0, 0), (0, 0)))
    vw_pad = jnp.pad(v_win, ((0, 0), (WINDOW, 0), (0, 0), (0, 0)))
    scale = NSA_DH ** -0.5
    b_ix = jnp.arange(B)[:, None, None, None]
    g_ix = jnp.arange(G)[None, :, None, None]
    j_blk = jnp.arange(ns)
    sel_off = jnp.arange(SEL_BLOCK)

    def block(nb):
        q0 = nb * QB
        t = q0 + jnp.arange(QB)
        qb = lax.dynamic_slice_in_dim(q, q0, QB, axis=1).reshape(B, QB, G, HPG, dh) * scale
        m_c = cmp_end[None, :] <= t[:, None]
        p_c = masked_softmax(jnp.einsum('bqghd,bngd->bghqn', qb, kc), m_c)
        p_c = p_c * jnp.any(m_c, axis=-1)[:, None].astype(jnp.float32)
        o_cmp = jnp.einsum('bghqn,bngd->bqghd', p_c, vc)
        imp = jnp.einsum('bghqn,nj->bgqj', p_c, overlap)
        cur = t // SEL_BLOCK
        forced = (j_blk[None, :] == 0) | (j_blk[None, :] == cur[:, None]) | (j_blk[None, :] == cur[:, None] - 1)
        valid = j_blk[None, :] * SEL_BLOCK <= t[:, None]
        imp = jnp.where(forced, imp + FORCE_BONUS, imp)
        imp = jnp.where(valid, imp, -FORCE_BONUS)
        _, idx = lax.top_k(imp, n_sel)
        kg = ks_blk[b_ix, g_ix, idx]
        vg = vs_blk[b_ix, g_ix, idx]
        kpos = idx[..., None] * SEL_BLOCK + sel_off
        m_s = (kpos <= t[None, None, :, None, None])[:, :, None]
        s_s = jnp.einsum('bqghd,bgqnld->bghqnl', qb, kg)
        s_s = jnp.where(m_s, s_s.astype(jnp.float32), NEG).reshape(B, G, HPG, QB, n_sel * SEL_BLOCK)
        p_s = jax.nn.softmax(s_s, axis=-1).reshape(B, G, HPG, QB, n_sel, SEL_BLOCK)
        o_slc = jnp.einsum('bghqnl,bgqnld->bqghd', p_s, vg)
        kw = lax.dynamic_slice_in_dim(kw_pad, q0, WINDOW + QB, axis=1)
        vw = lax.dynamic_slice_in_dim(vw_pad, q0, WINDOW + QB, axis=1)
        wpos = q0 - WINDOW + jnp.arange(WINDOW + QB)
        m_w = (wpos[None, :] <= t[:, None]) & (wpos[None, :] > t[:, None] - WINDOW) & (wpos[None, :] >= 0)
        p_w = masked_softmax(jnp.einsum('bqghd,bkgd->bghqk', qb, kw), m_w)
        o_win = jnp.einsum('bghqk,bkgd->bqghd', p_w, vw)
        g = lax.dynamic_slice_in_dim(gates, q0, QB, axis=1).reshape(B, QB, G, HPG, 3).astype(jnp.float32)
        o = g[..., 0:1] * o_cmp + g[..., 1:2] * o_slc + g[..., 2:3] * o_win
        return o.reshape(B, QB, G * HPG * dh).astype(q.dtype)

    out = lax.map(block, jnp.arange(S // QB))
    return out.transpose(1, 0, 2, 3).reshape(B, S, NSA_QW)

def retention(q, k, v, pos):
    B, S, H, dk = q.shape
    dv = v.shape[-1]
    C = RET_CHUNK
    n_chunk = S // C
    q = rope(q, pos)
    k = rope(k, pos) * (dk ** -0.5)
    log_g = jnp.log(1.0 - 2.0 ** (-5.0 - jnp.arange(H, dtype=jnp.float32)))
    i = jnp.arange(C, dtype=jnp.float32)
    diff = i[:, None] - i[None, :]
    decay_mat = jnp.where(diff >= 0, jnp.exp(log_g[:, None, None] * jnp.maximum(diff, 0.0)), 0.0)
    q_decay = jnp.exp(log_g[:, None] * (i + 1.0))[..., None]
    k_decay = jnp.exp(log_g[:, None] * (C - 1.0 - i))[..., None]
    chunk_decay = jnp.exp(log_g * C)[:, None, None]
    qc = q.reshape(B, n_chunk, C, H, dk).transpose(1, 0, 3, 2, 4)
    kc = k.reshape(B, n_chunk, C, H, dk).transpose(1, 0, 3, 2, 4)
    vc = v.reshape(B, n_chunk, C, H, dv).transpose(1, 0, 3, 2, 4)

    def step(state, inp):
        qi, ki, vi = inp
        inner = jnp.einsum('bhid,bhjd->bhij', qi, ki) * decay_mat
        o = jnp.einsum('bhij,bhjv->bhiv', inner, vi) + jnp.einsum('bhid,bhdv->bhiv', qi, state) * q_decay
        state = state * chunk_decay + jnp.einsum('bhjd,bhjv->bhdv', ki * k_decay, vi)
        return state, o

    state0 = jnp.zeros((B, H, dk, dv), jnp.float32)
    _, o = lax.scan(step, state0, (qc, kc, vc))
    return o.transpose(1, 0, 3, 2, 4).reshape(B, S, H, dv)

def second_inputs(seed: int = 0) -> dict:
    key = jax.random.key(seed)
    ks = jax.random.split(key, 26)
    f32 = jnp.float32
    L, D = DEPTH, D_MODEL

    def nrm(k, shape, s):
        return jax.random.normal(k, shape, f32) * s

    return {
        "x": nrm(ks[0], (BATCH, SEQ, D), 1.0),
        "c": nrm(ks[1], (BATCH, D), 1.0),
        "ada_w": nrm(ks[2], (L, D, 9 * D), D ** -0.5),
        "ada_b": nrm(ks[3], (L, 9 * D), 0.01),
        "norm1_w": 1.0 + nrm(ks[4], (L, D), 0.02),
        "ffn1_w_in": nrm(ks[5], (L, D, 2 * D_FF), D ** -0.5),
        "ffn1_w_out": nrm(ks[6], (L, D_FF, D), D_FF ** -0.5),
        "norm2_w": 1.0 + nrm(ks[7], (L, D), 0.02),
        "w_in": nrm(ks[8], (L, D, IN_W), D ** -0.5),
        "cmp_k_pe": nrm(ks[9], (L, CMP_LEN, NSA_DH), 0.1),
        "cmp_k_w1": nrm(ks[10], (L, CMP_LEN * NSA_DH, CMP_HIDDEN), (CMP_LEN * NSA_DH) ** -0.5),
        "cmp_k_w2": nrm(ks[11], (L, CMP_HIDDEN, NSA_DH), CMP_HIDDEN ** -0.5),
        "cmp_v_pe": nrm(ks[12], (L, CMP_LEN, NSA_DH), 0.1),
        "cmp_v_w1": nrm(ks[13], (L, CMP_LEN * NSA_DH, CMP_HIDDEN), (CMP_LEN * NSA_DH) ** -0.5),
        "cmp_v_w2": nrm(ks[14], (L, CMP_HIDDEN, NSA_DH), CMP_HIDDEN ** -0.5),
        "ret_norm_w": 1.0 + nrm(ks[15], (L, RET_VW), 0.02),
        "w_nsa_up": nrm(ks[16], (L, NSA_QW, D), NSA_QW ** -0.5),
        "w_ret_up": nrm(ks[17], (L, RET_VW, D), RET_VW ** -0.5),
        "w_out": nrm(ks[18], (L, D, D), D ** -0.5),
        "norm3_w": 1.0 + nrm(ks[19], (L, D), 0.02),
        "ffn2_w_in": nrm(ks[20], (L, D, 2 * D_FF), D ** -0.5),
        "ffn2_w_out": nrm(ks[21], (L, D_FF, D), D_FF ** -0.5),
        "final_norm_w": 1.0 + nrm(ks[22], (D,), 0.02),
    }

def second_block(x, c, ada_w, ada_b, norm1_w, ffn1_w_in, ffn1_w_out, norm2_w, w_in,
              cmp_k_pe, cmp_k_w1, cmp_k_w2, cmp_v_pe, cmp_v_w1, cmp_v_w2, ret_norm_w,
              w_nsa_up, w_ret_up, w_out, norm3_w, ffn2_w_in, ffn2_w_out, final_norm_w):
    B, S, D = x.shape
    pos = jnp.arange(S)
    split_pts = np.cumsum(IN_WIDTHS)[:-1].tolist()
    h = x
    for l in range(DEPTH):
        mod = jax.nn.silu(c) @ ada_w[l] + ada_b[l]
        sh1, sc1, gt1, sh2, sc2, gt2, sh3, sc3, gt3 = jnp.split(mod, 9, axis=-1)
        u = modulate(rmsnorm_2(h, norm1_w[l]), sh1, sc1)
        h = h + 0.5 * gt1[:, None, :] * swiglu_2(u, ffn1_w_in[l], ffn1_w_out[l])
        u = modulate(rmsnorm_2(h, norm2_w[l]), sh2, sc2)
        proj = u @ w_in[l]
        (nq, nkc, nvc, nks, nvs, nkw, nvw, ngt, rq, rk, rv, rg, ga, gb) = jnp.split(proj, split_pts, axis=-1)
        g4 = lambda a: a.reshape(B, S, NSA_GROUPS, NSA_DH)
        o_nsa = nsa_attention(nq.reshape(B, S, NSA_HEADS, NSA_DH), g4(nkc), g4(nvc), g4(nks), g4(nvs),
                              g4(nkw), g4(nvw), jax.nn.sigmoid(ngt).reshape(B, S, NSA_HEADS, 3),
                              cmp_k_pe[l], cmp_k_w1[l], cmp_k_w2[l], cmp_v_pe[l], cmp_v_w1[l], cmp_v_w2[l])
        o_ret = retention(rq.reshape(B, S, RET_HEADS, RET_DK), rk.reshape(B, S, RET_HEADS, RET_DK),
                          rv.reshape(B, S, RET_HEADS, RET_DV), pos)
        mu = jnp.mean(o_ret, axis=-1, keepdims=True)
        var = jnp.mean(jnp.square(o_ret - mu), axis=-1, keepdims=True)
        o_ret = ((o_ret - mu) * lax.rsqrt(var + EPS)).reshape(B, S, RET_VW) * ret_norm_w[l].astype(jnp.float32)
        o_ret = (o_ret * jax.nn.silu(rg.astype(jnp.float32))).astype(x.dtype)
        y_nsa = o_nsa @ w_nsa_up[l]
        y_ret = o_ret @ w_ret_up[l]
        mixed = jax.nn.sigmoid(ga) * y_nsa + jax.nn.sigmoid(gb) * y_ret
        h = h + gt2[:, None, :] * (mixed @ w_out[l])
        u = modulate(rmsnorm_2(h, norm3_w[l]), sh3, sc3)
        h = h + 0.5 * gt3[:, None, :] * swiglu_2(u, ffn2_w_in[l], ffn2_w_out[l])
    return rmsnorm_2(h, final_norm_w)


def setup_inputs(seed=0):
    out = dict(first_inputs(seed))
    for name, value in second_inputs(seed + 1).items():
        if name != "x":
            out[name + "_2"] = value
    return out


def reference(
    x, c, w_ada, b_ada, g_pre, g_post, w_gu1, w_dn1, w_gu2, w_dn2, w_in, w_a2, b_a, b_f, g_gla,
    w_pa, w_pb, w_out, c_2, ada_w_2, ada_b_2, norm1_w_2, ffn1_w_in_2, ffn1_w_out_2, norm2_w_2,
    w_in_2, cmp_k_pe_2, cmp_k_w1_2, cmp_k_w2_2, cmp_v_pe_2, cmp_v_w1_2, cmp_v_w2_2,
    ret_norm_w_2, w_nsa_up_2, w_ret_up_2, w_out_2, norm3_w_2, ffn2_w_in_2, ffn2_w_out_2,
    final_norm_w_2,
):
    x = first_block(
        x, c, w_ada, b_ada, g_pre, g_post, w_gu1, w_dn1, w_gu2, w_dn2, w_in, w_a2, b_a, b_f,
        g_gla, w_pa, w_pb, w_out,
    )
    return second_block(
        x, c_2, ada_w_2, ada_b_2, norm1_w_2, ffn1_w_in_2, ffn1_w_out_2, norm2_w_2, w_in_2,
        cmp_k_pe_2, cmp_k_w1_2, cmp_k_w2_2, cmp_v_pe_2, cmp_v_w1_2, cmp_v_w2_2, ret_norm_w_2,
        w_nsa_up_2, w_ret_up_2, w_out_2, norm3_w_2, ffn2_w_in_2, ffn2_w_out_2, final_norm_w_2,
    )


_drawn_inputs = setup_inputs


def setup_inputs(seed=0):
    import zlib

    import numpy as np

    out = dict(_drawn_inputs(seed))
    spreads = {}
    factors = {'g_post': 2.71,
     'b_a': 4.386,
     'b_f': 56.464,
     'g_gla': 4.439,
     'ada_b_2': 4.115,
     'norm1_w_2': 6.657,
     'norm2_w_2': 5.734,
     'cmp_k_pe_2': 25.947,
     'cmp_v_pe_2': 38.864,
     'ret_norm_w_2': 27.466,
     'norm3_w_2': 23.212,
     'final_norm_w_2': 8.629}
    for name, (base, spread) in spreads.items():
        noise = np.random.default_rng([zlib.crc32(name.encode()), seed]).standard_normal(out[name].shape)
        drawn = base * np.exp(spread * noise) if base else spread * noise
        out[name] = __import__('jax').numpy.asarray(drawn.astype(out[name].dtype))
    for name, factor in factors.items():
        out[name] = (out[name] * factor).astype(out[name].dtype)
    return out
```

```python
from contextlib import ExitStack

import numpy as np

import concourse.bass as bass
from concourse import mybir

ALU = mybir.AluOpType
ACT = mybir.ActivationFunctionType
AX = mybir.AxisListType
F32 = mybir.dt.float32
F32R = mybir.dt.float32r
BF16 = mybir.dt.bfloat16

I8 = mybir.dt.int8

P = 128
D = 1024
T = 512
DF = 2816
KT = D // P
FT = DF // P
TT = T // P
EPS = 1e-6
NEG = -1e30
HG = 4
FP = 8
NP = 4
NC = T // 16 - 1
LEVELS = (128, 64, 32, 16, 8, 4, 2)

COLS = {}


def _cols(names):
    at = 0
    for name, n in names:
        COLS[name] = at
        at += n
    return at


NCOLS = _cols([("c1", 8), ("c2", 8), ("b_ada1", 72), ("b_ada2", 72), ("g_pre", 24), ("g_post", 24),
               ("norm1", 8), ("norm2", 8), ("norm3", 8), ("final", 8), ("b_a", 4), ("g_gla", 8),
               ("b_f", 1), ("ret_norm", 4)])

FFN_SLABS = 2 * FT + 3 * KT
NSA_LINKS = 28
RET_LINKS = 4


def plan(stages):
    out, c, m = [], 0, 0
    for kind, n in stages:
        out.append((kind, c, m, n))
        if kind == "ffn":
            c += FFN_SLABS
            m += 2 * FT + KT
        elif kind == "mix1":
            c += 1 + 6 * HG + 4 * FP + 3 * KT + KT
            m += 1 + 6 * HG + 4 * FP + 3 * KT + KT
        elif kind == "mix2":
            c += 6 + 1 + 4 * NP + 4 * NP + 4 + KT + KT
            m += 6 + 1 + 4 * NP + 4 * NP + 4 + 2 * KT + KT
    return out, c


STAGES = [("ffn", 0), ("mix1", 0), ("ffn", 1), ("ffn", 2), ("mix2", 0), ("ffn", 3)]


class Chain:

    def __init__(self, engine, sem):
        self.engine, self.sem, self.base, self.k, self.per, self.i = engine, sem, 0, 0, 0, 0

    def link(self, instruction):
        instruction.then_inc(self.sem, 1)
        self.k += 1
        self.engine.wait_ge(self.sem, self.base + self.k + self.per * self.i)

    def enter(self, i, per):
        self.base, self.k, self.per, self.i = self.base + self.k, 0, per, i

    def leave(self, runs):
        assert self.k == self.per, f"{self.k} links in the body, {self.per} said"
        self.base, self.k, self.per, self.i = self.base + self.per * runs, 0, 0, 0


def build(nc, A, stages=STAGES, last=True):
    phases, n_slabs = plan(stages)
    AP = bass.AP
    ds = bass.ds
    with ExitStack() as ctx:
        def sem(name):
            return ctx.enter_context(nc.semaphore(name))

        cursor = [nc.sbuf_base + (-nc.sbuf_base) % 64]

        def sb(name, shape, dt=F32):
            size = int(np.prod(shape[1:])) * {BF16: 2}.get(dt, 4)
            t = nc.alloc_sbuf_tensor_at(name, shape, dt, offset=cursor[0])
            cursor[0] += size + (-size) % 64
            assert cursor[0] <= nc.sbuf_usable_end, (name, cursor[0] - nc.sbuf_usable_end)
            return t

        x = sb("x", [P, KT, T])
        h_at = cursor[0]
        hh = sb("h_hi", [P, KT, T], F32R)
        hl = sb("h_lo", [P, KT, T], F32R)
        h_end = cursor[0]
        cursor[0] = h_at
        y = sb("y", [P, KT, T])
        cursor[0] = h_end
        raw = sb("raw", [P, 2, KT, P])
        wh = [sb(f"w_hi{s}", [P, KT, P], F32R) for s in range(2)]
        wl = [sb(f"w_lo{s}", [P, KT, P], F32R) for s in range(2)]
        ssacc = sb("ssacc", [P, T])
        sq = sb("sq", [P, 2, T])
        rstd = sb("rstd", [P, T])
        ones = sb("ones", [P, P])
        ident = sb("ident", [P, P])
        cols = sb("cols", [P, NCOLS])
        silu_c = sb("silu_c", [P, 2, KT])
        mod = sb("mod", [P, 2, 72])
        pre_a = sb("pre_a", [P, KT])
        post_g = sb("post_g", [P, KT])
        epsc = sb("epsc", [P, 1])
        tick = sb("tick", [1, 8])
        wa2 = sb("wa2", [16, 4 * P])
        shared = cursor[0]

        act_h = sb("act_hi", [P, FT, T], F32R)
        act_l = sb("act_lo", [P, FT, T], F32R)
        sg = sb("sg", [P, T])
        prod = sb("prod", [P, T])
        adaw = sb("adaw", [P, 2, KT, 256])
        adac = sb("adac", [P, 2, 256])
        nu = sb("norm_u", [P, 2, T])
        nv = sb("norm_v", [P, 2, T])

        cursor[0] = shared
        oah = sb("oa_hi", [P, KT, T], F32R)
        oal = sb("oa_lo", [P, KT, T], F32R)
        fneg16 = sb("fneg16", [48, T])
        ob_at = cursor[0]
        lac = sb("lac", [P, HG, T])
        cs = sb("cs", [P, T])
        lev = sb("lev", [P, len(LEVELS), T])
        lmask = sb("lmask", [P, len(LEVELS) + 1, P], mybir.dt.int32)
        segm = sb("segm", [P, T])
        lt4 = sb("lt4", [P, HG, T])
        nar = sb("nar", [48, T])
        nar2 = sb("nar2", [48, T])
        gq = sb("gq", [P, T])
        gk = sb("gk", [P, T])
        eq = sb("eq", [P, T])
        ek = sb("ek", [P, T])
        qp = sb("qp", [P, T])
        kp = sb("kp", [P, T])
        qc = sb("qc", [P, 2 * P])
        k0 = sb("k0", [P, P])
        vt = sb("vt", [P, 2, T])
        vtok = sb("vtok", [P, TT, 2 * P])
        adiag = sb("adiag", [P, TT, P])
        ac0 = sb("ac0", [P, T])
        ac1 = sb("ac1", [P, 2 * P])
        sr = sb("sr", [P, 2, T])
        osq = sb("osq", [P, 2, T])
        osum = sb("osum", [P, T])
        og = sb("og", [P, 2, T])
        gsel = sb("gsel", [P, 2])
        cursor[0] = ob_at
        obh = sb("ob_hi", [P, KT, T], F32R)
        obl = sb("ob_lo", [P, KT, T], F32R)
        sgb = sb("sgb", [P, KT, T])
        att_at = cursor[0]
        fq = sb("fq", [P, T])
        fk = sb("fk", [P, T])
        fv = sb("fv", [P, T])
        fvtok = sb("fvtok", [P, TT, P])
        fneg = sb("fneg", [P, 2, T])
        pb = sb("pb", [P, 4, T])
        pt = sb("pt", [P, 2, TT, T])
        nm = sb("nm", [P, 8])
        rs = sb("rs", [P, 8])
        ri = sb("ri", [P, 8])
        identb = sb("identb", [P, P], BF16)
        trib = sb("trib", [P, P], BF16)
        cursor[0] = att_at
        mg = sb("mg", [P, KT, T])
        sga1 = sb("sga1", [P, T])
        mt = sb("mt", [P, 2, T])

        cursor[0] = shared
        onh = sb("on_hi", [P, NP, T], F32R)
        onl = sb("on_lo", [P, NP, T], F32R)
        orh = sb("or_hi", [P, NP, T], F32R)
        orl = sb("or_lo", [P, NP, T], F32R)
        gates_at = cursor[0]
        sga2 = sb("sga2", [P, KT, T])
        sgb2 = sb("sgb2", [P, KT, T])
        m2_at = cursor[0]
        cursor[0] = gates_at
        w1 = sb("w1", [P, 2, 32, P])
        cursor[0] = m2_at
        ks = sb("ks", [P, T])
        kw = sb("kw", [P, T])
        vstok = sb("vstok", [P, TT, P])
        vwtok = sb("vwtok", [P, TT, P])
        kct = sb("kct", [P, 32])
        vctok = sb("vctok", [NC, 2, 64])
        gtok = sb("gtok", [P, TT, 24])
        gcur = sb("gcur", [P, 2, 3, TT])
        causal = sb("causal", [P, T])
        cmask = sb("cmask", [P, TT, NC])
        cvalid = sb("cvalid", [P, TT])
        loop_at = cursor[0]
        craw = sb("craw", [P, 2, T])
        cpe = sb("cpe", [P, 2, 32])
        cab = sb("cab", [P, 2, 2, T])
        chid = sb("chid", [P, 2, 2, NC])
        w2 = sb("w2", [P, 2, 64])
        vst = sb("vst", [P, 2, T])
        gt24 = sb("gt24", [24, T])
        cursor[0] = loop_at
        nq = sb("nq", [P, T])
        npb = sb("npb", [P, 4, T])
        npt = sb("npt", [P, 2, TT, T])
        nnm = sb("nnm", [P, 16])
        nrs = sb("nrs", [P, 16])
        nri = sb("nri", [P, 16])
        cb = sb("cb", [P, TT, NC])
        cm = sb("cm", [P, TT])
        csum = sb("csum", [P, TT])
        ct = sb("ct", [NC, T])
        cursor[0] = m2_at
        rqr = sb("rqr", [P, 2, T])
        rqk = sb("rqk", [P, 2, T])
        rtmp = sb("rtmp", [P, 2, T])
        rcos = sb("rcos", [P, T])
        rsin = sb("rsin", [P, T])
        rrot = sb("rrot", [P, P])
        rblk = sb("rblk", [P, P])
        rvt = sb("rvt", [P, T])
        rvtok = sb("rvtok", [P, TT, P])
        rdec = sb("rdec", [P, 2, T])
        rad = sb("rad", [P, 4, T])
        rsg = sb("rsg", [P, T])
        ro = sb("ro", [P, T])
        rcen = sb("rcen", [P, T])
        rsq = sb("rsq", [P, T])
        rout = sb("rout", [P, T])
        rw = sb("rw", [P, 1])
        cursor[0] = m2_at
        mh2 = sb("m2_hi", [P, KT, T], F32R)
        ml2 = sb("m2_lo", [P, KT, T], F32R)
        mt2 = sb("mt2", [P, 4, T])

        bank = [ctx.enter_context(nc.psum_tensor(f"bank{b}", [P, T], F32)) for b in range(8)]
        acc = bank[0:2]
        ST, SC0, SC1, SC2, TP, OV = bank[2:8]
        SC = [SC0, SC1]
        TB = [TP, ST]

        raw_in = [sem("raw_in0"), sem("raw_in1")]
        hi_done, lo_done = sem("hi_done"), sem("lo_done")
        slab_done = sem("slab_done")
        acc_free = [sem("acc_free0"), sem("acc_free1")]
        const_in, x_in = sem("const_in"), sem("x_in")
        dve_chain, act_chain = sem("dve_chain"), sem("act_chain")
        silu_c_done = sem("silu_c_done")
        ready = sem("ready")
        ada_in = [sem("ada_in0"), sem("ada_in1")]
        ada_acc, ada_cols, ada_mod = sem("ada_acc"), sem("ada_cols"), sem("ada_mod")
        sq_done, ssadd, ss_sum, std_done = sem("sq_done"), sem("ssadd"), sem("ss_sum"), sem("std_done")
        u_done, hh_done, h_done = sem("u_done"), sem("hh_done"), sem("h_done")
        x_done = sem("x_done")
        prodhi, prodlo = sem("prodhi"), sem("prodlo")
        out_ready = sem("out_ready")
        m1_in = sem("m1_in")
        la_ready, la_x, la_l, la_done = sem("la_ready"), sem("la_x"), sem("la_l"), sem("la_done")
        f_stored, fneg_in = sem("f_stored"), sem("fneg_in")
        g_lev_diff, g_lev_exp, g_cross_exp = sem("g_lev_diff"), sem("g_lev_exp"), sem("g_cross_exp")
        g_lev_ready, g_cross_ready = sem("g_lev_ready"), sem("g_cross_ready")
        g_vT, g_vtok, g_scores, g_picked = sem("g_vT"), sem("g_vtok"), sem("g_scores"), sem("g_picked")
        g_cross, g_cross_out, g_o, g_osq = sem("g_cross"), sem("g_cross_out"), sem("g_o"), sem("g_osq")
        g_osum, g_ss, g_std, g_read = sem("g_osum"), sem("g_ss"), sem("g_std"), sem("g_read")
        g_gated, g_hi, g_lo = sem("g_gated"), sem("g_hi"), sem("g_lo")
        f_vT, f_vtok, f_s, f_sm, f_e = sem("f_vT"), sem("f_vtok"), sem("f_s"), sem("f_sm"), sem("f_e")
        f_p, f_t, f_te, f_o, f_hi, f_lo = sem("f_p"), sem("f_t"), sem("f_te"), sem("f_o"), sem("f_hi"), sem("f_lo")
        p_sum, p_hi, p_lo = sem("p_sum"), sem("p_hi"), sem("p_lo")
        m2_in, n_pe, n_hid, n_act = sem("m2_in"), sem("n_pe"), sem("n_hid"), sem("n_act")
        n_cw, n_kc, n_vT, n_vtok = sem("n_cw"), sem("n_kc"), sem("n_vT"), sem("n_vtok")
        n_cs, n_cd, n_ce, n_cp, n_ct, n_cte = (sem(f"n_{z}") for z in ("cs", "cd", "ce", "cp", "ct", "cte"))
        n_s, n_sm, n_e, n_p, n_t, n_te, n_o, n_hi, n_lo = (sem(f"n_{z}") for z in ("s", "sm", "e", "p", "t", "te", "o", "hi", "lo"))
        r_in, r_dec, r_rot, r_qk, r_vT, r_vtok = (sem(f"r_{z}") for z in ("in", "dec", "rot", "qk", "vT", "vtok"))
        r_s, r_ad, r_pv, r_ro, r_mean, r_cen = (sem(f"r_{z}") for z in ("s", "ad", "pv", "ro", "mean", "cen"))
        r_sq, r_var, r_std, r_g, r_hi, r_lo = (sem(f"r_{z}") for z in ("sq", "var", "std", "g", "hi", "lo"))
        q_sum, q_hi, q_lo = sem("q_sum"), sem("q_hi"), sem("q_lo")
        out_sent = [sem("out_sent0"), sem("out_sent1")]

        hx, hz = hh[:], hl[:]

        def lin(c, n=0, i=0):
            return c + n * i if n else c

        def group_of(kind, n):
            return {("x", 0): 0, ("ffn", 0): 1, ("mix1", 0): 3, ("ffn", 1): 5, ("ffn", 2): 7,
                    ("mix2", 0): 8, ("ffn", 3): 9}[kind, n]

        def tile_evacuated(eng, m, n=0, i=0):
            eng.wait_ge(acc_free[m % 2], lin(m // 2 + 1, n // 2, i))

        block = ctx.enter_context(nc.Block())

        @block.sync
        def _(sp):
            W = A["slabs"]
            for c in range(2):
                sp.dma_start(raw[:, c], W[c]).then_inc(raw_in[c], 16)
            with sp.Fori(1, n_slabs // 2) as i:
                for s in range(2):
                    sp.wait_ge(lo_done, 2 * i + s - 1)
                    sp.dma_start(raw[:, s], W[ds(2 * i + s, 1)].rearrange("a p k n -> p (a k) n"))\
                      .then_inc(raw_in[s], 16)
            if n_slabs % 2:
                sp.wait_ge(lo_done, n_slabs - 2)
                sp.dma_start(raw[:, 0], W[n_slabs - 1]).then_inc(raw_in[0], 16)

        @block.gpsimd
        def _(pool):
            def low(s, c):
                pool.wait_ge(hi_done, c + 1)
                nc.gpsimd.tensor_tensor(wl[s][:], raw[:, s], wh[s][:], ALU.subtract).then_inc(lo_done, 1)
            with pool.Fori(0, n_slabs // 2) as i:
                for s in range(2):
                    low(s, 2 * i + s)
            if n_slabs % 2:
                low(0, n_slabs - 1)

        @block.scalar
        def _(act):
            chain = Chain(act, act_chain)

            def high(c, n=0, i=0):
                if c >= n_slabs and not n:
                    return
                act.wait_ge(raw_in[c % 2], lin(16 * (c // 2 + 1), 8 * n, i))
                if c >= 2:
                    act.wait_ge(slab_done, lin(c - 1, n, i))
                nc.scalar.activation(wh[c % 2][:], raw[:, c % 2], ACT.Copy).then_inc(hi_done, 1)

            def ada_load(g, n=0, i=0):
                if g >= 2:
                    act.wait_ge(ada_acc, lin(g - 1, n, i))
                piece = A["ada"][g] if not n else A["ada"][ds(lin(g, n, i), 1)].rearrange("a p k n -> p (a k) n")
                act.dma_start(adaw[:, g % 2], piece).then_inc(ada_in[g % 2], 16)

            def square(src, k, j, n=0, i=0):
                if 9 * k + j:
                    act.wait_ge(ssadd, lin(9 * k + j, n, i))
                nc.scalar.activation(sq[:, j % 2], src, ACT.Square).then_inc(sq_done, 1)

            def std(k):
                act.wait_ge(ss_sum, k + 1)
                nc.scalar.activation(rstd[:], ST[:], ACT.Sqrt, scale=1.0 / D, bias=epsc[:, 0:1]).then_inc(std_done, 1)

            def split_h(p, sh):
                for n in range(KT):
                    act.wait_ge(u_done, 8 * p + n + 1)
                    nc.scalar.activation(hh[:, n], nu[:, n % 2], ACT.Identity, scale=pre_a[:, n:n + 1],
                                         bias=sh[:, n:n + 1]).then_inc(hh_done, 1)

            def residual(block1, k):
                if block1:
                    std(k)
                    for n in range(KT):
                        act.wait_ge(x_done, 8 * [1, 3, 5].index(k) + n + 1)
                        square(x[:, n], k + 1, n)

            def out_tiles(c, m, per, block1, k):
                def pair(i, n):
                    for u in range(2):
                        for s in range(per):
                            cc = c + u * per + s
                            act.wait_ge(slab_done, lin(cc + 1, n, i))
                            high(cc + 2, n, i)
                        t = m + u
                        if block1:
                            square(acc[t % 2][:], k, u, 2 if n else 0, i)
                            j = ds(2 * i + u, 1) if n else ds(u, 1)
                            act_y = y[:, j].rearrange("p a t -> p (a t)")
                            nc.scalar.activation(act_y, acc[t % 2][:], ACT.Copy).then_inc(acc_free[t % 2], 1)
                        else:
                            tile_evacuated(act, t, 2 if n else 0, i)
                            j = ds(2 * i + u, 1)
                            square(x[:, j].rearrange("p a t -> p (a t)"), k, u, 2 if n else 0, i)
                end = c + KT * per == n_slabs
                with act.Fori(0, KT // 2 - (1 if end else 0)) as i:
                    pair(i, 2 * per)
                if end:
                    i = KT // 2 - 1
                    for u in range(2):
                        for s in range(per):
                            cc = c + 2 * per * i + u * per + s
                            act.wait_ge(slab_done, cc + 1)
                            high(cc + 2)
                        t = m + 2 * i + u
                        j = 2 * i + u
                        if block1:
                            square(acc[t % 2][:], k, j)
                            nc.scalar.activation(y[:, j], acc[t % 2][:], ACT.Copy).then_inc(acc_free[t % 2], 1)
                        else:
                            tile_evacuated(act, t)
                            square(x[:, j], k, j)

            def ffn(c, m, f):
                def unit(i, ada):
                    act.wait_ge(slab_done, lin(c + 1, 2, i))
                    high(c + 2, 2, i)
                    act.wait_ge(acc_free[(m + 1) % 2], (m + 1) // 2 + i)
                    nc.scalar.activation(sg[:], acc[m % 2][:], ACT.Silu).then_inc(acc_free[m % 2], 1)
                    act.wait_ge(slab_done, lin(c + 2, 2, i))
                    high(c + 3, 2, i)
                    tile_evacuated(act, m + 1, 2, i)
                    nc.scalar.activation(act_h[:, ds(i, 1)].rearrange("p a t -> p (a t)"), prod[:], ACT.Copy)\
                        .then_inc(prodhi, 1)
                    if ada is not None:
                        ada_load(ada + 2, 2, i)
                        ada_load(ada + 3, 2, i)
                if f == 1:
                    act.wait_ge(h_done, 24)
                    ada_load(36)
                    ada_load(37)
                for first, runs, ada, load in ADA_RUNS[f]:
                    with act.Fori(first, first + runs) as i:
                        unit(i, ada if load else None)
                k = group_of("ffn", f)
                out_tiles(c + 2 * FT, m + 2 * FT, 3, f < 2, k)
                residual(f < 2, k)

            def step(c, n=0, i=0):
                act.wait_ge(slab_done, lin(c + 1, n, i))
                high(c + 2, n, i)

            def leave(dst, m, func=ACT.Copy, **kw):
                nc.scalar.activation(dst, acc[m % 2][:], func, **kw).then_inc(acc_free[m % 2], 1)

            def mix1(c, m, _):
                act.wait_ge(slab_done, c)
                act.wait_ge(h_done, 16)
                for dst, name in ((lmask, "lmask"), (segm, "segm")):
                    act.dma_start(dst[:], A[name]).then_inc(m1_in, 16)
                step(c)
                nc.scalar.activation(nar[:], acc[m % 2][0:48, :], ACT.Copy).then_inc(acc_free[m % 2], 1)
                tile_evacuated(act, m)
                chain.link(nc.scalar.activation(nar2[32:48, :], nar[32:48, :], ACT.Identity,
                                                bias=cols[32:48, COLS["b_f"]:COLS["b_f"] + 1]))
                chain.link(nc.scalar.activation(nar[32:48, :], nar2[32:48, :], ACT.Abs))
                chain.link(nc.scalar.activation(nar[32:48, :], nar[32:48, :], ACT.Exp, scale=-1.0))
                nc.scalar.activation(nar[32:48, :], nar[32:48, :], ACT.Ln, bias=1.0).then_inc(la_l, 1)
                for h in range(HG):
                    act.wait_ge(la_ready, h + 1)
                    b = COLS["b_a"] + h
                    nc.scalar.activation(lev[:, h], (SC0, SC1, SC2, TP)[h][:], ACT.Identity, bias=cols[:, b:b + 1]).then_inc(la_x, 1)
                act.wait_ge(la_x, HG)
                chain.link(nc.scalar.activation(lt4[:], lev[:, 0:HG], ACT.Abs))
                chain.link(nc.scalar.activation(lt4[:], lt4[:], ACT.Exp, scale=-1.0))
                nc.scalar.activation(lt4[:], lt4[:], ACT.Ln, bias=1.0).then_inc(la_l, 1)
                act.wait_ge(la_done, 1)
                act.dma_start(A["fneg_dram"], fneg16[32:48, :]).then_inc(f_stored, 16)
                c, m = c + 1, m + 1
                with act.Fori(0, HG) as i:
                    gla_head(c, m, i)
                c, m = c + 6 * HG, m + 6 * HG
                act.wait_ge(f_stored, 16)
                act.wait_ge(g_lo, 2 * HG)
                act.dma_start(identb[:], A["identb"]).then_inc(m1_in, 16)
                act.dma_start(trib[:], A["trib"]).then_inc(m1_in, 16)
                with act.Fori(0, FP) as i:
                    fox_pair(c, m, i)
                c, m = c + 4 * FP, m + 4 * FP
                act.wait_ge(f_lo, FP)
                with act.Fori(0, KT) as i:
                    step(c, 2, i)
                    act.wait_ge(acc_free[(m + 1) % 2], (m + 1) // 2 + i)
                    leave(sga1[:], m, ACT.Sigmoid)
                    step(c + 1, 2, i)
                c, m = c + 2 * KT, m + 2 * KT
                with act.Fori(0, KT // 2) as i:
                    for u in range(2):
                        step(c + u, 2, i)
                        act.wait_ge(p_sum, 2 * i + u + 1)
                        nc.scalar.activation(oah[:, ds(2 * i + u, 1)].rearrange("p a t -> p (a t)"), mt[:, u], ACT.Copy)\
                            .then_inc(p_hi, 1)
                c, m = c + KT, m + KT
                k = group_of("mix1", 0)
                out_tiles(c, m, 1, True, k)
                residual(True, k)

            def gla_head(c, m, i):
                act.wait_ge(g_lev_diff, i + 1)
                nc.scalar.activation(lev[:], lev[:], ACT.Exp).then_inc(g_lev_exp, 1)
                act.wait_ge(g_cross_ready, i)
                nc.scalar.activation(eq[:], cs[:], ACT.Exp)
                for t in range(TT):
                    last = nc.scalar.activation(ek[:, P * t:P * (t + 1)], cs[:, P * t:P * (t + 1)], ACT.Exp, scale=-1.0,
                                                bias=cs[:, P * t + P - 1:P * t + P])
                last.then_inc(g_cross_exp, 1)
                step(c, 6, i)
                leave(gq[:], m, scale=float(P) ** -0.5)
                step(c + 1, 6, i)
                leave(gk[:], m + 1)
                for e in range(2):
                    step(c + 2 + e, 6, i)
                    leave(vt[:, e], m + 2 + e)
                step(c + 4, 6, i)
                act.wait_ge(g_gated, 2 * i)
                leave(sr[:, 0], m + 4, ACT.Silu)
                act.wait_ge(g_cross, 2 * i + 1)
                nc.scalar.activation(ac0[:], SC2[:], ACT.Copy).then_inc(g_cross_out, 1)
                act.wait_ge(g_cross, 2 * i + 2)
                nc.scalar.activation(ac1[:], ST[:, 0:2 * P], ACT.Copy).then_inc(g_cross_out, 1)
                step(c + 5, 6, i)
                leave(sr[:, 1], m + 5, ACT.Silu)
                act.wait_ge(g_o, 2 * i + 2)
                act.wait_ge(g_osum, i)
                nc.scalar.activation(osq[:, 0], OV[:], ACT.Square).then_inc(g_osq, 1)
                nc.scalar.activation(osq[:, 1], TP[:], ACT.Square).then_inc(g_osq, 1)
                act.wait_ge(g_ss, i + 1)
                nc.scalar.activation(rstd[:], SC0[:], ACT.Sqrt, scale=1.0 / (2 * P), bias=epsc[:, 0:1]).then_inc(g_std, 1)
                for e in range(2):
                    act.wait_ge(g_gated, 2 * i + e + 1)
                    nc.scalar.activation(oah[:, ds(2 * i + e, 1)].rearrange("p a t -> p (a t)"), og[:, e], ACT.Copy)\
                        .then_inc(g_hi, 1)

            def fox_pair(c, m, i):
                act.wait_ge(f_sm, 8 * i)
                act.dma_start(fneg[:], A["fneg_dram"][ds(2 * i, 2), :].rearrange("(o a) t -> o a t", o=1)
                              .to_broadcast([P, 2, T])).then_inc(fneg_in, 16)
                step(c, 4, i)
                leave(fq[:], m, scale=0.125)
                step(c + 1, 4, i)
                leave(fk[:], m + 1)
                step(c + 2, 4, i)
                leave(fv[:], m + 2)
                step(c + 3, 4, i)
                leave(sgb[:, ds(i, 1)].rearrange("p a t -> p (a t)"), m + 3, ACT.Sigmoid)
                for n in range(8 + 2):
                    if n < 8:
                        w = P * (n % 4 + 1)
                        act.wait_ge(f_sm, 8 * i + n + 1)
                        nc.scalar.activation(pb[:, n % 4, 0:w], pb[:, n % 4, 0:w], ACT.Exp, scale=-1.0,
                                             bias=nm[:, n:n + 1], accum_out=rs[:, n:n + 1]).then_inc(f_e, 1)
                    if n >= 2:
                        j = n - 2
                        a, t = j // 4, j % 4
                        act.wait_ge(f_t, 8 * i + j + 1)
                        nc.scalar.activation(pt[:, a, 0:t + 1, P * t:P * (t + 1)],
                                             TB[j % 2][:, 0:P * (t + 1)].rearrange("p (k q) -> p k q", q=P), ACT.Copy)\
                            .then_inc(f_te, 1)
                act.wait_ge(f_o, i + 1)
                nc.scalar.activation(obh[:, ds(i, 1)].rearrange("p a t -> p (a t)"), OV[:], ACT.Copy).then_inc(f_hi, 1)

            def mix2(c, m, _):
                act.wait_ge(h_done, 40)
                for dst, name in ((w1, "w1"), (w2, "w2"), (cpe, "cpe"), (causal, "causal"), (cmask, "cmask"), (cvalid, "cvalid")):
                    act.dma_start(dst[:], A[name]).then_inc(m2_in, 16)
                for u, dst in enumerate((craw[:, 0], craw[:, 1], ks[:], vst[:, 0], kw[:], vst[:, 1])):
                    step(c + u)
                    leave(dst, m + u)
                step(c + 6)
                nc.scalar.activation(gt24[:], acc[(m + 6) % 2][0:24, :], ACT.Sigmoid).then_inc(acc_free[(m + 6) % 2], 1)
                for kv in range(2):
                    for g in range(2):
                        z = 2 * kv + g
                        act.wait_ge(n_hid, z + 1)
                        nc.scalar.activation(chid[:, kv, g], (SC0, SC1, SC2, TP)[z][:, 0:NC], ACT.Silu).then_inc(n_act, 1)
                act.wait_ge(n_cw, 1)
                nc.scalar.activation(kct[:, 0:NC], ST[:, 0:NC], ACT.Copy).then_inc(n_kc, 1)
                act.wait_ge(n_cw, 2)
                nc.scalar.activation(vctok[:].rearrange("n g d -> n (g d)"), OV[0:NC, 0:P], ACT.Copy).then_inc(n_kc, 1)
                c, m = c + 7, m + 7
                with act.Fori(0, NP) as i:
                    nsa_pair(c, m, i)
                c, m = c + 4 * NP, m + 4 * NP
                act.wait_ge(n_lo, NP)
                for dst, name in ((rcos, "rcos"), (rsin, "rsin"), (rrot, "rrot"), (rblk, "rblk")):
                    act.dma_start(dst[:], A[name]).then_inc(r_in, 16)
                with act.Fori(0, NP) as i:
                    ret_pair(c, m, i)
                c, m = c + 4 * NP, m + 4 * NP
                with act.Fori(0, 2) as i:
                    for u in range(2):
                        step(c + u, 2, i)
                        leave(sgb2[:, ds(2 * i + u + 4, 1)].rearrange("p a t -> p (a t)"), m + u, ACT.Sigmoid)
                c, m = c + 4, m + 4
                with act.Fori(0, KT // 2) as i:
                    for u in range(2):
                        step(c + u, 2, i)
                        act.wait_ge(q_sum, 2 * i + u + 1)
                        nc.scalar.activation(mh2[:, ds(2 * i + u, 1)].rearrange("p a t -> p (a t)"), mt2[:, u], ACT.Copy)\
                            .then_inc(q_hi, 1)
                c, m = c + KT, m + 2 * KT
                k = group_of("mix2", 0)
                out_tiles(c, m, 1, False, k)

            def nsa_pair(c, m, i):
                step(c, 4, i)
                leave(nq[:], m, scale=0.125)
                for u in range(2):
                    step(c + 1 + u, 4, i)
                    leave(sga2[:, ds(2 * i + u, 1)].rearrange("p a t -> p (a t)"), m + 1 + u, ACT.Sigmoid)
                step(c + 3, 4, i)
                leave(sgb2[:, ds(i, 1)].rearrange("p a t -> p (a t)"), m + 3, ACT.Sigmoid)

                def cmp_exp(a):
                    act.wait_ge(n_cd, 2 * i + a + 1)
                    nc.scalar.activation(cb[:], cb[:], ACT.Exp).then_inc(n_ce, 1)

                def cmp_out(a):
                    act.wait_ge(n_ct, 2 * i + a + 1)
                    nc.scalar.activation(ct[:], SC2[0:NC, :], ACT.Copy).then_inc(n_cte, 1)
                cmp_exp(0)
                for n in range(16 + 2):
                    if n < 16:
                        w = P * (n % 4 + 1)
                        act.wait_ge(n_sm, 16 * i + n + 1)
                        nc.scalar.activation(npb[:, n % 4, 0:w], npb[:, n % 4, 0:w], ACT.Exp, scale=-1.0,
                                             bias=nnm[:, n:n + 1], accum_out=nrs[:, n:n + 1]).then_inc(n_e, 1)
                    if n >= 2:
                        j = n - 2
                        t = j % 4
                        act.wait_ge(n_t, 16 * i + j + 1)
                        nc.scalar.activation(npt[:, (j // 4) % 2, 0:t + 1, P * t:P * (t + 1)],
                                             TB[j % 2][:, 0:P * (t + 1)].rearrange("p (k q) -> p k q", q=P), ACT.Copy)\
                            .then_inc(n_te, 1)
                    if n == 3:
                        cmp_out(0)
                    if n == 5:
                        cmp_exp(1)
                    if n == 7:
                        cmp_out(1)
                act.wait_ge(n_o, i + 1)
                nc.scalar.activation(onh[:, ds(i, 1)].rearrange("p a t -> p (a t)"), OV[:], ACT.Copy).then_inc(n_hi, 1)

            def ret_pair(c, m, i):
                act.wait_ge(r_ad, 8 * i)
                act.dma_start(rdec[:], A["rdec"][ds(2 * i, 2)].rearrange("a p t -> p a t")).then_inc(r_dec, 16)
                act.wait_ge(r_qk, 2 * i)
                step(c, 4, i)
                leave(rqr[:, 0], m)
                step(c + 1, 4, i)
                leave(rqr[:, 1], m + 1, scale=0.125)
                step(c + 2, 4, i)
                leave(rvt[:], m + 2)
                step(c + 3, 4, i)
                act.wait_ge(r_lo, i)
                leave(rsg[:], m + 3, ACT.Silu)
                act.wait_ge(r_pv, 8 * i + 8)
                nc.scalar.activation(ro[:], OV[:], ACT.Copy).then_inc(r_ro, 1)
                act.wait_ge(r_cen, i + 1)
                nc.scalar.activation(rsq[:], rcen[:], ACT.Square).then_inc(r_sq, 1)
                act.wait_ge(r_var, i + 1)
                nc.scalar.activation(rstd[:], TP[:], ACT.Sqrt, bias=epsc[:, 0:1]).then_inc(r_std, 1)
                act.wait_ge(r_g, i + 1)
                nc.scalar.activation(orh[:, ds(i, 1)].rearrange("p a t -> p (a t)"), rout[:], ACT.Copy).then_inc(r_hi, 1)

            act.dma_start(cols[:], A["cols"]).then_inc(const_in, 16)
            act.dma_start(ident[:], A["ident"]).then_inc(const_in, 16)
            act.dma_start(wa2[:], A["w_a2"]).then_inc(const_in, 16)
            act.dma_start(x[:], A["xt"]).then_inc(x_in, 16)
            ada_load(0)
            ada_load(1)
            high(0)
            high(1)
            act.wait_ge(const_in, 48)
            nc.scalar.activation(silu_c[:].rearrange("p a k -> p (a k)"), cols[:, 0:2 * KT], ACT.Silu).then_inc(silu_c_done, 1)
            act.wait_ge(x_in, 16)
            act.wait_ge(ready, 1)
            for n in range(KT):
                square(x[:, n], 0, n)
            for g in range(2, 10):
                ada_load(g)
            p = 0
            for kind, c, m, n in phases:
                std(PRE_GROUP[p])
                split_h(p, mod[:, PRE_MOD[p][0], 24 * PRE_MOD[p][1]:24 * PRE_MOD[p][1] + 8])
                {"ffn": ffn, "mix1": mix1, "mix2": mix2}[kind](c, m, n)
                p += 1
            if last:
                std(PRE_GROUP[p])
            for n in range(KT):
                act.wait_ge(out_ready, n + 1)
                act.dma_start(A["out"][:, n], nu[:, n % 2] if last else x[:, n]).then_inc(out_sent[n % 2], 16)
            for s in range(2):
                act.wait_ge(out_sent[s], 16 * KT // 2)

        @block.vector
        def _(dve):
            V = nc.vector
            chain = Chain(dve, dve_chain)

            def ada_sum(g, b, n=0, i=0):
                s = g % 2
                dve.wait_ge(ada_in[s], lin(16 * (g // 2 + 1), 8 * n, i))
                if g >= 2:
                    dve.wait_ge(ada_cols, lin(g - 1, n, i))
                chain.link(V.tensor_scalar(adac[:, s], adaw[:, s, 0], silu_c[:, b, 0:1], None, ALU.mult))
                for k in range(1, KT):
                    ins = V.scalar_tensor_tensor(adac[:, s], adaw[:, s, k], silu_c[:, b, k:k + 1], adac[:, s],
                                                 ALU.mult, ALU.add)
                    if k < KT - 1:
                        chain.link(ins)
                ins.then_inc(ada_acc, 1)

            def ada_add(g, b, n=0, i=0):
                dve.wait_ge(ada_cols, lin(g + 1, n, i))
                at = 2 * (g - 36 * b)
                j = ds(lin(at, 2 * n, i), 2)
                jb = ds(lin(COLS["b_ada1"] + 72 * b + at, 2 * n, i), 2)
                V.tensor_tensor(mod[:, b, j], (TP if g % 2 == 0 else OV)[:, 0:2], cols[:, jb], ALU.add).then_inc(ada_mod, 1)

            def add_squares(k, j, n=0, i=0):
                dve.wait_ge(sq_done, lin(8 * k + j + 1, n, i))
                dve.wait_ge(ssadd, lin(9 * k + j + 1, n, i))
                V.tensor_tensor(ssacc[:], ssacc[:], sq[:, j % 2], ALU.add).then_inc(ssadd, 1)

            def clear_squares(k):
                if k:
                    dve.wait_ge(ss_sum, k)
                V.memset(ssacc[:], 0.0).then_inc(ssadd, 1)

            def reciprocal_std(k):
                dve.wait_ge(std_done, k + 1)
                chain.link(V.reciprocal(rstd[:], rstd[:]))

            def norm_h(p):
                b, v = PRE_MOD[p]
                gain = cols[:, PRE_GAIN[p]:PRE_GAIN[p] + KT]
                chain.link(V.scalar_tensor_tensor(pre_a[:], mod[:, b, 24 * v + 8:24 * v + 16], 1.0, gain, ALU.add, ALU.mult))
                reciprocal_std(PRE_GROUP[p])

                def u(n):
                    V.tensor_tensor(nu[:, n % 2], x[:, n], rstd[:], ALU.mult).then_inc(u_done, 1)
                u(0)
                for n in range(KT):
                    if n + 1 < KT:
                        u(n + 1)
                    dve.wait_ge(u_done, 8 * p + n + 1)
                    chain.link(V.tensor_scalar(nv[:, n % 2], nu[:, n % 2], pre_a[:, n:n + 1],
                                               mod[:, b, 24 * v + n:24 * v + n + 1], ALU.mult, ALU.add))
                    dve.wait_ge(hh_done, 8 * p + n + 1)
                    V.tensor_tensor(hl[:, n], nv[:, n % 2], hh[:, n], ALU.subtract).then_inc(h_done, 1)

            def set_post(b, v, half, gain):
                gate = mod[:, b, 24 * v + 16:24 * v + 24]
                if gain is not None:
                    chain.link(V.scalar_tensor_tensor(post_g[:], gate, half, cols[:, gain:gain + KT], ALU.mult, ALU.mult))
                else:
                    chain.link(V.tensor_scalar(post_g[:], gate, half, None, ALU.mult))

            def out_tiles(c, m, per, block1, k):
                clear_squares(k)
                with dve.Fori(0, KT // 2) as i:
                    for u in range(2):
                        t = m + u
                        if not block1:
                            dve.wait_ge(slab_done, lin(c + (u + 1) * per, 2 * per, i))
                            j = ds(2 * i + u, 1)
                            xj = x[:, j].rearrange("p a t -> p (a t)")
                            V.scalar_tensor_tensor(xj, acc[t % 2][:], post_g[:, j], xj, ALU.mult, ALU.add)\
                                .then_inc(acc_free[t % 2], 1)
                        add_squares(k, u, 2, i)

            def residual(block1, k):
                if not block1:
                    return
                reciprocal_std(k)
                clear_squares(k + 1)
                base = 8 * [1, 3, 5].index(k)
                for n in range(KT):
                    chain.link(V.scalar_tensor_tensor(nu[:, n % 2], y[:, n], post_g[:, n:n + 1], rstd[:], ALU.mult, ALU.mult))
                    V.tensor_tensor(x[:, n], x[:, n], nu[:, n % 2], ALU.add).then_inc(x_done, 1)
                    if n:
                        add_squares(k + 1, n - 1)
                add_squares(k + 1, KT - 1)

            def ffn(c, m, f):
                def unit(i, ada, b):
                    if ada is not None:
                        ada_sum(ada, b, 2, i)
                        ada_sum(ada + 1, b, 2, i)
                    dve.wait_ge(slab_done, lin(c + 2, 2, i))
                    tile_evacuated(dve, m, 2, i)
                    dve.wait_ge(prodhi, FT * f + i)
                    dve.wait_ge(prodlo, FT * f + i)
                    V.tensor_tensor(prod[:], acc[(m + 1) % 2][:], sg[:], ALU.mult)\
                        .then_inc(acc_free[(m + 1) % 2], 1)
                    if ada is not None:
                        ada_add(ada, b, 2, i)
                        ada_add(ada + 1, b, 2, i)
                    tile_evacuated(dve, m + 1, 2, i)
                    dve.wait_ge(prodhi, FT * f + i + 1)
                    j = ds(i, 1)
                    V.tensor_tensor(act_l[:, j].rearrange("p a t -> p (a t)"), prod[:],
                                    act_h[:, j].rearrange("p a t -> p (a t)"), ALU.subtract).then_inc(prodlo, 1)
                for first, runs, ada, load in ADA_RUNS[f]:
                    with dve.Fori(first, first + runs) as i:
                        b = 0 if ada is not None and ada < 36 else 1
                        chain.enter(i - first, 14 if ada is not None else 0)
                        unit(i, ada, b)
                    chain.leave(runs)
                b, v = ((0, 0), (0, 2), (1, 0), (1, 2))[f]
                set_post(b, v, 0.5, COLS["g_post"] + 8 * v if b == 0 else None)
                k = group_of("ffn", f)
                out_tiles(c + 2 * FT, m + 2 * FT, 3, f < 2, k)
                residual(f < 2, k)

            def holds_waits(n):
                V.memset(tick[:, n % 8:n % 8 + 1], 0.0)

            def mix1(c, m, _):
                dve.wait_ge(m1_in, 32)
                dve.wait_ge(la_l, 1)
                chain.link(V.scalar_tensor_tensor(nar2[32:48, :], nar2[32:48, :], 0.0, nar[32:48, :], ALU.min, ALU.subtract))
                chain.link(V.memset(fneg16[32:48, :], 1.0))
                chain.link(V.tensor_tensor_scan(nar[32:48, :], fneg16[32:48, :], nar2[32:48, :], 0.0, ALU.mult, ALU.subtract))
                V.tensor_copy(fneg16[32:48, :], nar[32:48, :]).then_inc(la_done, 1)
                dve.wait_ge(la_l, 2)
                chain.link(V.scalar_tensor_tensor(lt4[:], lev[:, 0:HG], 0.0, lt4[:], ALU.min, ALU.subtract))
                chain.link(V.tensor_scalar(lt4[:], lt4[:], 1.0 / 16.0, None, ALU.mult))
                for h in range(HG):
                    ins = V.tensor_tensor_scan(lac[:, h], segm[:], lt4[:, h], 0.0, ALU.mult, ALU.add)
                chain.link(ins)
                c, m = c + 1, m + 1
                with dve.Fori(0, HG) as i:
                    chain.enter(i, 4)
                    gla_head(c, m, i)
                chain.leave(HG)
                c, m = c + 6 * HG, m + 6 * HG
                with dve.Fori(0, FP) as i:
                    chain.enter(i, 8)
                    fox_pair(c, m, i)
                chain.leave(FP)
                c, m = c + 4 * FP, m + 4 * FP
                set_post(0, 1, 1.0, COLS["g_post"] + 8)
                with dve.Fori(0, KT) as i:
                    dve.wait_ge(slab_done, c + 2 + 2 * i)
                    tile_evacuated(dve, m, 2, i)
                    V.tensor_tensor(mg[:, ds(i, 1)].rearrange("p a t -> p (a t)"), acc[(m + 1) % 2][:], sga1[:], ALU.mult)\
                        .then_inc(acc_free[(m + 1) % 2], 1)
                c, m = c + 2 * KT, m + 2 * KT
                with dve.Fori(0, KT // 2) as i:
                    for u in range(2):
                        j = ds(2 * i + u, 1)
                        flat = lambda b: b[:, j].rearrange("p a t -> p (a t)")
                        dve.wait_ge(slab_done, c + u + 1 + 2 * i)
                        dve.wait_ge(p_lo, 2 * i + u)
                        V.tensor_tensor(mt[:, u], acc[(m + u) % 2][:], flat(sgb), ALU.mult).then_inc(acc_free[(m + u) % 2], 1)
                        tile_evacuated(dve, m + u, 2, i)
                        V.tensor_tensor(mt[:, u], mt[:, u], flat(mg), ALU.add).then_inc(p_sum, 1)
                        dve.wait_ge(p_sum, 2 * i + u + 1)
                        dve.wait_ge(p_hi, 2 * i + u + 1)
                        V.tensor_tensor(flat(oal), mt[:, u], flat(oah), ALU.subtract).then_inc(p_lo, 1)
                c, m = c + KT, m + KT
                k = group_of("mix1", 0)
                out_tiles(c, m, 1, True, k)
                residual(True, k)

            def gla_head(c, m, i):
                dve.wait_ge(g_cross_exp, i)
                chain.link(V.tensor_copy(cs[:], lac[:, ds(i, 1)].rearrange("p a t -> p (a t)")))
                V.tensor_copy(gsel[:], cols[:, ds(COLS["g_gla"] + 2 * i, 2)])
                dve.wait_ge(g_o, 2 * i)
                for l, b in enumerate(LEVELS):
                    cv = cs[:].rearrange("p (n b) -> p n b", b=b)
                    lv = lev[:, l].rearrange("p (n b) -> p n b", b=b)
                    ref = cv[:, :, b // 2 - 1:b // 2].to_broadcast([P, T // b, b // 2])
                    V.tensor_tensor(lv[:, :, b // 2:], cv[:, :, b // 2:], ref, ALU.subtract)
                    ins = V.tensor_tensor(lv[:, :, :b // 2], ref, cv[:, :, :b // 2], ALU.subtract)
                ins.then_inc(g_lev_diff, 1)
                chain.link(V.memset(adiag[:], 0.0))
                dve.wait_ge(g_lev_exp, i + 1)
                tile_evacuated(dve, m, 6, i)
                tile_evacuated(dve, m + 1, 6, i)
                for l, b in enumerate(LEVELS):
                    lv = lev[:, l].rearrange("p (n b) -> p n b", b=b)
                    qv, kv = (z[:].rearrange("p (n b) -> p n b", b=b) for z in (gq, gk))
                    V.tensor_tensor(lv[:, :, b // 2:], lv[:, :, b // 2:], qv[:, :, b // 2:], ALU.mult)
                    ins = V.tensor_tensor(lv[:, :, :b // 2], lv[:, :, :b // 2], kv[:, :, :b // 2], ALU.mult)
                ins.then_inc(g_lev_ready, 1)
                dve.wait_ge(g_cross_exp, i + 1)
                V.tensor_tensor(qp[:], gq[:], eq[:], ALU.mult)
                chain.link(V.tensor_tensor(kp[:], gk[:], ek[:], ALU.mult))
                V.tensor_scalar(k0[:], kp[:, 0:P], eq[:, 2 * P - 1:2 * P], None, ALU.mult)
                V.tensor_copy(qc[:, 0:P], qp[:, 2 * P:3 * P])
                V.tensor_scalar(qc[:, P:2 * P], qp[:, 3 * P:4 * P], eq[:, 3 * P - 1:3 * P], None, ALU.mult).then_inc(g_cross_ready, 1)
                for e in range(2):
                    dve.wait_ge(g_vT, 2 * i + e + 1)
                    V.tensor_copy(vtok[:, :, P * e:P * (e + 1)], (TP, OV)[e][:].rearrange("p (k q) -> p k q", q=P)).then_inc(g_vtok, 1)
                for l in range(len(LEVELS) + 1):
                    dve.wait_ge(g_scores, 8 * i + l + 1)
                    dve.wait_ge(g_picked, 8 * i + l)
                    holds_waits(l)
                    V.copy_predicated(adiag[:], lmask[:, l:l + 1].to_broadcast([P, TT, P]),
                                      SC[l % 2][:].rearrange("p (k q) -> p k q", q=P)).then_inc(g_picked, 1)
                dve.wait_ge(g_osq, 2 * i + 2)
                dve.wait_ge(g_osum, i)
                V.tensor_tensor(osum[:], osq[:, 0], osq[:, 1], ALU.add).then_inc(g_osum, 1)
                dve.wait_ge(g_std, i + 1)
                chain.link(V.reciprocal(rstd[:], rstd[:]))
                dve.wait_ge(g_lo, 2 * i)
                for e in range(2):
                    ins = V.scalar_tensor_tensor(og[:, e], (OV, TP)[e][:], gsel[:, e:e + 1], rstd[:], ALU.mult, ALU.mult)
                    ins.then_inc(g_read, 1)
                dve.wait_ge(g_read, 2 * i + 2)
                tile_evacuated(dve, m + 4, 6, i)
                tile_evacuated(dve, m + 5, 6, i)
                for e in range(2):
                    V.tensor_tensor(og[:, e], og[:, e], sr[:, e], ALU.mult).then_inc(g_gated, 1)
                dve.wait_ge(g_gated, 2 * i + 2)
                for e in range(2):
                    dve.wait_ge(g_hi, 2 * i + e + 1)
                    j = ds(2 * i + e, 1)
                    V.tensor_tensor(oal[:, j].rearrange("p a t -> p (a t)"), og[:, e],
                                    oah[:, j].rearrange("p a t -> p (a t)"), ALU.subtract).then_inc(g_lo, 1)

            def fox_pair(c, m, i):
                dve.wait_ge(f_vT, i + 1)
                V.tensor_copy(fvtok[:], SC2[:].rearrange("p (k q) -> p k q", q=P)).then_inc(f_vtok, 1)
                dve.wait_ge(fneg_in, 16 * i + 16)
                for n in range(8 + 1):
                    if n < 8:
                        w = P * (n % 4 + 1)
                        dve.wait_ge(f_s, 8 * i + n + 1)
                        if n >= 4:
                            dve.wait_ge(f_t, 8 * i + n - 3)
                        holds_waits(n)
                        V.tensor_tensor_reduce(out=pb[:, n % 4, 0:w], in0=SC[n % 2][:, 0:w], in1=fneg[:, n // 4, 0:w],
                                               scale=-1.0, scalar=3e38, op0=ALU.add, op1=ALU.min,
                                               accum_out=nm[:, n:n + 1]).then_inc(f_sm, 1)
                    if n >= 1:
                        j = n - 1
                        w = P * (j % 4 + 1)
                        dve.wait_ge(f_e, 8 * i + j + 1)
                        chain.link(V.reciprocal(ri[:, j:j + 1], rs[:, j:j + 1]))
                        V.tensor_scalar(pb[:, j % 4, 0:w], pb[:, j % 4, 0:w], ri[:, j:j + 1], None, ALU.mult).then_inc(f_p, 1)
                dve.wait_ge(f_hi, i + 1)
                j = ds(i, 1)
                V.tensor_tensor(obl[:, j].rearrange("p a t -> p (a t)"), OV[:], obh[:, j].rearrange("p a t -> p (a t)"),
                                ALU.subtract).then_inc(f_lo, 1)

            def mix2(c, m, _):
                dve.wait_ge(m2_in, 96)
                for kv in range(2):
                    tile_evacuated(dve, m + kv)
                    for half in range(2):
                        V.tensor_tensor(cab[:, kv, half].rearrange("p (n l) -> p n l", l=16),
                                        craw[:, kv].rearrange("p (n l) -> p n l", l=16),
                                        cpe[:, kv:kv + 1, 16 * half:16 * half + 16].to_broadcast([P, 32, 16]), ALU.add)\
                            .then_inc(n_pe, 1)
                for z, dst in enumerate((vstok, vwtok)):
                    dve.wait_ge(n_vT, z + 1)
                    V.tensor_copy(dst[:], SC[z][:].rearrange("p (k q) -> p k q", q=P)).then_inc(n_vtok, 1)
                dve.wait_ge(n_vT, 3)
                V.tensor_copy(gtok[:], SC2[:, 0:24 * TT].rearrange("p (t j) -> p t j", j=24)).then_inc(n_vtok, 1)
                dve.wait_ge(n_vtok, 3)
                c, m = c + 7, m + 7
                with dve.Fori(0, NP) as i:
                    chain.enter(i, NSA_LINKS)
                    nsa_pair(c, m, i)
                chain.leave(NP)
                c, m = c + 4 * NP, m + 4 * NP
                dve.wait_ge(r_in, 64)
                with dve.Fori(0, NP) as i:
                    chain.enter(i, RET_LINKS)
                    ret_pair(c, m, i)
                chain.leave(NP)
                c, m = c + 4 * NP, m + 4 * NP
                set_post(1, 1, 1.0, None)
                c, m = c + 4, m + 4
                with dve.Fori(0, KT // 2) as i:
                    for u in range(2):
                        j = ds(2 * i + u, 1)
                        flat = lambda b: b[:, j].rearrange("p a t -> p (a t)")
                        dve.wait_ge(slab_done, c + u + 1 + 2 * i)
                        dve.wait_ge(q_lo, 2 * i + u)
                        for z, gate in enumerate((sga2, sgb2)):
                            t = m + 2 * u + z
                            V.tensor_tensor(mt2[:, u + 2 * z], acc[t % 2][:], flat(gate), ALU.mult).then_inc(acc_free[t % 2], 1)
                        tile_evacuated(dve, m + 2 * u, 4, i)
                        tile_evacuated(dve, m + 2 * u + 1, 4, i)
                        V.tensor_tensor(mt2[:, u], mt2[:, u], mt2[:, u + 2], ALU.add).then_inc(q_sum, 1)
                        dve.wait_ge(q_sum, 2 * i + u + 1)
                        dve.wait_ge(q_hi, 2 * i + u + 1)
                        V.tensor_tensor(flat(ml2), mt2[:, u], flat(mh2), ALU.subtract).then_inc(q_lo, 1)
                c, m = c + KT, m + 2 * KT
                out_tiles(c, m, 1, False, group_of("mix2", 0))

            def nsa_pair(c, m, i):
                dve.wait_ge(n_p, 16 * i)
                for a in range(2):
                    V.tensor_copy(gcur[:, a], gtok[:, :, ds(3 * i + 12 * a, 3)].rearrange("p t b -> p b t"))

                def cmp_shift(a):
                    dve.wait_ge(n_cs, 2 * i + a + 1)
                    dve.wait_ge(n_ct, 2 * i + a)
                    chain.link(V.tensor_tensor(cb[:], SC2[:, 0:32 * TT].rearrange("p (t j) -> p t j", j=32)[:, :, 0:NC], cmask[:], ALU.add))
                    chain.link(V.tensor_reduce(cm[:], cb[:], AX.X, ALU.max))
                    V.tensor_tensor(cb[:], cb[:], cm[:].rearrange("p (t o) -> p t o", o=1).to_broadcast([P, TT, NC]), ALU.subtract)\
                        .then_inc(n_cd, 1)

                def cmp_scale(a):
                    dve.wait_ge(n_ce, 2 * i + a + 1)
                    chain.link(V.tensor_reduce(csum[:], cb[:], AX.X, ALU.add))
                    chain.link(V.reciprocal(csum[:], csum[:]))
                    chain.link(V.tensor_tensor(csum[:], csum[:], gcur[:, a, 0], ALU.mult))
                    chain.link(V.tensor_tensor(csum[:], csum[:], cvalid[:], ALU.mult))
                    V.tensor_tensor(cb[:], cb[:], csum[:].rearrange("p (t o) -> p t o", o=1).to_broadcast([P, TT, NC]), ALU.mult)\
                        .then_inc(n_cp, 1)
                cmp_shift(0)
                for n in range(16 + 1):
                    if n < 16:
                        w = P * (n % 4 + 1)
                        dve.wait_ge(n_s, 16 * i + n + 1)
                        if n >= 4:
                            dve.wait_ge(n_t, 16 * i + n - 3)
                        holds_waits(n)
                        V.tensor_tensor_reduce(out=npb[:, n % 4, 0:w], in0=SC[n % 2][:, 0:w], in1=causal[:, T - w:T],
                                               scale=-1.0, scalar=3e38, op0=ALU.add, op1=ALU.min,
                                               accum_out=nnm[:, n:n + 1]).then_inc(n_sm, 1)
                    if n >= 1:
                        j = n - 1
                        w = P * (j % 4 + 1)
                        dve.wait_ge(n_e, 16 * i + j + 1)
                        chain.link(V.reciprocal(nri[:, j:j + 1], nrs[:, j:j + 1]))
                        V.tensor_scalar(npb[:, j % 4, 0:w], npb[:, j % 4, 0:w], nri[:, j:j + 1],
                                        gcur[:, j // 8, 1 + (j // 4) % 2, j % 4:j % 4 + 1], ALU.mult, ALU.mult).then_inc(n_p, 1)
                    if n == 1:
                        cmp_scale(0)
                    if n == 5:
                        cmp_shift(1)
                    if n == 6:
                        cmp_scale(1)
                dve.wait_ge(n_hi, i + 1)
                j = ds(i, 1)
                V.tensor_tensor(onl[:, j].rearrange("p a t -> p (a t)"), OV[:], onh[:, j].rearrange("p a t -> p (a t)"),
                                ALU.subtract).then_inc(n_lo, 1)

            def ret_pair(c, m, i):
                V.tensor_copy(rw[:], cols[:, ds(i + COLS["ret_norm"], 1)])
                for z in range(2):
                    dve.wait_ge(r_rot, 2 * i + z + 1)
                    V.tensor_tensor(rtmp[:, z], SC[z][:], rsin[:], ALU.mult)
                    chain.link(V.tensor_tensor(rqk[:, z], rqr[:, z], rcos[:], ALU.mult))
                    V.tensor_tensor(rqk[:, z], rqk[:, z], rtmp[:, z], ALU.add).then_inc(r_qk, 1)
                dve.wait_ge(r_vT, i + 1)
                V.tensor_copy(rvtok[:], SC2[:].rearrange("p (k q) -> p k q", q=P)).then_inc(r_vtok, 1)
                dve.wait_ge(r_dec, 16 * i + 16)
                for n in range(8):
                    w = T - P * (n % 4)
                    dve.wait_ge(r_s, 8 * i + n + 1)
                    if n >= 4:
                        dve.wait_ge(r_pv, 8 * i + n - 3)
                    V.tensor_tensor(rad[:, n % 4, 0:w], SC[n % 2][:, 0:w], rdec[:, n // 4, 0:w], ALU.mult).then_inc(r_ad, 1)
                dve.wait_ge(r_mean, i + 1)
                V.tensor_tensor(rcen[:], ro[:], SC2[:], ALU.subtract).then_inc(r_cen, 1)
                dve.wait_ge(r_std, i + 1)
                chain.link(V.reciprocal(rstd[:], rstd[:]))
                chain.link(V.scalar_tensor_tensor(rout[:], rcen[:], rw[:, 0:1], rstd[:], ALU.mult, ALU.mult))
                tile_evacuated(dve, m + 3, 4, i)
                V.tensor_tensor(rout[:], rout[:], rsg[:], ALU.mult).then_inc(r_g, 1)
                dve.wait_ge(r_g, i + 1)
                dve.wait_ge(r_hi, i + 1)
                j = ds(i, 1)
                V.tensor_tensor(orl[:, j].rearrange("p a t -> p (a t)"), rout[:], orh[:, j].rearrange("p a t -> p (a t)"),
                                ALU.subtract).then_inc(r_lo, 1)

            V.memset(ones[:], 1.0)
            V.memset(epsc[:], EPS).then_inc(ready, 1)
            clear_squares(0)
            dve.wait_ge(silu_c_done, 1)
            for n in range(KT):
                add_squares(0, n)
            for g in range(8):
                ada_sum(g, 0)
                if g:
                    ada_add(g - 1, 0)
            ada_add(7, 0)
            dve.wait_ge(ada_mod, 8)
            p = 0
            for kind, c, m, n in phases:
                norm_h(p)
                {"ffn": ffn, "mix1": mix1, "mix2": mix2}[kind](c, m, n)
                p += 1
            if last:
                reciprocal_std(PRE_GROUP[p])
            for n in range(KT):
                if last:
                    if n >= 2:
                        dve.wait_ge(out_sent[n % 2], 16 * (n // 2))
                    V.scalar_tensor_tensor(nu[:, n % 2], x[:, n], cols[:, COLS["final"] + n:COLS["final"] + n + 1], rstd[:],
                                           ALU.mult, ALU.mult).then_inc(out_ready, 1)
                else:
                    V.memset(epsc[:], EPS).then_inc(out_ready, 1)
                    dve.wait_ge(out_ready, n + 1)

        @block.tensor
        def _(pe):
            MM = nc.tensor.matmul

            def bank_free(m, n=0, i=0):
                if m >= 2:
                    pe.wait_ge(acc_free[m % 2], lin(m // 2, n // 2, i))

            def slab(c, out, xh, xl, n=0, i=0, tiles=range(KT), first=True, end=True, signal=True, wait=True):
                if wait:
                    pe.wait_ge(lo_done, lin(c + 1, n, i))
                s = c % 2
                for j, k in enumerate(tiles):
                    a, b = xh(k), xl(k)
                    MM(out, wh[s][:, k], a, start=first and j == 0, stop=False)
                    MM(out, wh[s][:, k], b, start=False, stop=False)
                    ins = MM(out, wl[s][:, k], a, start=False, stop=end and j == len(tiles) - 1)
                if signal:
                    ins.then_inc(slab_done, 1)

            def of(h, l, at=0):
                return (lambda k: h[:, k + at]), (lambda k: l[:, k + at])

            def sum_squares(k):
                pe.wait_ge(ssadd, 9 * (k + 1))
                MM(ST[:], ones[:], ssacc[:], start=True, stop=True).then_inc(ss_sum, 1)

            def ada_columns(g, n=0, i=0):
                s = g % 2
                pe.wait_ge(ada_acc, lin(g + 1, n, i))
                if g >= 2:
                    pe.wait_ge(ada_mod, lin(g - 1, n, i))
                b = (TP, OV)[s]
                MM(b[:, 0:1], adac[:, s, 0:P], ones[:, 0:1], start=True, stop=True)
                MM(b[:, 1:2], adac[:, s, P:2 * P], ones[:, 0:1], start=True, stop=True).then_inc(ada_cols, 1)

            def out_tiles(c, m, per, xh, xl, k):
                with pe.Fori(0, KT // 2) as i:
                    for u in range(2):
                        bank_free(m + u, 2, i)
                        for s in range(per):
                            tiles = range(min(KT, FT - KT * s)) if per > 1 else range(KT)
                            a, b = of(xh, xl, KT * s)
                            slab(c + u * per + s, acc[(m + u) % 2][:], a, b, 2 * per, i, tiles, s == 0, s == per - 1)
                sum_squares(k)
                if k in (1, 3, 5):
                    sum_squares(k + 1)

            def ffn(c, m, f):
                for first, runs, ada, load in ADA_RUNS[f]:
                    with pe.Fori(first, first + runs) as i:
                        for u in range(2):
                            if m + u >= 2:
                                bank_free(m + u, 2, i)
                            elif first == 0:
                                pe.wait_ge(acc_free[u], i)
                            else:
                                pe.wait_ge(acc_free[u], i)
                            slab(c + u, acc[(m + u) % 2][:], *of(hh, hl), 2, i)
                        if ada is not None:
                            ada_columns(ada, 2, i)
                            ada_columns(ada + 1, 2, i)
                pe.wait_ge(prodlo, FT * (f + 1))
                out_tiles(c + 2 * FT, m + 2 * FT, 3, act_h, act_l, group_of("ffn", f))

            def mix1(c, m, _):
                bank_free(m)
                slab(c, acc[m % 2][:], *of(hh, hl))
                tile_evacuated(pe, m)
                for h in range(HG):
                    MM((SC0, SC1, SC2, TP)[h][:], wa2[0:16, P * h:P * (h + 1)], nar[0:16, :], start=True, stop=True)\
                        .then_inc(la_ready, 1)
                pe.wait_ge(la_x, HG)
                c, m = c + 1, m + 1
                with pe.Fori(0, HG) as i:
                    gla_head(c, m, i)
                c, m = c + 6 * HG, m + 6 * HG
                with pe.Fori(0, FP) as i:
                    fox_pair(c, m, i)
                c, m = c + 4 * FP, m + 4 * FP
                with pe.Fori(0, KT) as i:
                    bank_free(m, 2, i)
                    slab(c, acc[m % 2][:], *of(hh, hl), 2, i)
                    bank_free(m + 1, 2, i)
                    slab(c + 1, acc[(m + 1) % 2][:], *of(oah, oal), 2, i)
                c, m = c + 2 * KT, m + 2 * KT
                pe.wait_ge(f_lo, FP)
                with pe.Fori(0, KT // 2) as i:
                    for u in range(2):
                        bank_free(m + u, 2, i)
                        slab(c + u, acc[(m + u) % 2][:], *of(obh, obl), 2, i)
                c, m = c + KT, m + KT
                pe.wait_ge(p_lo, KT)
                out_tiles(c, m, 1, oah, oal, group_of("mix1", 0))

            def gla_head(c, m, i):
                def project(u):
                    bank_free(m + u, 6, i)
                    slab(c + u, acc[(m + u) % 2][:], *of(hh, hl), 6, i)
                for u in range(4):
                    project(u)
                pe.wait_ge(g_read, 2 * i)
                for e in range(2):
                    tile_evacuated(pe, m + 2 + e, 6, i)
                    for t in range(TT):
                        ins = nc.tensor.transpose((TP, OV)[e][:, P * t:P * (t + 1)], vt[:, e, P * t:P * (t + 1)], ident[:])
                    ins.then_inc(g_vT, 1)
                project(4)
                pe.wait_ge(g_lev_ready, i + 1)
                pe.wait_ge(g_std, i)
                for l in range(len(LEVELS) + 1):
                    if l >= 2:
                        pe.wait_ge(g_picked, 8 * i + l - 1)
                    for t in range(TT):
                        s = slice(P * t, P * (t + 1))
                        a, b = (lev[:, l, s], lev[:, l, s]) if l < len(LEVELS) else (gk[:, s], gq[:, s])
                        ins = MM(SC[l % 2][:, s], a, b, start=True, stop=True)
                    ins.then_inc(g_scores, 1)
                pe.wait_ge(g_cross_ready, i + 1)
                pe.wait_ge(g_cross_out, 2 * i)
                MM(SC2[:, 0:P], kp[:, 0:P], qp[:, P:2 * P], start=True, stop=True)
                MM(SC2[:, P:3 * P], k0[:], qc[:], start=True, stop=True)
                MM(SC2[:, 3 * P:4 * P], kp[:, 2 * P:3 * P], qp[:, 3 * P:4 * P], start=True, stop=True).then_inc(g_cross, 1)
                MM(ST[:, 0:2 * P], kp[:, P:2 * P], qc[:], start=True, stop=True).then_inc(g_cross, 1)
                project(5)
                pe.wait_ge(g_vtok, 2 * i + 2)
                pe.wait_ge(g_picked, 8 * i + 8)
                pe.wait_ge(g_cross_out, 2 * i + 2)
                for e in range(2):
                    out = (OV, TP)[e]

                    def v(s):
                        return vtok[:, s, P * e:P * (e + 1)]
                    MM(out[:, 0:P], v(0), adiag[:, 0], start=True, stop=False, skip_group_check=True)
                    MM(out[:, P:4 * P], v(0), ac0[:, 0:3 * P], start=False, stop=False, skip_group_check=True)
                    MM(out[:, P:2 * P], v(1), adiag[:, 1], start=False, stop=False, skip_group_check=True)
                    MM(out[:, 2 * P:4 * P], v(1), ac1[:], start=False, stop=False, skip_group_check=True)
                    MM(out[:, 2 * P:3 * P], v(2), adiag[:, 2], start=False, stop=False, skip_group_check=True)
                    MM(out[:, 3 * P:4 * P], v(2), ac0[:, 3 * P:4 * P], start=False, stop=False, skip_group_check=True)
                    MM(out[:, 3 * P:4 * P], v(3), adiag[:, 3], start=False, stop=True, skip_group_check=True).then_inc(g_o, 1)
                pe.wait_ge(g_osum, i + 1)
                MM(SC0[:], ones[:], osum[:], start=True, stop=True).then_inc(g_ss, 1)

            def fox_pair(c, m, i):
                def project(u):
                    bank_free(m + u, 4, i)
                    slab(c + u, acc[(m + u) % 2][:], *of(hh, hl), 4, i)
                for u in range(3):
                    project(u)
                tile_evacuated(pe, m + 2, 4, i)
                for t in range(TT):
                    ins = nc.tensor.transpose(SC2[:, P * t:P * (t + 1)], fv[:, P * t:P * (t + 1)], ident[:])
                ins.then_inc(f_vT, 1)
                project(3)
                pe.wait_ge(m1_in, 64)
                for n in range(8 + 2 + 2):
                    if n < 8:
                        a, t = n // 4, n % 4
                        w = P * (t + 1)
                        h = slice(64 * a, 64 * (a + 1))
                        if n >= 2:
                            pe.wait_ge(f_sm, 8 * i + n - 1)
                        MM(SC[n % 2][:, 0:w], fq[h, P * t:w], fk[h, 0:w], start=True, stop=False)
                        MM(SC[n % 2][:, P * t:w], identb[:], trib[:], start=False, stop=True).then_inc(f_s, 1)
                    if 2 <= n < 10:
                        j = n - 2
                        t = j % 4
                        pe.wait_ge(f_p, 8 * i + j + 1)
                        if j >= 2:
                            pe.wait_ge(f_te, 8 * i + j - 1)
                        for k in range(t + 1):
                            ins = nc.tensor.transpose(TB[j % 2][:, P * k:P * (k + 1)], pb[:, j % 4, P * k:P * (k + 1)], ident[:])
                        ins.then_inc(f_t, 1)
                    if n in (7, 11):
                        a = (n - 7) // 4
                        pe.wait_ge(f_te, 8 * i + 4 * a + 4)
                        if a == 0:
                            pe.wait_ge(f_vtok, i + 1)
                            pe.wait_ge(f_lo, i)
                        for k in range(TT):
                            ins = MM(OV[64 * a:64 * (a + 1), P * k:T], fvtok[:, k, 64 * a:64 * (a + 1)], pt[:, a, k, P * k:T],
                                     start=k == 0, stop=k == TT - 1, skip_group_check=True)
                        if a == 1:
                            ins.then_inc(f_o, 1)

            def mix2(c, m, _):
                for u in range(7):
                    bank_free(m + u)
                    slab(c + u, acc[(m + u) % 2][:], *of(hh, hl))
                pe.wait_ge(n_pe, 4)
                pe.wait_ge(m2_in, 96)
                for kv in range(2):
                    for g in range(2):
                        h = slice(64 * g, 64 * (g + 1))
                        for l in range(32):
                            ins = MM((SC0, SC1, SC2, TP)[2 * kv + g][:, 0:NC], w1[h, kv, l],
                                     cab[h, kv, l // 16, l:l + 16 * (NC - 1) + 1:16], start=l == 0, stop=l == 31)
                        ins.then_inc(n_hid, 1)
                pe.wait_ge(n_act, 4)
                for g in range(2):
                    ins = MM(ST[64 * g:64 * (g + 1), 0:NC], w2[:, 0], chid[:, 0, g], start=True, stop=True)
                ins.then_inc(n_cw, 1)
                for g in range(2):
                    ins = MM(OV[0:NC, 64 * g:64 * (g + 1)], chid[:, 1, g], w2[:, 1], start=True, stop=True)
                ins.then_inc(n_cw, 1)
                tile_evacuated(pe, m + 5)
                tile_evacuated(pe, m + 6)
                for z in range(2):
                    for t in range(TT):
                        ins = nc.tensor.transpose(SC[z][:, P * t:P * (t + 1)], vst[:, z, P * t:P * (t + 1)], ident[:])
                    ins.then_inc(n_vT, 1)
                for t in range(TT):
                    ins = nc.tensor.transpose(SC2[:, 24 * t:24 * (t + 1)], gt24[:, P * t:P * (t + 1)], ident[0:24, 0:24])
                ins.then_inc(n_vT, 1)
                c, m = c + 7, m + 7
                pe.wait_ge(n_vtok, 3)
                pe.wait_ge(n_kc, 2)
                with pe.Fori(0, NP) as i:
                    nsa_pair(c, m, i)
                c, m = c + 4 * NP, m + 4 * NP
                pe.wait_ge(r_in, 64)
                with pe.Fori(0, NP) as i:
                    ret_pair(c, m, i)
                c, m = c + 4 * NP, m + 4 * NP
                with pe.Fori(0, 2) as i:
                    for u in range(2):
                        bank_free(m + u, 2, i)
                        slab(c + u, acc[(m + u) % 2][:], *of(hh, hl), 2, i)
                c, m = c + 4, m + 4
                pe.wait_ge(r_lo, NP)
                with pe.Fori(0, KT // 2) as i:
                    for u in range(2):
                        t = m + 2 * u
                        bank_free(t, 4, i)
                        slab(c + u, acc[t % 2][:], *of(onh, onl), 2, i, range(NP), signal=False)
                        bank_free(t + 1, 4, i)
                        slab(c + u, acc[(t + 1) % 2][:], *of(orh, orl, -NP), 2, i, range(NP, 2 * NP), wait=False)
                c, m = c + KT, m + 2 * KT
                pe.wait_ge(q_lo, KT)
                out_tiles(c, m, 1, mh2, ml2, group_of("mix2", 0))

            def nsa_pair(c, m, i):
                for u in range(4):
                    bank_free(m + u, 4, i)
                    slab(c + u, acc[(m + u) % 2][:], *of(hh, hl), 4, i)

                def half(a):
                    return slice(64 * a, 64 * (a + 1))

                def cmp_scores(a):
                    for t in range(TT):
                        ins = MM(SC2[:, 32 * t:32 * t + NC], nq[half(a), P * t:P * (t + 1)], kct[half(a), 0:NC], start=True, stop=True)
                    ins.then_inc(n_cs, 1)

                def cmp_transpose(a):
                    pe.wait_ge(n_cp, 2 * i + a + 1)
                    for t in range(TT):
                        ins = nc.tensor.transpose(SC2[0:NC, P * t:P * (t + 1)], cb[:, t], ident[:])
                    ins.then_inc(n_ct, 1)

                def cmp_values(a):
                    pe.wait_ge(n_cte, 2 * i + a + 1)
                    if a == 0:
                        pe.wait_ge(n_lo, i)
                    MM(OV[half(a), :], vctok[:, a], ct[:], start=True, stop=False, skip_group_check=True)
                cmp_scores(0)
                for n in range(16 + 4):
                    if n < 16:
                        a, t = n // 8, n % 4
                        w = P * (t + 1)
                        if n >= 2:
                            pe.wait_ge(n_sm, 16 * i + n - 1)
                        MM(SC[n % 2][:, 0:w], nq[half(a), P * t:w], (ks, kw)[(n // 4) % 2][half(a), 0:w], start=True, stop=True)\
                            .then_inc(n_s, 1)
                    if 2 <= n < 18:
                        j = n - 2
                        t = j % 4
                        pe.wait_ge(n_p, 16 * i + j + 1)
                        if j >= 2:
                            pe.wait_ge(n_te, 16 * i + j - 1)
                        for k in range(t + 1):
                            ins = nc.tensor.transpose(TB[j % 2][:, P * k:P * (k + 1)], npb[:, j % 4, P * k:P * (k + 1)], ident[:])
                        ins.then_inc(n_t, 1)
                    if n == 2:
                        cmp_transpose(0)
                    if n == 4:
                        cmp_values(0)
                        cmp_scores(1)
                    if n == 6:
                        cmp_transpose(1)
                    if n == 8:
                        cmp_values(1)
                    if n % 4 == 3 and n >= 7:
                        g = (n - 7) // 4
                        a, br = g // 2, g % 2
                        pe.wait_ge(n_te, 16 * i + 4 * g + 4)
                        for k in range(TT):
                            ins = MM(OV[half(a), P * k:T], (vstok, vwtok)[br][:, k, half(a)], npt[:, g % 2, k, P * k:T],
                                     start=False, stop=br == 1 and k == TT - 1, skip_group_check=True)
                        if g == 3:
                            ins.then_inc(n_o, 1)

            def ret_pair(c, m, i):
                def project(u):
                    bank_free(m + u, 4, i)
                    slab(c + u, acc[(m + u) % 2][:], *of(hh, hl), 4, i)
                project(0)
                project(1)
                for z in range(2):
                    tile_evacuated(pe, m + z, 4, i)
                    MM(SC[z][:], rrot[:], rqr[:, z], start=True, stop=True).then_inc(r_rot, 1)
                project(2)
                tile_evacuated(pe, m + 2, 4, i)
                pe.wait_ge(r_cen, i)
                for t in range(TT):
                    ins = nc.tensor.transpose(SC2[:, P * t:P * (t + 1)], rvt[:, P * t:P * (t + 1)], ident[:])
                ins.then_inc(r_vT, 1)
                project(3)
                pe.wait_ge(r_qk, 2 * i + 2)
                pe.wait_ge(r_vtok, i + 1)
                pe.wait_ge(r_ro, i)
                for n in range(8 + 2):
                    if n < 8:
                        a, s = n // 4, n % 4
                        h = slice(64 * a, 64 * (a + 1))
                        if n >= 2:
                            pe.wait_ge(r_ad, 8 * i + n - 1)
                        MM(SC[n % 2][:, 0:T - P * s], rqk[h, 1, P * s:P * (s + 1)], rqk[h, 0, P * s:T], start=True, stop=True)\
                            .then_inc(r_s, 1)
                    if n >= 2:
                        j = n - 2
                        a, s = j // 4, j % 4
                        h = slice(64 * a, 64 * (a + 1))
                        pe.wait_ge(r_ad, 8 * i + j + 1)
                        MM(OV[h, P * s:T], rvtok[:, s, h], rad[:, j % 4, 0:T - P * s], start=s == 0, stop=s == TT - 1,
                           skip_group_check=True).then_inc(r_pv, 1)
                pe.wait_ge(r_ro, i + 1)
                MM(SC2[:], rblk[:], ro[:], start=True, stop=True).then_inc(r_mean, 1)
                pe.wait_ge(r_sq, i + 1)
                MM(TP[:], rblk[:], rsq[:], start=True, stop=True).then_inc(r_var, 1)

            pe.wait_ge(ready, 1)
            sum_squares(0)
            for g in range(8):
                ada_columns(g)
            p = 0
            for kind, c, m, n in phases:
                pe.wait_ge(h_done, 8 * (p + 1))
                {"ffn": ffn, "mix1": mix1, "mix2": mix2}[kind](c, m, n)
                p += 1


ADA_RUNS = {
    0: [(0, 13, 8, True), (13, 1, 8, False), (14, 8, None, False)],
    1: [(0, 17, 36, True), (17, 1, 36, False), (18, 4, None, False)],
    2: [(0, 22, None, False)],
    3: [(0, 22, None, False)],
}
PRE_GROUP = [0, 2, 4, 6, 7, 8, 9]
PRE_MOD = [(0, 0), (0, 1), (0, 2), (1, 0), (1, 1), (1, 2)]
PRE_GAIN = [COLS["g_pre"], COLS["g_pre"] + 8, COLS["g_pre"] + 16, COLS["norm1"], COLS["norm2"], COLS["norm3"]]


def _tiles(w):
    rows, n = w.shape
    k = -(-rows // D)
    padded = np.zeros((k * D, n), np.float32)
    padded[:rows] = w
    return padded.reshape(k, KT, P, n // P, P).transpose(3, 0, 2, 1, 4).reshape(-1, P, KT, P)


def _ffn_slabs(w_gu, w_dn):
    gu = _tiles(w_gu)
    both = np.stack([gu[:FT], gu[FT:]], 1).reshape(-1, P, KT, P)
    return [both, _tiles(w_dn)]


def _interleave(*lists):
    runs = len(lists[0][0]) // lists[0][1]
    return np.concatenate([s[i * k:(i + 1) * k] for i in range(runs) for s, k in lists])


def _mix1_slabs(w_in, w_pa, w_pb, w_out):
    w = _split_cols(w_in, (512, 512, 1024, 16, 1024, 1024, 1024, 1024, 16, 1024, 1024))
    q_a, k_a, v_a, a_low, r_a, q_b, k_b, v_b, f_b, gate_a, gate_b = w
    narrow = np.zeros((D, P), np.float32)
    narrow[:, 0:16] = a_low
    narrow[:, 32:48] = f_b
    t = _tiles
    return [t(narrow),
            _interleave((t(q_a), 1), (t(k_a), 1), (t(v_a), 2), (t(r_a), 2)),
            _interleave((t(q_b), 1), (t(k_b), 1), (t(v_b), 1), (t(gate_b), 1)),
            _interleave((t(gate_a), 1), (t(w_pa), 1)),
            t(w_pb), t(w_out)]


def _split_cols(w, widths):
    return np.split(w, np.cumsum(widths)[:-1], axis=1)


def _mix2_slabs(w_in, w_nsa, w_ret, w_out):
    w = _split_cols(w_in, (512, 128, 128, 128, 128, 128, 128, 24, 512, 512, 512, 512, 1024, 1024))
    nq, kc, vc, ks, vs, kw, vw, gates, rq, rk, rv, rg, ga, gb = w
    pairs = [h for j in range(NP) for h in (j, NP + j)]
    nq = nq.reshape(D, 8, 64)[:, pairs].reshape(D, 512)
    w_nsa = w_nsa.reshape(8, 64, D)[pairs].reshape(512, D)
    narrow = np.zeros((D, P), np.float32)
    narrow[:, 0:24] = gates
    t = _tiles
    gb = t(gb)
    return [t(kc), t(vc), t(ks), t(vs), t(kw), t(vw), t(narrow),
            _interleave((t(nq), 1), (t(ga), 2), (gb[:4], 1)),
            _interleave((t(rq), 1), (t(rk), 1), (t(rv), 1), (t(rg), 1)),
            gb[4:], t(np.concatenate([w_nsa, w_ret])), t(w_out)]


def _ada_pieces(w):
    return w.reshape(KT, P, 36, 256).transpose(2, 1, 0, 3)


def _constants():
    f = np.float32
    c = {"ident": np.eye(P, dtype=f)}
    p, j = np.arange(P)[:, None], np.arange(P)[None, :]
    levels = [((p // b == j // b) & (p % b < b // 2) & (j % b >= b // 2)) for b in LEVELS] + [p == j]
    c["lmask"] = np.stack(levels, 1).astype(np.int32)
    c["segm"] = np.broadcast_to((np.arange(T) % P != 0).astype(f), (P, T)).copy()
    tri = np.where(j <= p, 0, NEG).astype(f)
    c["trib"] = tri.astype(mybir.dt.np(BF16))
    c["identb"] = c["ident"].astype(mybir.dt.np(BF16))
    c["causal"] = np.concatenate([np.zeros((P, T - P), f), tri], 1)
    t = np.arange(T).reshape(TT, P).T[:, :, None]
    end = (np.arange(NC) * 16 + 31)[None, None, :]
    c["cmask"] = np.where(end <= t, 0, NEG).astype(f)
    c["cvalid"] = (t[:, :, 0] >= 31).astype(f)
    inv = (f(10000.0) ** (-np.arange(32, dtype=f) / f(32))).astype(f)
    ang = (np.arange(T, dtype=f)[None, :] * np.tile(inv, 4)[:, None]).astype(f)
    c["rcos"], c["rsin"] = np.cos(ang).astype(f), np.sin(ang).astype(f)
    rot = np.zeros((P, P), f)
    for b in range(0, P, 64):
        for d in range(32):
            rot[b + 32 + d, b + d] = -1
            rot[b + d, b + 32 + d] = 1
    c["rrot"] = rot
    c["rblk"] = np.kron(np.eye(2), np.full((64, 64), 1 / 64)).astype(f)
    g = np.log1p(-2.0 ** (-5.0 - np.arange(8)))[:, None, None]
    diff = np.arange(T)[None, None, :] - np.arange(P)[None, :, None]
    c["rdec"] = np.where(diff >= 0, np.exp(g * np.maximum(diff, 0)), 0).astype(f)
    return c


def _layout(i):
    def c(v):
        return np.asarray(v, np.float32).reshape(-1, P).T
    b_f = np.zeros((P, 1), np.float32)
    b_f[32:48, 0] = i["b_f"][0]
    table = {"c1": c(i["c"]), "c2": c(i["c_2"]), "b_ada1": c(i["b_ada"]), "b_ada2": c(i["ada_b_2"]),
             "g_pre": c(i["g_pre"]), "g_post": c(i["g_post"]), "norm1": c(i["norm1_w_2"]), "norm2": c(i["norm2_w_2"]),
             "norm3": c(i["norm3_w_2"]), "final": c(i["final_norm_w_2"]), "b_a": c(i["b_a"]), "g_gla": c(i["g_gla"]),
             "b_f": b_f, "ret_norm": c(i["ret_norm_w_2"])}
    arrays = {"cols": np.concatenate([table[n] for n in COLS], 1)}
    slabs = (_ffn_slabs(i["w_gu1"][0], i["w_dn1"][0])
             + _mix1_slabs(i["w_in"][0], i["w_pa"][0], i["w_pb"][0], i["w_out"][0])
             + _ffn_slabs(i["w_gu2"][0], i["w_dn2"][0])
             + _ffn_slabs(i["ffn1_w_in_2"][0], i["ffn1_w_out_2"][0])
             + _mix2_slabs(i["w_in_2"][0], i["w_nsa_up_2"][0], i["w_ret_up_2"][0], i["w_out_2"][0])
             + _ffn_slabs(i["ffn2_w_in_2"][0], i["ffn2_w_out_2"][0]))
    arrays["slabs"] = np.concatenate(slabs)
    arrays["ada"] = np.concatenate([_ada_pieces(i["w_ada"][0]), _ada_pieces(i["ada_w_2"][0])])
    arrays["xt"] = i["x"][0].T.reshape(KT, P, T).transpose(1, 0, 2)
    arrays["w_a2"] = i["w_a2"][0]
    w1 = np.stack([i["cmp_k_w1_2"][0], i["cmp_v_w1_2"][0]]).reshape(2, 32, 64, P).transpose(2, 0, 1, 3)
    arrays["w1"] = np.concatenate([w1, w1])
    arrays["w2"] = np.stack([i["cmp_k_w2_2"][0], i["cmp_v_w2_2"][0]], 1)
    pe = np.stack([i["cmp_k_pe_2"][0].T, i["cmp_v_pe_2"][0].T], 1)
    arrays["cpe"] = np.concatenate([pe, pe])
    arrays.update(_constants())
    return {k: np.ascontiguousarray(v) for k, v in arrays.items()}


def kernel(**inputs):
    import concourse.bacc as bacc
    from concourse.bass_utils import run_bass_kernel_spmd

    arrays = _layout({k: np.asarray(v) for k, v in inputs.items()})
    nc = bacc.Bacc("TRN2", target_bir_lowering=False, num_devices=1)
    tensors = {k: nc.dram_tensor(k + "_dram", v.shape, mybir.dt.from_np(v.dtype), kind="ExternalInput").ap()
               for k, v in arrays.items()}
    tensors["out"] = nc.dram_tensor("out_dram", (P, KT, T), F32, kind="ExternalOutput").ap()
    tensors["fneg_dram"] = nc.dram_tensor("fneg_scratch", (16, T), F32, kind="Internal").ap()
    build(nc, tensors)
    r = run_bass_kernel_spmd(nc, [{k + "_dram": v for k, v in arrays.items()}], core_ids=[0])
    out = r.results[0]["out_dram"]
    return out.transpose(2, 1, 0).reshape(1, T, D)
```

```python
from contextlib import ExitStack

import numpy as np

import concourse.bass as bass
from concourse import mybir

ALU = mybir.AluOpType
ACT = mybir.ActivationFunctionType
AX = mybir.AxisListType
F32 = mybir.dt.float32
F32R = mybir.dt.float32r
BF16 = mybir.dt.bfloat16

P = 128
D = 1024
T = 512
DF = 2816
KT = D // P
FT = DF // P
TT = T // P
EPS = 1e-6
NEG = -1e30
HG = 4
FP = 8
NP = 4
NC = T // 16 - 1
LEVELS = (128, 64, 32, 16, 8, 4, 2)

COLS = {}


def _cols(names):
    at = 0
    for name, n in names:
        COLS[name] = at
        at += n
    return at


NCOLS = _cols([("c1", 8), ("c2", 8), ("b_ada1", 72), ("b_ada2", 72), ("g_pre", 24), ("g_post", 24),
               ("norm1", 8), ("norm2", 8), ("norm3", 8), ("final", 8), ("b_a", 4), ("g_gla", 8),
               ("b_f", 1), ("ret_norm", 4)])

FFN_SLABS = 2 * FT + 3 * KT
NSA_LINKS = 28
RET_LINKS = 4


def plan(stages):
    out, c, m = [], 0, 0
    for kind, n in stages:
        out.append((kind, c, m, n))
        if kind == "ffn":
            c += FFN_SLABS
            m += 2 * FT + KT
        elif kind == "mix1":
            c += 1 + 6 * HG + 4 * FP + 3 * KT + KT
            m += 1 + 6 * HG + 4 * FP + 3 * KT + KT
        elif kind == "mix2":
            c += 6 + 1 + 4 * NP + 4 * NP + 4 + KT + KT
            m += 6 + 1 + 4 * NP + 4 * NP + 4 + 2 * KT + KT
    return out, c


STAGES = [("ffn", 0), ("mix1", 0), ("ffn", 1), ("ffn", 2), ("mix2", 0), ("ffn", 3)]


class Chain:

    def __init__(self, engine, sem):
        self.engine, self.sem, self.base, self.k, self.per, self.i = engine, sem, 0, 0, 0, 0

    def link(self, instruction):
        instruction.then_inc(self.sem, 1)
        self.k += 1
        self.engine.wait_ge(self.sem, self.base + self.k + self.per * self.i)

    def enter(self, i, per):
        self.base, self.k, self.per, self.i = self.base + self.k, 0, per, i

    def leave(self, runs):
        assert self.k == self.per, f"{self.k} links in the body, {self.per} said"
        self.base, self.k, self.per, self.i = self.base + self.per * runs, 0, 0, 0


def build(nc, A, stages=STAGES, last=True):
    phases, n_slabs = plan(stages)
    ds = bass.ds
    with ExitStack() as ctx:
        def sem(name):
            return ctx.enter_context(nc.semaphore(name))

        cursor = [nc.sbuf_base + (-nc.sbuf_base) % 64]

        def sb(name, shape, dt=F32):
            size = int(np.prod(shape[1:])) * {BF16: 2}.get(dt, 4)
            t = nc.alloc_sbuf_tensor_at(name, shape, dt, offset=cursor[0])
            cursor[0] += size + (-size) % 64
            assert cursor[0] <= nc.sbuf_usable_end, (name, cursor[0] - nc.sbuf_usable_end)
            return t

        x = sb("x", [P, KT, T])
        h_at = cursor[0]
        hh = sb("h_hi", [P, KT, T], F32R)
        hl = sb("h_lo", [P, KT, T], F32R)
        h_end = cursor[0]
        cursor[0] = h_at
        y = sb("y", [P, KT, T])
        cursor[0] = h_end
        raw = sb("raw", [P, 2, KT, P])
        wh = [sb(f"w_hi{s}", [P, KT, P], F32R) for s in range(2)]
        wl = [sb(f"w_lo{s}", [P, KT, P], F32R) for s in range(2)]
        ssacc = sb("ssacc", [P, T])
        sq = sb("sq", [P, 2, T])
        rstd = sb("rstd", [P, T])
        rcol = sb("rcol", [P, TT])
        ones = sb("ones", [P, P])
        ident = sb("ident", [P, P])
        cols = sb("cols", [P, NCOLS])
        silu_c = sb("silu_c", [P, 2, KT])
        mod = sb("mod", [P, 2, 72])
        pre_a = sb("pre_a", [P, KT])
        post_g = sb("post_g", [P, KT])
        epsc = sb("epsc", [P, 1])
        tick = sb("tick", [1, 8])
        wa2 = sb("wa2", [16, 4 * P])
        shared = cursor[0]

        act_h = sb("act_hi", [P, FT, T], F32R)
        act_l = sb("act_lo", [P, FT, T], F32R)
        sg = sb("sg", [P, T])
        prod = sb("prod", [P, T])
        adaw = sb("adaw", [P, 2, KT, 256])
        adac = sb("adac", [P, 2, 256])
        ada_end = cursor[0]
        cursor[0] = shared
        ada0 = sb("ada0", [P, ADA0, KT, 256])
        ada_row = sb("ada_row", [1, ADA0 // 2, T])
        cursor[0] = ada_end
        nu = sb("norm_u", [P, 3, T])
        nv = sb("norm_v", [P, 2, T])

        cursor[0] = shared
        oah = sb("oa_hi", [P, KT, T], F32R)
        oal = sb("oa_lo", [P, KT, T], F32R)
        fneg16 = sb("fneg16", [48, T])
        ob_at = cursor[0]
        lac = sb("lac", [P, HG, T])
        cs = sb("cs", [P, T])
        lev = sb("lev", [P, len(LEVELS), T])
        lmask = sb("lmask", [P, len(LEVELS) + 1, P], mybir.dt.int32)
        segm = sb("segm", [P, T])
        lt4 = sb("lt4", [P, HG, T])
        nar = sb("nar", [48, T])
        nar2 = sb("nar2", [48, T])
        gq = sb("gq", [P, T])
        gk = sb("gk", [P, T])
        eq = sb("eq", [P, T])
        ek = sb("ek", [P, T])
        qp = sb("qp", [P, T])
        kp = sb("kp", [P, T])
        qc = sb("qc", [P, 2 * P])
        k0 = sb("k0", [P, P])
        vt = sb("vt", [P, 2, T])
        vtok = sb("vtok", [P, TT, 2 * P])
        adiag = sb("adiag", [P, TT, P])
        ac0 = sb("ac0", [P, T])
        ac1 = sb("ac1", [P, 2 * P])
        sr = sb("sr", [P, 2, T])
        osq = sb("osq", [P, 2, T])
        osum = sb("osum", [P, T])
        og = sb("og", [P, 2, T])
        gsel = sb("gsel", [P, 2])
        cursor[0] = ob_at
        obh = sb("ob_hi", [P, KT, T], F32R)
        obl = sb("ob_lo", [P, KT, T], F32R)
        sgb = sb("sgb", [P, KT, T])
        att_at = cursor[0]
        fq = sb("fq", [P, 2, T])
        fk = sb("fk", [P, 2, T])
        fv = sb("fv", [P, T])
        fvtok = sb("fvtok", [P, TT, P])
        fneg = (sb("fneg", [P, 2, T]), sq)
        pb = sb("pb", [P, 4, T])
        pt = sb("pt", [P, 2, TT, T])
        nm = sb("nm", [P, 8])
        rs = sb("rs", [P, 8])
        ri = sb("ri", [P, 8])
        identb = sb("identb", [P, P], BF16)
        trib = sb("trib", [P, P], BF16)
        cursor[0] = att_at
        mg = sb("mg", [P, KT, T])
        sga1 = sb("sga1", [P, T])
        mt = sb("mt", [P, 2, T])

        cursor[0] = shared
        onh = sb("on_hi", [P, NP, T], F32R)
        onl = sb("on_lo", [P, NP, T], F32R)
        orh = sb("or_hi", [P, NP, T], F32R)
        orl = sb("or_lo", [P, NP, T], F32R)
        gates_at = cursor[0]
        sga2 = sb("sga2", [P, KT, T])
        sgb2 = sb("sgb2", [P, KT, T])
        m2_at = cursor[0]
        cursor[0] = gates_at
        w1 = sb("w1", [P, 2, 16, P])
        cursor[0] = m2_at
        ks = sb("ks", [P, T])
        kw = sb("kw", [P, T])
        vstok = sb("vstok", [P, TT, P])
        vwtok = sb("vwtok", [P, TT, P])
        kct = sb("kct", [P, 32])
        vctok = sb("vctok", [NC, 2, 64])
        gtok = sb("gtok", [P, TT, 24])
        gcur = sb("gcur", [P, 2, 3, TT])
        causal = sb("causal", [P, T])
        cmask = sb("cmask", [P, TT, NC])
        cvalid = sb("cvalid", [P, TT])
        loop_at = cursor[0]
        craw = sb("craw", [P, 2, T])
        cpe = sb("cpe", [P, 2, 32])
        cab = sb("cab", [P, 2, 2, T])
        chid = sb("chid", [P, 2, 2, NC])
        w2 = sb("w2", [P, 2, 64])
        vst = sb("vst", [P, 2, T])
        gt24 = sb("gt24", [24, T])
        cursor[0] = loop_at
        nq = sb("nq", [P, T])
        npb = sb("npb", [P, 4, T])
        npt = sb("npt", [P, 2, TT, T])
        nnm = sb("nnm", [P, 16])
        nrs = sb("nrs", [P, 16])
        nri = sb("nri", [P, 16])
        cb = sb("cb", [P, TT, NC])
        cm = sb("cm", [P, TT])
        csum = sb("csum", [P, TT])
        ct = sb("ct", [NC, T])
        cursor[0] = m2_at
        rqr = sb("rqr", [P, 2, T])
        rqk = sb("rqk", [P, 2, T])
        rtmp = sb("rtmp", [P, 2, T])
        rcos = sb("rcos", [P, T])
        rsin = sb("rsin", [P, T])
        rrot = sb("rrot", [P, P])
        rblk = sb("rblk", [P, P])
        rvt = sb("rvt", [P, T])
        rvtok = sb("rvtok", [P, TT, P])
        rdec = sb("rdec", [P, 2, T])
        rad = sb("rad", [P, 4, T])
        rsg = sb("rsg", [P, T])
        ro = sb("ro", [P, T])
        rcen = sb("rcen", [P, T])
        rsq = sb("rsq", [P, T])
        rout = sb("rout", [P, T])
        rw = sb("rw", [P, 1])
        cursor[0] = m2_at
        mh2 = sb("m2_hi", [P, KT, T], F32R)
        ml2 = sb("m2_lo", [P, KT, T], F32R)
        mt2 = sb("mt2", [P, 4, T])

        bank = [ctx.enter_context(nc.psum_tensor(f"bank{b}", [P, T], F32)) for b in range(8)]
        acc = bank[0:2]
        ST, SC0, SC1, SC2, TP, OV = bank[2:8]
        SC = [SC0, SC1]
        TB = [TP, ST]
        RSTD = SC1

        raw_in = [sem("raw_in0"), sem("raw_in1")]
        hi_done, lo_done = sem("hi_done"), sem("lo_done")
        slab_done = sem("slab_done")
        acc_free = [sem("acc_free0"), sem("acc_free1")]
        cols_in = sem("cols_in")
        const_in, x_in = sem("const_in"), sem("x_in")
        dve_chain, act_chain = sem("dve_chain"), sem("act_chain")
        silu_c_done = sem("silu_c_done")
        ready = sem("ready")
        ada_in = [sem("ada_in0"), sem("ada_in1")]
        ada0_in = [sem(f"ada0_in{z}") for z in range(ADA0 // 2)]
        ada0_rows, ada0_row_out, ada0_cols = sem("ada0_rows"), sem("ada0_row_out"), sem("ada0_cols")
        ada_acc, ada_cols, ada_mod = sem("ada_acc"), sem("ada_cols"), sem("ada_mod")
        sq_done, ssadd, ss_sum, std_done = sem("sq_done"), sem("ssadd"), sem("ss_sum"), sem("std_done")
        rcol_done, rstd_done = sem("rcol_done"), sem("rstd_done")
        y_done, u_done, v_done, hh_done, h_done = sem("y_done"), sem("u_done"), sem("v_done"), sem("hh_done"), sem("h_done")
        x_done = sem("x_done")
        prodhi, prodlo = sem("prodhi"), sem("prodlo")
        out_ready = sem("out_ready")
        m1_in = sem("m1_in")
        la_ready, la_x, la_l, la_done = sem("la_ready"), sem("la_x"), sem("la_l"), sem("la_done")
        f_stored, fneg_in = sem("f_stored"), sem("fneg_in")
        g_lev_diff, g_lev_exp, g_cross_exp = sem("g_lev_diff"), sem("g_lev_exp"), sem("g_cross_exp")
        g_lev_ready, g_cross_ready = sem("g_lev_ready"), sem("g_cross_ready")
        g_vT, g_vtok, g_scores, g_picked = sem("g_vT"), sem("g_vtok"), sem("g_scores"), sem("g_picked")
        g_cross, g_cross_out, g_o, g_osq = sem("g_cross"), sem("g_cross_out"), sem("g_o"), sem("g_osq")
        g_osum, g_ss, g_std, g_read = sem("g_osum"), sem("g_ss"), sem("g_std"), sem("g_read")
        g_gated, g_hi, g_lo = sem("g_gated"), sem("g_hi"), sem("g_lo")
        f_vT, f_vtok, f_s, f_sm, f_e = sem("f_vT"), sem("f_vtok"), sem("f_s"), sem("f_sm"), sem("f_e")
        f_p, f_t, f_te, f_o, f_hi, f_lo = sem("f_p"), sem("f_t"), sem("f_te"), sem("f_o"), sem("f_hi"), sem("f_lo")
        p_sum, p_hi, p_lo = sem("p_sum"), sem("p_hi"), sem("p_lo")
        n_swap = sem("n_swap")
        m2_in, n_pe, n_hid, n_act = sem("m2_in"), sem("n_pe"), sem("n_hid"), sem("n_act")
        n_cw, n_kc, n_vT, n_vtok = sem("n_cw"), sem("n_kc"), sem("n_vT"), sem("n_vtok")
        n_cs, n_cd, n_ce, n_cp, n_ct, n_cte = (sem(f"n_{z}") for z in ("cs", "cd", "ce", "cp", "ct", "cte"))
        n_s, n_sm, n_e, n_p, n_t, n_te, n_o, n_hi, n_lo = (sem(f"n_{z}") for z in ("s", "sm", "e", "p", "t", "te", "o", "hi", "lo"))
        r_in, r_dec, r_rot, r_qk, r_vT, r_vtok = (sem(f"r_{z}") for z in ("in", "dec", "rot", "qk", "vT", "vtok"))
        r_s, r_ad, r_pv, r_ro, r_mean, r_cen = (sem(f"r_{z}") for z in ("s", "ad", "pv", "ro", "mean", "cen"))
        r_sq, r_var, r_std, r_g, r_hi, r_lo = (sem(f"r_{z}") for z in ("sq", "var", "std", "g", "hi", "lo"))
        q_half = sem("q_half")
        q_sum, q_hi, q_lo = sem("q_sum"), sem("q_hi"), sem("q_lo")
        out_sent = [sem("out_sent0"), sem("out_sent1")]

        def lin(c, n=0, i=0):
            return c + n * i if n else c

        def group_of(kind, n):
            return {("x", 0): 0, ("ffn", 0): 1, ("mix1", 0): 3, ("ffn", 1): 5, ("ffn", 2): 7,
                    ("mix2", 0): 8, ("ffn", 3): 9}[kind, n]

        def tile_evacuated(eng, m, n=0, i=0):
            eng.wait_ge(acc_free[m % 2], lin(m // 2 + 1, n // 2, i))

        block = ctx.enter_context(nc.Block())

        @block.sync
        def _(sp):
            W = A["slabs"]
            for c in range(2):
                sp.dma_start(raw[:, c], W[c]).then_inc(raw_in[c], 16)
            with sp.Fori(1, n_slabs // 2) as i:
                for s in range(2):
                    sp.wait_ge(lo_done, 2 * i + s - 1)
                    sp.dma_start(raw[:, s], W[ds(2 * i + s, 1)].rearrange("a p k n -> p (a k) n"))\
                      .then_inc(raw_in[s], 16)
            if n_slabs % 2:
                sp.wait_ge(lo_done, n_slabs - 2)
                sp.dma_start(raw[:, 0], W[n_slabs - 1]).then_inc(raw_in[0], 16)

        @block.gpsimd
        def _(pool):
            def low(s, c):
                pool.wait_ge(hi_done, c + 1)
                nc.gpsimd.tensor_tensor(wl[s][:], raw[:, s], wh[s][:], ALU.subtract).then_inc(lo_done, 1)
            def lows(first, end):
                if first % 2:
                    low(1, first)
                    first += 1
                with pool.Fori(first // 2, end // 2) as i:
                    for s in range(2):
                        low(s, 2 * i + s)
                if end % 2:
                    low(0, end - 1)

            def add_squares(k):
                for j in range(KT - 2):
                    pool.wait_ge(sq_done, 8 * k + j + 1)
                    pool.wait_ge(ssadd, 9 * k + j + 1)
                    nc.gpsimd.tensor_tensor(ssacc[:], ssacc[:], sq[:, j % 2], ALU.add).then_inc(ssadd, 1)

            def shift_h(p):
                b, v = PRE_MOD[p]
                for n in range(KT):
                    pool.wait_ge(u_done, 8 * p + n + 1)
                    if n >= 2:
                        pool.wait_ge(h_done, 8 * p + n - 1)
                    nc.gpsimd.tensor_scalar(nv[:, n % 2], nu[:, n % 3], pre_a[:, n:n + 1],
                                            mod[:, b, 24 * v + n:24 * v + n + 1], ALU.mult, ALU.add).then_inc(v_done, 1)

            low(0, 0)
            low(1, 1)
            p = 0
            for kind, c, m, n in phases:
                shift_h(p)
                p += 1
                lows(c + 2, min(phases[p][1] + 2 if p < len(phases) else n_slabs, n_slabs))
                if kind == "mix1" or (kind == "ffn" and n < 2):
                    add_squares(group_of(kind, n) + 1)

        @block.scalar
        def _(act):
            chain = Chain(act, act_chain)

            def high(c, n=0, i=0):
                if c >= n_slabs and not n:
                    return
                act.wait_ge(raw_in[c % 2], lin(16 * (c // 2 + 1), 8 * n, i))
                if c >= 2:
                    act.wait_ge(slab_done, lin(c - 1, n, i))
                nc.scalar.activation(wh[c % 2][:], raw[:, c % 2], ACT.Copy).then_inc(hi_done, 1)

            def ada_load(e, n=0, i=0):
                if e >= 2:
                    act.wait_ge(ada_acc, lin(e - 1, n, i))
                piece = A["ada"][ds(lin(e + ADA0, n, i), 1)].rearrange("a p k n -> p (a k) n")
                act.dma_start(adaw[:, e % 2], piece).then_inc(ada_in[e % 2], 16)

            def square(src, k, j, n=0, i=0):
                if 9 * k + j:
                    act.wait_ge(ssadd, lin(9 * k + j, n, i))
                nc.scalar.activation(sq[:, j % 2], src, ACT.Square).then_inc(sq_done, 1)

            def std(k):
                act.wait_ge(ss_sum, k + 1)
                nc.scalar.activation(rcol[:], ST[:, 0:TT], ACT.Sqrt, scale=1.0 / D, bias=epsc[:, 0:1]).then_inc(std_done, 1)

            def split_h(p, sh):
                for n in range(KT):
                    act.wait_ge(u_done, 8 * p + n + 1)
                    nc.scalar.activation(hh[:, n], nu[:, n % 3], ACT.Identity, scale=pre_a[:, n:n + 1],
                                         bias=sh[:, n:n + 1]).then_inc(hh_done, 1)

            def residual(block1, k):
                if block1:
                    std(k)
                    for n in range(KT):
                        act.wait_ge(x_done, 8 * [1, 3, 5].index(k) + n + 1)
                        square(x[:, n], k + 1, n)

            def out_tiles(c, m, per, block1, k):
                def pair(i, n):
                    for u in range(2):
                        for s in range(per):
                            cc = c + u * per + s
                            act.wait_ge(slab_done, lin(cc + 1, n, i))
                            high(cc + 2, n, i)
                        t = m + u
                        if block1:
                            square(acc[t % 2][:], k, u, 2 if n else 0, i)
                            j = ds(2 * i + u, 1) if n else ds(u, 1)
                            act_y = y[:, j].rearrange("p a t -> p (a t)")
                            nc.scalar.activation(act_y, acc[t % 2][:], ACT.Copy).then_inc(acc_free[t % 2], 1)
                        else:
                            tile_evacuated(act, t, 2 if n else 0, i)
                            j = ds(2 * i + u, 1)
                            square(x[:, j].rearrange("p a t -> p (a t)"), k, u, 2 if n else 0, i)
                end = c + KT * per == n_slabs
                with act.Fori(0, KT // 2 - (1 if end else 0)) as i:
                    pair(i, 2 * per)
                if end:
                    i = KT // 2 - 1
                    for u in range(2):
                        for s in range(per):
                            cc = c + 2 * per * i + u * per + s
                            act.wait_ge(slab_done, cc + 1)
                            high(cc + 2)
                        t = m + 2 * i + u
                        j = 2 * i + u
                        if block1:
                            square(acc[t % 2][:], k, j)
                            nc.scalar.activation(y[:, j], acc[t % 2][:], ACT.Copy).then_inc(acc_free[t % 2], 1)
                        else:
                            tile_evacuated(act, t)
                            square(x[:, j], k, j)

            def ffn(c, m, f):
                def unit(c, m, i, j, pieces):
                    act.wait_ge(slab_done, lin(c + 1, 4, i))
                    high(c + 2, 4, i)
                    act.wait_ge(acc_free[(m + 1) % 2], lin((m + 1) // 2, 2, i))
                    nc.scalar.activation(sg[:], acc[m % 2][:], ACT.Silu).then_inc(acc_free[m % 2], 1)
                    act.wait_ge(slab_done, lin(c + 2, 4, i))
                    high(c + 3, 4, i)
                    tile_evacuated(act, m + 1, 4, i)
                    nc.scalar.activation(act_h[:, ds(j, 1)].rearrange("p a t -> p (a t)"), prod[:], ACT.Copy)\
                        .then_inc(prodhi, 1)
                    for e, n in pieces:
                        ada_load(e + 2, n, i)
                for first, runs, e, per, load in ADA_RUNS[f]:
                    with act.Fori(first, first + runs) as i:
                        for u in range(2):
                            unit(c + 2 * u, m + 2 * u, i, 2 * i + u, ada_pieces(first, e, per, u) if load else [])
                if f == 1:
                    for piece in range(2):
                        ada_load(ADA_RUNS[2][0][2] + piece)
                k = group_of("ffn", f)
                out_tiles(c + 2 * FT, m + 2 * FT, 3, f < 2, k)
                residual(f < 2, k)

            def step(c, n=0, i=0):
                act.wait_ge(slab_done, lin(c + 1, n, i))
                high(c + 2, n, i)

            def leave(dst, m, func=ACT.Copy, **kw):
                nc.scalar.activation(dst, acc[m % 2][:], func, **kw).then_inc(acc_free[m % 2], 1)

            def mix1(c, m, _):
                act.wait_ge(slab_done, c)
                act.wait_ge(h_done, 2 * KT)
                for dst, name in ((lmask, "lmask"), (segm, "segm")):
                    act.dma_start(dst[:], A[name]).then_inc(m1_in, 16)
                step(c)
                nc.scalar.activation(nar[:], acc[m % 2][0:48, :], ACT.Copy).then_inc(acc_free[m % 2], 1)
                tile_evacuated(act, m)
                chain.link(nc.scalar.activation(nar2[32:48, :], nar[32:48, :], ACT.Identity,
                                                bias=cols[32:48, COLS["b_f"]:COLS["b_f"] + 1]))
                chain.link(nc.scalar.activation(nar[32:48, :], nar2[32:48, :], ACT.Abs))
                chain.link(nc.scalar.activation(nar[32:48, :], nar[32:48, :], ACT.Exp, scale=-1.0))
                nc.scalar.activation(nar[32:48, :], nar[32:48, :], ACT.Ln, bias=1.0).then_inc(la_l, 1)
                for h in range(HG):
                    act.wait_ge(la_ready, h + 1)
                    b = COLS["b_a"] + h
                    nc.scalar.activation(lev[:, h], (SC0, SC1, SC2, TP)[h][:], ACT.Identity, bias=cols[:, b:b + 1]).then_inc(la_x, 1)
                act.wait_ge(la_x, HG)
                chain.link(nc.scalar.activation(lt4[:], lev[:, 0:HG], ACT.Abs))
                chain.link(nc.scalar.activation(lt4[:], lt4[:], ACT.Exp, scale=-1.0))
                nc.scalar.activation(lt4[:], lt4[:], ACT.Ln, bias=1.0).then_inc(la_l, 1)
                gla_query(c + 1, m + 1, 0)
                gla_key(c + 1, m + 1, 0)
                act.wait_ge(la_done, 1)
                act.dma_start(A["fneg_dram"], fneg16[32:48, :]).then_inc(f_stored, 16)
                c, m = c + 1, m + 1
                gla_value(c, m, 0, 0)
                gla_exponentials(0)
                gla_head(c, m, 0, True, values=(1,))
                with act.Fori(1, HG - 1) as i:
                    gla_head(c, m, i, True)
                gla_head(c, m, HG - 1, False)
                c, m = c + 6 * HG, m + 6 * HG
                act.wait_ge(f_stored, 16)
                act.wait_ge(g_lo, 2 * HG)
                act.dma_start(identb[:], A["identb"]).then_inc(m1_in, 16)
                act.dma_start(trib[:], A["trib"]).then_inc(m1_in, 16)
                act.dma_start(fneg[0][:], forget_rows(0)).then_inc(fneg_in, 16)
                for z in range(3):
                    fox_step(c, m, z, 0, 0)
                with act.Fori(0, FP // 2 - 1) as i:
                    for u in range(2):
                        fox_pair(c, m, 2 * i + u, u, 4)
                fox_pair(c, m, FP - 2, 0, 4)
                fox_pair(c, m, FP - 1, 1, 1)
                c, m = c + 4 * FP, m + 4 * FP
                act.wait_ge(f_lo, FP)
                with act.Fori(0, KT) as i:
                    step(c, 2, i)
                    act.wait_ge(acc_free[(m + 1) % 2], (m + 1) // 2 + i)
                    leave(sga1[:], m, ACT.Sigmoid)
                    step(c + 1, 2, i)
                c, m = c + 2 * KT, m + 2 * KT
                with act.Fori(0, KT // 2) as i:
                    for u in range(2):
                        step(c + u, 2, i)
                        act.wait_ge(p_sum, 2 * i + u + 1)
                        nc.scalar.activation(oah[:, ds(2 * i + u, 1)].rearrange("p a t -> p (a t)"), mt[:, u], ACT.Copy)\
                            .then_inc(p_hi, 1)
                c, m = c + KT, m + KT
                act.wait_ge(p_lo, KT)
                for piece in range(2):
                    ada_load(ADA_RUNS[1][0][2] + piece)
                k = group_of("mix1", 0)
                out_tiles(c, m, 1, True, k)
                residual(True, k)

            def gla_exponentials(i):
                act.wait_ge(g_lev_diff, i + 1)
                nc.scalar.activation(lev[:], lev[:], ACT.Exp).then_inc(g_lev_exp, 1)
                act.wait_ge(g_cross_ready, i)
                nc.scalar.activation(eq[:], cs[:], ACT.Exp)
                for t in range(TT):
                    ins = nc.scalar.activation(ek[:, P * t:P * (t + 1)], cs[:, P * t:P * (t + 1)], ACT.Exp, scale=-1.0,
                                               bias=cs[:, P * t + P - 1:P * t + P])
                ins.then_inc(g_cross_exp, 1)

            def gla_query(c, m, i):
                step(c, 6, i)
                act.wait_ge(g_scores, 8 * i)
                leave(gq[:], m, scale=float(P) ** -0.5)

            def gla_key(c, m, i):
                step(c + 1, 6, i)
                leave(gk[:], m + 1)

            def gla_value(c, m, i, e):
                step(c + 2 + e, 6, i)
                leave(vt[:, e], m + 2 + e)

            def gla_head(c, m, i, ahead, values=(0, 1)):
                for e in values:
                    gla_value(c, m, i, e)
                step(c + 4, 6, i)
                act.wait_ge(g_gated, 2 * i)
                leave(sr[:, 0], m + 4, ACT.Silu)
                act.wait_ge(g_cross, 2 * i + 1)
                nc.scalar.activation(ac0[:], SC2[:], ACT.Copy).then_inc(g_cross_out, 1)
                act.wait_ge(g_cross, 2 * i + 2)
                nc.scalar.activation(ac1[:], ST[:, 0:2 * P], ACT.Copy).then_inc(g_cross_out, 1)
                step(c + 5, 6, i)
                leave(sr[:, 1], m + 5, ACT.Silu)
                if ahead:
                    gla_exponentials(i + 1)
                act.wait_ge(g_o, 2 * i + 2)
                act.wait_ge(g_osum, i)
                nc.scalar.activation(osq[:, 0], OV[:], ACT.Square).then_inc(g_osq, 1)
                nc.scalar.activation(osq[:, 1], TP[:], ACT.Square).then_inc(g_osq, 1)
                if ahead:
                    gla_query(c, m, i + 1)
                act.wait_ge(g_ss, i + 1)
                nc.scalar.activation(rstd[:], SC0[:], ACT.Sqrt, scale=1.0 / (2 * P), bias=epsc[:, 0:1]).then_inc(g_std, 1)
                if ahead:
                    gla_key(c, m, i + 1)
                for e in range(2):
                    act.wait_ge(g_gated, 2 * i + e + 1)
                    nc.scalar.activation(oah[:, ds(2 * i + e, 1)].rearrange("p a t -> p (a t)"), og[:, e], ACT.Copy)\
                        .then_inc(g_hi, 1)

            def forget_rows(i):
                return A["fneg_dram"][ds(2 * i, 2), :].rearrange("(o a) t -> o a t", o=1).to_broadcast([P, 2, T])

            def fox_step(c, m, z, i, u):
                step(c + z, 4, i)
                if z == 0:
                    leave(fq[:, u], m, scale=0.125)
                elif z == 1:
                    leave(fk[:, u], m + 1)
                elif z == 2:
                    act.wait_ge(f_vT, i)
                    leave(fv[:], m + 2)
                else:
                    leave(sgb[:, ds(i, 1)].rearrange("p a t -> p (a t)"), m + 3, ACT.Sigmoid)

            def fox_pair(c, m, i, u, slabs):
                behind = 0
                for n in range(8 + 2):
                    if n in (2, 5, 7) and behind < slabs:
                        fox_step(c, m, (behind + 3) % 4, i + (behind > 0), u if behind == 0 else 1 - u)
                        behind += 1
                    if n < 8:
                        w = P * (n % 4 + 1)
                        act.wait_ge(f_sm, 8 * i + n + 1)
                        nc.scalar.activation(pb[:, n % 4, 0:w], pb[:, n % 4, 0:w], ACT.Exp, scale=-1.0,
                                             bias=nm[:, n:n + 1], accum_out=rs[:, n:n + 1]).then_inc(f_e, 1)
                    if n >= 2:
                        j = n - 2
                        a, t = j // 4, j % 4
                        act.wait_ge(f_t, 8 * i + j + 1)
                        nc.scalar.activation(pt[:, a, 0:t + 1, P * t:P * (t + 1)],
                                             TB[j % 2][:, 0:P * (t + 1)].rearrange("p (k q) -> p k q", q=P), ACT.Copy)\
                            .then_inc(f_te, 1)
                    if n == 1 and slabs > 1:
                        act.dma_start(fneg[1 - u][:], forget_rows(i + 1)).then_inc(fneg_in, 16)
                for z in range(behind, slabs):
                    fox_step(c, m, (z + 3) % 4, i + (z > 0), u if z == 0 else 1 - u)
                act.wait_ge(f_o, i + 1)
                nc.scalar.activation(obh[:, ds(i, 1)].rearrange("p a t -> p (a t)"), OV[:], ACT.Copy).then_inc(f_hi, 1)

            def mix2(c, m, _):
                act.wait_ge(h_done, 5 * KT)
                for dst, name in ((w1, "w1"), (w2, "w2"), (cpe, "cpe"), (causal, "causal"), (cmask, "cmask"), (cvalid, "cvalid")):
                    act.dma_start(dst[:], A[name]).then_inc(m2_in, 16)
                for u, dst in enumerate((craw[:, 0], craw[:, 1], ks[:], vst[:, 0], kw[:], vst[:, 1])):
                    step(c + u)
                    leave(dst, m + u)
                step(c + 6)
                nc.scalar.activation(gt24[:], acc[(m + 6) % 2][0:24, :], ACT.Sigmoid).then_inc(acc_free[(m + 6) % 2], 1)
                for kv in range(2):
                    for g in range(2):
                        z = 2 * kv + g
                        act.wait_ge(n_hid, z + 1)
                        nc.scalar.activation(chid[:, kv, g], (SC0, SC1, SC2, TP)[z][:, 0:NC], ACT.Silu).then_inc(n_act, 1)
                act.wait_ge(n_cw, 1)
                nc.scalar.activation(kct[:, 0:NC], ST[:, 0:NC], ACT.Copy).then_inc(n_kc, 1)
                act.wait_ge(n_cw, 2)
                nc.scalar.activation(vctok[:].rearrange("n g d -> n (g d)"), OV[0:NC, 0:P], ACT.Copy).then_inc(n_kc, 1)
                c, m = c + 7, m + 7
                step(c)
                leave(nq[:], m, scale=0.125)
                with act.Fori(0, NP - 1) as i:
                    nsa_pair(c, m, i, 4)
                nsa_pair(c, m, NP - 1, 3)
                c, m = c + 4 * NP, m + 4 * NP
                act.wait_ge(n_lo, NP)
                for dst, name in ((rcos, "rcos"), (rsin, "rsin"), (rrot, "rrot"), (rblk, "rblk")):
                    act.dma_start(dst[:], A[name]).then_inc(r_in, 16)
                act.dma_start(rdec[:], decays(0)).then_inc(r_dec, 16)
                for z in range(3):
                    ret_step(c, m, z, 0)
                with act.Fori(0, NP - 1) as i:
                    ret_pair(c, m, i, False)
                ret_pair(c, m, NP - 1, True)
                c, m = c + 4 * NP + 4, m + 4 * NP + 4
                with act.Fori(0, KT // 2) as i:
                    for u in range(2):
                        step(c + u, 2, i)
                        act.wait_ge(q_sum, 2 * i + u + 1)
                        nc.scalar.activation(mh2[:, ds(2 * i + u, 1)].rearrange("p a t -> p (a t)"), mt2[:, u], ACT.Copy)\
                            .then_inc(q_hi, 1)
                c, m = c + KT, m + 2 * KT
                k = group_of("mix2", 0)
                out_tiles(c, m, 1, False, k)

            def nsa_pair(c, m, i, slabs):
                def cmp_exp(a):
                    act.wait_ge(n_cd, 2 * i + a + 1)
                    nc.scalar.activation(cb[:], cb[:], ACT.Exp).then_inc(n_ce, 1)

                def cmp_out(a):
                    act.wait_ge(n_ct, 2 * i + a + 1)
                    nc.scalar.activation(ct[:], SC2[0:NC, :], ACT.Copy).then_inc(n_cte, 1)
                cmp_exp(0)
                for n in range(16 + 2):
                    if n in (3, 7):
                        u = n // 7
                        step(c + 1 + u, 4, i)
                        leave(sga2[:, ds(2 * i + u, 1)].rearrange("p a t -> p (a t)"), m + 1 + u, ACT.Sigmoid)
                    if n == 11:
                        step(c + 3, 4, i)
                        leave(sgb2[:, ds(i, 1)].rearrange("p a t -> p (a t)"), m + 3, ACT.Sigmoid)
                    if n < 16:
                        w = P * (n % 4 + 1)
                        act.wait_ge(n_sm, 16 * i + n + 1)
                        nc.scalar.activation(npb[:, n % 4, 0:w], npb[:, n % 4, 0:w], ACT.Exp, scale=-1.0,
                                             bias=nnm[:, n:n + 1], accum_out=nrs[:, n:n + 1]).then_inc(n_e, 1)
                    if n >= 2:
                        j = n - 2
                        t = j % 4
                        act.wait_ge(n_t, 16 * i + j + 1)
                        nc.scalar.activation(npt[:, (j // 4) % 2, 0:t + 1, P * t:P * (t + 1)],
                                             TB[j % 2][:, 0:P * (t + 1)].rearrange("p (k q) -> p k q", q=P), ACT.Copy)\
                            .then_inc(n_te, 1)
                    if n == 4:
                        cmp_out(0)
                    if n == 7:
                        cmp_exp(1)
                    if n == 10:
                        cmp_out(1)
                if slabs == 4:
                    act.wait_ge(slab_done, lin(c + 5, 4, i))
                    act.wait_ge(n_s, 16 * i + 16)
                    leave(nq[:], m + 4, scale=0.125)
                    high(c + 6, 4, i)
                act.wait_ge(n_o, i + 1)
                nc.scalar.activation(onh[:, ds(i, 1)].rearrange("p a t -> p (a t)"), OV[:], ACT.Copy).then_inc(n_hi, 1)

            def decays(i):
                return A["rdec"][ds(2 * i, 2)].rearrange("a p t -> p a t")

            def ret_step(c, m, z, i):
                step(c + z, 4, i)
                if z < 2:
                    act.wait_ge(r_qk, 2 * i)
                    leave(rqr[:, z], m + z, scale=(1.0, 0.125)[z])
                elif z == 2:
                    act.wait_ge(r_vT, i)
                    leave(rvt[:], m + 2)
                else:
                    act.wait_ge(r_lo, i)
                    leave(rsg[:], m + 3, ACT.Silu)

            def ret_pair(c, m, i, last_pair):
                def among(z):
                    if not last_pair:
                        ret_step(c, m, z, i + 1)
                    else:
                        step(c + 4 + z, 4, i)
                        leave(sgb2[:, 4 + z], m + 4 + z, ACT.Sigmoid)
                ret_step(c, m, 3, i)
                if not last_pair:
                    act.wait_ge(r_ad, 8 * i + 8)
                    act.dma_start(rdec[:], decays(i + 1)).then_inc(r_dec, 16)
                act.wait_ge(r_pv, 8 * i + 8)
                nc.scalar.activation(ro[:], OV[:], ACT.Copy).then_inc(r_ro, 1)
                among(0)
                act.wait_ge(r_cen, i + 1)
                nc.scalar.activation(rsq[:], rcen[:], ACT.Square).then_inc(r_sq, 1)
                among(1)
                act.wait_ge(r_var, i + 1)
                nc.scalar.activation(rstd[:], TP[:], ACT.Sqrt, bias=epsc[:, 0:1]).then_inc(r_std, 1)
                act.wait_ge(r_g, i + 1)
                nc.scalar.activation(orh[:, ds(i, 1)].rearrange("p a t -> p (a t)"), rout[:], ACT.Copy).then_inc(r_hi, 1)
                among(2)
                if last_pair:
                    among(3)

            act.dma_start(cols[:], A["cols"]).then_inc(cols_in, 16)
            for g in range(ADA0):
                if g == ADA0 // 2:
                    act.dma_start(x[:], A["xt"]).then_inc(x_in, 16)
                    act.dma_start(ident[:], A["ident"]).then_inc(const_in, 16)
                    act.dma_start(wa2[:], A["w_a2"]).then_inc(const_in, 16)
                act.dma_start(ada0[:, g], A["ada"][g]).then_inc(ada0_in[g // 2], 16)
            ada_load(0)
            ada_load(1)
            act.wait_ge(cols_in, 16)
            nc.scalar.activation(silu_c[:].rearrange("p a k -> p (a k)"), cols[:, 0:2 * KT], ACT.Silu).then_inc(silu_c_done, 1)
            act.wait_ge(x_in, 16)
            act.wait_ge(const_in, 32)
            act.wait_ge(ready, 1)
            for n in range(KT):
                square(x[:, n], 0, n)
            high(0)
            high(1)
            for z in range(ADA0 // 2):
                if z == ADA0 // 2 - 1:
                    std(0)
                act.wait_ge(ada0_rows, z + 1)
                nc.scalar.activation(ada_row[:, z], (SC0, SC1, SC2, OV)[z][0:1, :], ACT.Copy).then_inc(ada0_row_out, 1)
            p = 0
            for kind, c, m, n in phases:
                if p:
                    std(PRE_GROUP[p])
                split_h(p, mod[:, PRE_MOD[p][0], 24 * PRE_MOD[p][1]:24 * PRE_MOD[p][1] + 8])
                {"ffn": ffn, "mix1": mix1, "mix2": mix2}[kind](c, m, n)
                p += 1
            if last:
                std(PRE_GROUP[p])
            for n in range(KT):
                act.wait_ge(out_ready, n + 1)
                act.dma_start(A["out"][:, n], nu[:, n % 2] if last else x[:, n]).then_inc(out_sent[n % 2], 16)
            for s in range(2):
                act.wait_ge(out_sent[s], 16 * KT // 2)

        @block.vector
        def _(dve):
            V = nc.vector
            chain = Chain(dve, dve_chain)

            def ada_sum(e, b, n=0, i=0):
                s = e % 2
                dve.wait_ge(ada_in[s], lin(16 * (e // 2 + 1), 8 * n, i))
                if e >= 2:
                    dve.wait_ge(ada_cols, lin(e - 1, n, i))
                chain.link(V.tensor_scalar(adac[:, s], adaw[:, s, 0], silu_c[:, b, 0:1], None, ALU.mult))
                for k in range(1, KT):
                    ins = V.scalar_tensor_tensor(adac[:, s], adaw[:, s, k], silu_c[:, b, k:k + 1], adac[:, s],
                                                 ALU.mult, ALU.add)
                    if k < KT - 1:
                        chain.link(ins)
                ins.then_inc(ada_acc, 1)

            def ada_add(e, n=0, i=0):
                dve.wait_ge(ada_cols, lin(e + 1, n, i))
                at = 2 * (e + ADA0)
                V.tensor_tensor(mod[:].rearrange("p b j -> p (b j)")[:, ds(lin(at, 2 * n, i), 2)], (TP, OV)[e % 2][:, 0:2],
                                cols[:, ds(lin(COLS["b_ada1"] + at, 2 * n, i), 2)], ALU.add).then_inc(ada_mod, 1)

            def add_squares(k, j, n=0, i=0):
                dve.wait_ge(sq_done, lin(8 * k + j + 1, n, i))
                dve.wait_ge(ssadd, lin(9 * k + j + 1, n, i))
                V.tensor_tensor(ssacc[:], ssacc[:], sq[:, j % 2], ALU.add).then_inc(ssadd, 1)

            def clear_squares(k):
                if k:
                    dve.wait_ge(ss_sum, k)
                V.memset(ssacc[:], 0.0).then_inc(ssadd, 1)

            def reciprocal_std(k):
                dve.wait_ge(std_done, k + 1)
                V.reciprocal(rcol[:], rcol[:]).then_inc(rcol_done, 1)

            def rstd_spread(k):
                dve.wait_ge(rstd_done, k + 1)

            def norm_h(p):
                b, v = PRE_MOD[p]
                gain = cols[:, PRE_GAIN[p]:PRE_GAIN[p] + KT]
                chain.link(V.scalar_tensor_tensor(pre_a[:], mod[:, b, 24 * v + 8:24 * v + 16], 1.0, gain, ALU.add, ALU.mult))
                if p:
                    reciprocal_std(PRE_GROUP[p])
                rstd_spread(PRE_GROUP[p])

                def u(n):
                    V.tensor_tensor(nu[:, n % 3], x[:, n], RSTD[:], ALU.mult).then_inc(u_done, 1)
                u(0)
                u(1)
                for n in range(KT):
                    if n + 2 < KT:
                        u(n + 2)
                    dve.wait_ge(v_done, 8 * p + n + 1)
                    dve.wait_ge(hh_done, 8 * p + n + 1)
                    V.tensor_tensor(hl[:, n], nv[:, n % 2], hh[:, n], ALU.subtract).then_inc(h_done, 1)

            def set_post(b, v, half, gain):
                gate = mod[:, b, 24 * v + 16:24 * v + 24]
                if gain is not None:
                    chain.link(V.scalar_tensor_tensor(post_g[:], gate, half, cols[:, gain:gain + KT], ALU.mult, ALU.mult))
                else:
                    chain.link(V.tensor_scalar(post_g[:], gate, half, None, ALU.mult))

            def out_tiles(c, m, per, block1, k):
                clear_squares(k)
                with dve.Fori(0, KT // 2) as i:
                    for u in range(2):
                        t = m + u
                        if not block1:
                            dve.wait_ge(slab_done, lin(c + (u + 1) * per, 2 * per, i))
                            j = ds(2 * i + u, 1)
                            xj = x[:, j].rearrange("p a t -> p (a t)")
                            V.scalar_tensor_tensor(xj, acc[t % 2][:], post_g[:, j], xj, ALU.mult, ALU.add)\
                                .then_inc(acc_free[t % 2], 1)
                        add_squares(k, u, 2, i)

            def residual(block1, k):
                if not block1:
                    return
                reciprocal_std(k)
                clear_squares(k + 1)
                rstd_spread(k)
                base = KT * [1, 3, 5].index(k)

                def scaled(n):
                    if n >= 3:
                        dve.wait_ge(x_done, base + n - 2)
                    V.scalar_tensor_tensor(nu[:, n % 3], y[:, n], post_g[:, n:n + 1], RSTD[:], ALU.mult, ALU.mult)\
                        .then_inc(y_done, 1)
                scaled(0)
                for n in range(KT):
                    if n + 1 < KT:
                        scaled(n + 1)
                    dve.wait_ge(y_done, base + n + 1)
                    V.tensor_tensor(x[:, n], x[:, n], nu[:, n % 3], ALU.add).then_inc(x_done, 1)
                for j in range(KT - 2, KT):
                    add_squares(k + 1, j)

            def ffn(c, m, f):
                def unit(c, m, i, j, b, pieces):
                    for e, n in pieces:
                        ada_sum(e, b, n, i)
                    dve.wait_ge(slab_done, lin(c + 2, 4, i))
                    tile_evacuated(dve, m, 4, i)
                    dve.wait_ge(prodhi, FT * f + j)
                    dve.wait_ge(prodlo, FT * f + j)
                    V.tensor_tensor(prod[:], acc[(m + 1) % 2][:], sg[:], ALU.mult)\
                        .then_inc(acc_free[(m + 1) % 2], 1)
                    for e, n in pieces:
                        ada_add(e, n, i)
                    tile_evacuated(dve, m + 1, 4, i)
                    dve.wait_ge(prodhi, FT * f + j + 1)
                    V.tensor_tensor(act_l[:, ds(j, 1)].rearrange("p a t -> p (a t)"), prod[:],
                                    act_h[:, ds(j, 1)].rearrange("p a t -> p (a t)"), ALU.subtract).then_inc(prodlo, 1)
                for first, runs, e, per, load in ADA_RUNS[f]:
                    with dve.Fori(first, first + runs) as i:
                        b = 0 if e is not None and e + ADA0 < 36 else 1
                        chain.enter(i - first, 2 * per * (KT - 1))
                        for u in range(2):
                            unit(c + 2 * u, m + 2 * u, i, 2 * i + u, b, ada_pieces(first, e, per, u))
                    chain.leave(runs)
                b, v = ((0, 0), (0, 2), (1, 0), (1, 2))[f]
                set_post(b, v, 0.5, COLS["g_post"] + 8 * v if b == 0 else None)
                k = group_of("ffn", f)
                out_tiles(c + 2 * FT, m + 2 * FT, 3, f < 2, k)
                residual(f < 2, k)

            def holds_waits(n):
                V.memset(tick[:, n % 8:n % 8 + 1], 0.0)

            def mix1(c, m, _):
                dve.wait_ge(m1_in, 32)
                dve.wait_ge(la_l, 1)
                chain.link(V.scalar_tensor_tensor(nar2[32:48, :], nar2[32:48, :], 0.0, nar[32:48, :], ALU.min, ALU.subtract))
                chain.link(V.memset(fneg16[32:48, :], 1.0))
                chain.link(V.tensor_tensor_scan(nar[32:48, :], fneg16[32:48, :], nar2[32:48, :], 0.0, ALU.mult, ALU.subtract))
                V.tensor_copy(fneg16[32:48, :], nar[32:48, :]).then_inc(la_done, 1)
                dve.wait_ge(la_l, 2)
                chain.link(V.scalar_tensor_tensor(lt4[:], lev[:, 0:HG], 0.0, lt4[:], ALU.min, ALU.subtract))
                chain.link(V.tensor_scalar(lt4[:], lt4[:], 1.0 / 16.0, None, ALU.mult))
                for h in range(HG):
                    ins = V.tensor_tensor_scan(lac[:, h], segm[:], lt4[:, h], 0.0, ALU.mult, ALU.add)
                chain.link(ins)
                c, m = c + 1, m + 1
                gla_distances(0)
                with dve.Fori(0, HG - 1) as i:
                    chain.enter(i, 4)
                    gla_head(c, m, i, True)
                chain.leave(HG - 1)
                gla_head(c, m, HG - 1, False)
                c, m = c + 6 * HG, m + 6 * HG
                with dve.Fori(0, FP // 2) as i:
                    chain.enter(i, 16)
                    for u in range(2):
                        fox_pair(2 * i + u, u)
                chain.leave(FP // 2)
                c, m = c + 4 * FP, m + 4 * FP
                set_post(0, 1, 1.0, COLS["g_post"] + 8)
                with dve.Fori(0, KT) as i:
                    dve.wait_ge(slab_done, c + 2 + 2 * i)
                    tile_evacuated(dve, m, 2, i)
                    V.tensor_tensor(mg[:, ds(i, 1)].rearrange("p a t -> p (a t)"), acc[(m + 1) % 2][:], sga1[:], ALU.mult)\
                        .then_inc(acc_free[(m + 1) % 2], 1)
                c, m = c + 2 * KT, m + 2 * KT
                with dve.Fori(0, KT // 2) as i:
                    for u in range(2):
                        j = ds(2 * i + u, 1)
                        flat = lambda b: b[:, j].rearrange("p a t -> p (a t)")
                        dve.wait_ge(slab_done, c + u + 1 + 2 * i)
                        dve.wait_ge(p_lo, 2 * i + u)
                        V.tensor_tensor(mt[:, u], acc[(m + u) % 2][:], flat(sgb), ALU.mult).then_inc(acc_free[(m + u) % 2], 1)
                        tile_evacuated(dve, m + u, 2, i)
                        V.tensor_tensor(mt[:, u], mt[:, u], flat(mg), ALU.add).then_inc(p_sum, 1)
                        dve.wait_ge(p_sum, 2 * i + u + 1)
                        dve.wait_ge(p_hi, 2 * i + u + 1)
                        V.tensor_tensor(flat(oal), mt[:, u], flat(oah), ALU.subtract).then_inc(p_lo, 1)
                c, m = c + KT, m + KT
                k = group_of("mix1", 0)
                out_tiles(c, m, 1, True, k)
                residual(True, k)

            def gla_distances(i):
                dve.wait_ge(g_cross_exp, i)
                chain.link(V.tensor_copy(cs[:], lac[:, ds(i, 1)].rearrange("p a t -> p (a t)")))
                dve.wait_ge(g_scores, 8 * i)
                for l, b in enumerate(LEVELS):
                    cv = cs[:].rearrange("p (n b) -> p n b", b=b)
                    lv = lev[:, l].rearrange("p (n b) -> p n b", b=b)
                    ref = cv[:, :, b // 2 - 1:b // 2].to_broadcast([P, T // b, b // 2])
                    V.tensor_tensor(lv[:, :, b // 2:], cv[:, :, b // 2:], ref, ALU.subtract)
                    ins = V.tensor_tensor(lv[:, :, :b // 2], ref, cv[:, :, :b // 2], ALU.subtract)
                ins.then_inc(g_lev_diff, 1)

            def gla_head(c, m, i, ahead):
                V.tensor_copy(gsel[:], cols[:, ds(COLS["g_gla"] + 2 * i, 2)])
                dve.wait_ge(g_o, 2 * i)
                chain.link(V.memset(adiag[:], 0.0))
                dve.wait_ge(g_lev_exp, i + 1)
                tile_evacuated(dve, m, 6, i)
                tile_evacuated(dve, m + 1, 6, i)
                for l, b in enumerate(LEVELS):
                    lv = lev[:, l].rearrange("p (n b) -> p n b", b=b)
                    qv, kv = (z[:].rearrange("p (n b) -> p n b", b=b) for z in (gq, gk))
                    V.tensor_tensor(lv[:, :, b // 2:], lv[:, :, b // 2:], qv[:, :, b // 2:], ALU.mult)
                    ins = V.tensor_tensor(lv[:, :, :b // 2], lv[:, :, :b // 2], kv[:, :, :b // 2], ALU.mult)
                ins.then_inc(g_lev_ready, 1)
                dve.wait_ge(g_cross_exp, i + 1)
                V.tensor_tensor(qp[:], gq[:], eq[:], ALU.mult)
                chain.link(V.tensor_tensor(kp[:], gk[:], ek[:], ALU.mult))
                V.tensor_scalar(k0[:], kp[:, 0:P], eq[:, 2 * P - 1:2 * P], None, ALU.mult)
                V.tensor_copy(qc[:, 0:P], qp[:, 2 * P:3 * P])
                V.tensor_scalar(qc[:, P:2 * P], qp[:, 3 * P:4 * P], eq[:, 3 * P - 1:3 * P], None, ALU.mult).then_inc(g_cross_ready, 1)
                for e in range(2):
                    dve.wait_ge(g_vT, 2 * i + e + 1)
                    V.tensor_copy(vtok[:, :, P * e:P * (e + 1)], (TP, OV)[e][:].rearrange("p (k q) -> p k q", q=P)).then_inc(g_vtok, 1)
                for l in range(len(LEVELS) + 1):
                    dve.wait_ge(g_scores, 8 * i + l + 1)
                    dve.wait_ge(g_picked, 8 * i + l)
                    holds_waits(l)
                    V.copy_predicated(adiag[:], lmask[:, l:l + 1].to_broadcast([P, TT, P]),
                                      SC[l % 2][:].rearrange("p (k q) -> p k q", q=P)).then_inc(g_picked, 1)
                if ahead:
                    gla_distances(i + 1)
                dve.wait_ge(g_osq, 2 * i + 2)
                dve.wait_ge(g_osum, i)
                V.tensor_tensor(osum[:], osq[:, 0], osq[:, 1], ALU.add).then_inc(g_osum, 1)
                dve.wait_ge(g_std, i + 1)
                chain.link(V.reciprocal(rstd[:], rstd[:]))
                dve.wait_ge(g_lo, 2 * i)
                for e in range(2):
                    ins = V.scalar_tensor_tensor(og[:, e], (OV, TP)[e][:], gsel[:, e:e + 1], rstd[:], ALU.mult, ALU.mult)
                    ins.then_inc(g_read, 1)
                dve.wait_ge(g_read, 2 * i + 2)
                tile_evacuated(dve, m + 4, 6, i)
                tile_evacuated(dve, m + 5, 6, i)
                for e in range(2):
                    V.tensor_tensor(og[:, e], og[:, e], sr[:, e], ALU.mult).then_inc(g_gated, 1)
                dve.wait_ge(g_gated, 2 * i + 2)
                for e in range(2):
                    dve.wait_ge(g_hi, 2 * i + e + 1)
                    j = ds(2 * i + e, 1)
                    V.tensor_tensor(oal[:, j].rearrange("p a t -> p (a t)"), og[:, e],
                                    oah[:, j].rearrange("p a t -> p (a t)"), ALU.subtract).then_inc(g_lo, 1)

            def fox_pair(i, u):
                dve.wait_ge(fneg_in, 16 * i + 16)
                for n in range(8 + 1):
                    if n < 8:
                        w = P * (n % 4 + 1)
                        dve.wait_ge(f_s, 8 * i + n + 1)
                        if n >= 4:
                            dve.wait_ge(f_t, 8 * i + n - 3)
                        holds_waits(n)
                        V.tensor_tensor_reduce(out=pb[:, n % 4, 0:w], in0=SC[n % 2][:, 0:w], in1=fneg[u][:, n // 4, 0:w],
                                               scale=-1.0, scalar=3e38, op0=ALU.add, op1=ALU.min,
                                               accum_out=nm[:, n:n + 1]).then_inc(f_sm, 1)
                    if n == 2:
                        dve.wait_ge(f_vT, i + 1)
                        V.tensor_copy(fvtok[:], SC2[:].rearrange("p (k q) -> p k q", q=P)).then_inc(f_vtok, 1)
                    if n >= 1:
                        j = n - 1
                        w = P * (j % 4 + 1)
                        dve.wait_ge(f_e, 8 * i + j + 1)
                        chain.link(V.reciprocal(ri[:, j:j + 1], rs[:, j:j + 1]))
                        V.tensor_scalar(pb[:, j % 4, 0:w], pb[:, j % 4, 0:w], ri[:, j:j + 1], None, ALU.mult).then_inc(f_p, 1)
                dve.wait_ge(f_hi, i + 1)
                j = ds(i, 1)
                V.tensor_tensor(obl[:, j].rearrange("p a t -> p (a t)"), OV[:], obh[:, j].rearrange("p a t -> p (a t)"),
                                ALU.subtract).then_inc(f_lo, 1)

            def mix2(c, m, _):
                dve.wait_ge(m2_in, 96)
                for kv in range(2):
                    tile_evacuated(dve, m + kv)
                    dve.wait_ge(n_swap, kv + 1)
                    for g in range(2):
                        for half in range(2):
                            h = slice(64 * half, 64 * (half + 1))
                            src = craw[h, kv] if g == half else (OV, ST)[kv][h, :]
                            V.tensor_tensor(cab[h, kv, g, 0:16 * NC].rearrange("p (n l) -> p n l", l=16),
                                            src[:, 16 * half:16 * (NC + half)].rearrange("p (n l) -> p n l", l=16),
                                            cpe[h, kv:kv + 1, 16 * half:16 * half + 16].to_broadcast([64, NC, 16]), ALU.add)\
                                .then_inc(n_pe, 1)
                for z, dst in enumerate((vstok, vwtok)):
                    dve.wait_ge(n_vT, z + 1)
                    V.tensor_copy(dst[:], SC[z][:].rearrange("p (k q) -> p k q", q=P)).then_inc(n_vtok, 1)
                dve.wait_ge(n_vT, 3)
                V.tensor_copy(gtok[:], SC2[:, 0:24 * TT].rearrange("p (t j) -> p t j", j=24)).then_inc(n_vtok, 1)
                dve.wait_ge(n_vtok, 3)
                c, m = c + 7, m + 7
                with dve.Fori(0, NP) as i:
                    chain.enter(i, NSA_LINKS)
                    nsa_pair(c, m, i)
                chain.leave(NP)
                c, m = c + 4 * NP, m + 4 * NP
                dve.wait_ge(r_in, 64)
                with dve.Fori(0, NP) as i:
                    chain.enter(i, RET_LINKS)
                    ret_pair(c, m, i)
                chain.leave(NP)
                c, m = c + 4 * NP, m + 4 * NP
                set_post(1, 1, 1.0, None)
                c, m = c + 4, m + 4
                with dve.Fori(0, KT // 2) as i:
                    for u in range(2):
                        j = ds(2 * i + u, 1)
                        flat = lambda b: b[:, j].rearrange("p a t -> p (a t)")
                        dve.wait_ge(q_lo, 2 * i + u)
                        for z, gate in enumerate((sga2, sgb2)):
                            if z:
                                dve.wait_ge(slab_done, c + u + 1 + 2 * i)
                            else:
                                dve.wait_ge(q_half, 2 * i + u + 1)
                            t = m + 2 * u + z
                            V.tensor_tensor(mt2[:, u + 2 * z], acc[t % 2][:], flat(gate), ALU.mult).then_inc(acc_free[t % 2], 1)
                        tile_evacuated(dve, m + 2 * u, 4, i)
                        tile_evacuated(dve, m + 2 * u + 1, 4, i)
                        V.tensor_tensor(mt2[:, u], mt2[:, u], mt2[:, u + 2], ALU.add).then_inc(q_sum, 1)
                        dve.wait_ge(q_sum, 2 * i + u + 1)
                        dve.wait_ge(q_hi, 2 * i + u + 1)
                        V.tensor_tensor(flat(ml2), mt2[:, u], flat(mh2), ALU.subtract).then_inc(q_lo, 1)
                c, m = c + KT, m + 2 * KT
                out_tiles(c, m, 1, False, group_of("mix2", 0))

            def nsa_pair(c, m, i):
                dve.wait_ge(n_p, 16 * i)
                for a in range(2):
                    V.tensor_copy(gcur[:, a], gtok[:, :, ds(3 * i + 12 * a, 3)].rearrange("p t b -> p b t"))

                def cmp_shift(a):
                    dve.wait_ge(n_cs, 2 * i + a + 1)
                    dve.wait_ge(n_ct, 2 * i + a)
                    chain.link(V.tensor_tensor(cb[:], SC2[:, 0:32 * TT].rearrange("p (t j) -> p t j", j=32)[:, :, 0:NC], cmask[:], ALU.add))
                    chain.link(V.tensor_reduce(cm[:], cb[:], AX.X, ALU.max))
                    V.tensor_tensor(cb[:], cb[:], cm[:].rearrange("p (t o) -> p t o", o=1).to_broadcast([P, TT, NC]), ALU.subtract)\
                        .then_inc(n_cd, 1)

                def cmp_scale(a):
                    dve.wait_ge(n_ce, 2 * i + a + 1)
                    chain.link(V.tensor_reduce(csum[:], cb[:], AX.X, ALU.add))
                    chain.link(V.reciprocal(csum[:], csum[:]))
                    chain.link(V.tensor_tensor(csum[:], csum[:], gcur[:, a, 0], ALU.mult))
                    chain.link(V.tensor_tensor(csum[:], csum[:], cvalid[:], ALU.mult))
                    V.tensor_tensor(cb[:], cb[:], csum[:].rearrange("p (t o) -> p t o", o=1).to_broadcast([P, TT, NC]), ALU.mult)\
                        .then_inc(n_cp, 1)
                cmp_shift(0)
                for n in range(16 + 1):
                    if n < 16:
                        w = P * (n % 4 + 1)
                        dve.wait_ge(n_s, 16 * i + n + 1)
                        if n >= 4:
                            dve.wait_ge(n_t, 16 * i + n - 3)
                        holds_waits(n)
                        V.tensor_tensor_reduce(out=npb[:, n % 4, 0:w], in0=SC[n % 2][:, 0:w], in1=causal[:, T - w:T],
                                               scale=-1.0, scalar=3e38, op0=ALU.add, op1=ALU.min,
                                               accum_out=nnm[:, n:n + 1]).then_inc(n_sm, 1)
                    if n >= 1:
                        j = n - 1
                        w = P * (j % 4 + 1)
                        dve.wait_ge(n_e, 16 * i + j + 1)
                        chain.link(V.reciprocal(nri[:, j:j + 1], nrs[:, j:j + 1]))
                        V.tensor_scalar(npb[:, j % 4, 0:w], npb[:, j % 4, 0:w], nri[:, j:j + 1],
                                        gcur[:, j // 8, 1 + (j // 4) % 2, j % 4:j % 4 + 1], ALU.mult, ALU.mult).then_inc(n_p, 1)
                    if n == 1:
                        cmp_scale(0)
                    if n == 6:
                        cmp_shift(1)
                    if n == 8:
                        cmp_scale(1)
                dve.wait_ge(n_hi, i + 1)
                j = ds(i, 1)
                V.tensor_tensor(onl[:, j].rearrange("p a t -> p (a t)"), OV[:], onh[:, j].rearrange("p a t -> p (a t)"),
                                ALU.subtract).then_inc(n_lo, 1)

            def ret_pair(c, m, i):
                V.tensor_copy(rw[:], cols[:, ds(i + COLS["ret_norm"], 1)])
                for z in range(2):
                    dve.wait_ge(r_rot, 2 * i + z + 1)
                    V.tensor_tensor(rtmp[:, z], SC[z][:], rsin[:], ALU.mult)
                    chain.link(V.tensor_tensor(rqk[:, z], rqr[:, z], rcos[:], ALU.mult))
                    V.tensor_tensor(rqk[:, z], rqk[:, z], rtmp[:, z], ALU.add).then_inc(r_qk, 1)
                dve.wait_ge(r_vT, i + 1)
                V.tensor_copy(rvtok[:], SC2[:].rearrange("p (k q) -> p k q", q=P)).then_inc(r_vtok, 1)
                dve.wait_ge(r_dec, 16 * i + 16)
                for n in range(8):
                    w = T - P * (n % 4)
                    dve.wait_ge(r_s, 8 * i + n + 1)
                    if n >= 4:
                        dve.wait_ge(r_pv, 8 * i + n - 3)
                    V.tensor_tensor(rad[:, n % 4, 0:w], SC[n % 2][:, 0:w], rdec[:, n // 4, 0:w], ALU.mult).then_inc(r_ad, 1)
                dve.wait_ge(r_mean, i + 1)
                V.tensor_tensor(rcen[:], ro[:], SC2[:], ALU.subtract).then_inc(r_cen, 1)
                dve.wait_ge(r_std, i + 1)
                chain.link(V.reciprocal(rstd[:], rstd[:]))
                chain.link(V.scalar_tensor_tensor(rout[:], rcen[:], rw[:, 0:1], rstd[:], ALU.mult, ALU.mult))
                tile_evacuated(dve, m + 3, 4, i)
                V.tensor_tensor(rout[:], rout[:], rsg[:], ALU.mult).then_inc(r_g, 1)
                dve.wait_ge(r_g, i + 1)
                dve.wait_ge(r_hi, i + 1)
                j = ds(i, 1)
                V.tensor_tensor(orl[:, j].rearrange("p a t -> p (a t)"), rout[:], orh[:, j].rearrange("p a t -> p (a t)"),
                                ALU.subtract).then_inc(r_lo, 1)

            V.memset(ones[:], 1.0)
            V.memset(epsc[:], EPS).then_inc(ready, 1)
            clear_squares(0)
            dve.wait_ge(silu_c_done, 1)
            for j in range(KT):
                add_squares(0, j)
            reciprocal_std(0)
            dve.wait_ge(ada0_cols, 1)
            chain.link(V.tensor_tensor(mod[:, 0, 0:2 * ADA0], TP[:, 0:2 * ADA0],
                                       cols[:, COLS["b_ada1"]:COLS["b_ada1"] + 2 * ADA0], ALU.add))
            p = 0
            for kind, c, m, n in phases:
                norm_h(p)
                {"ffn": ffn, "mix1": mix1, "mix2": mix2}[kind](c, m, n)
                p += 1
            if last:
                reciprocal_std(PRE_GROUP[p])
                rstd_spread(PRE_GROUP[p])
            for n in range(KT):
                if last:
                    if n >= 2:
                        dve.wait_ge(out_sent[n % 2], 16 * (n // 2))
                    V.scalar_tensor_tensor(nu[:, n % 2], x[:, n], cols[:, COLS["final"] + n:COLS["final"] + n + 1], RSTD[:],
                                           ALU.mult, ALU.mult).then_inc(out_ready, 1)
                else:
                    V.memset(epsc[:], EPS).then_inc(out_ready, 1)
                    dve.wait_ge(out_ready, n + 1)

        @block.tensor
        def _(pe):
            MM = nc.tensor.matmul

            def bank_free(m, n=0, i=0):
                if m >= 2:
                    pe.wait_ge(acc_free[m % 2], lin(m // 2, n // 2, i))

            def slab(c, out, xh, xl, n=0, i=0, tiles=range(KT), first=True, end=True, signal=slab_done, wait=True,
                     fresh=None):
                if wait:
                    pe.wait_ge(lo_done, lin(c + 1, n, i))
                s = c % 2
                for j, k in enumerate(tiles):
                    a, b = xh(k), xl(k)
                    if fresh:
                        pe.wait_ge(fresh[0], fresh[1] + k + 1)
                    MM(out, wh[s][:, k], a, start=first and j == 0, stop=False)
                    MM(out, wh[s][:, k], b, start=False, stop=False)
                    ins = MM(out, wl[s][:, k], a, start=False, stop=end and j == len(tiles) - 1)
                if signal:
                    ins.then_inc(signal, 1)

            def of(h, l, at=0):
                return (lambda k: h[:, k + at]), (lambda k: l[:, k + at])

            def sum_squares(k):
                pe.wait_ge(ssadd, 9 * (k + 1))
                for t in range(TT):
                    ins = MM(ST[:, t:t + 1], ssacc[:, P * t:P * (t + 1)], ones[:, 0:1], start=True, stop=True)
                ins.then_inc(ss_sum, 1)

            def spread(k):
                pe.wait_ge(rcol_done, k + 1)
                for t in range(TT):
                    ins = MM(RSTD[:, P * t:P * (t + 1)], rcol[:, t:t + 1].to_broadcast([P, P]), ident[:], start=True, stop=True)
                ins.then_inc(rstd_done, 1)

            def ada_rows(z):
                pe.wait_ge(ada0_in[z], 32)
                for g in range(2):
                    for k in range(KT):
                        ins = MM((SC0, SC1, SC2, OV)[z][0:1, 256 * g:256 * (g + 1)], silu_c[:, 0, k:k + 1], ada0[:, 2 * z + g, k],
                                 start=k == 0, stop=k == KT - 1)
                ins.then_inc(ada0_rows, 1)

            def ada_columns(e, n=0, i=0):
                s = e % 2
                pe.wait_ge(ada_acc, lin(e + 1, n, i))
                if e >= 2:
                    pe.wait_ge(ada_mod, lin(e - 1, n, i))
                b = (TP, OV)[s]
                MM(b[:, 0:1], adac[:, s, 0:P], ones[:, 0:1], start=True, stop=True)
                MM(b[:, 1:2], adac[:, s, P:2 * P], ones[:, 0:1], start=True, stop=True).then_inc(ada_cols, 1)

            def out_tiles(c, m, per, xh, xl, k, fresh):
                with pe.Fori(0, KT // 2) as i:
                    for u in range(2):
                        bank_free(m + u, 2, i)
                        for s in range(per):
                            tiles = range(min(KT, FT - KT * s)) if per > 1 else range(KT)
                            a, b = of(xh, xl, KT * s)
                            slab(c + u * per + s, acc[(m + u) % 2][:], a, b, 2 * per, i, tiles, s == 0, s == per - 1,
                                 fresh=(fresh[0], fresh[1] + KT * s) if u == 0 else None)
                sum_squares(k)
                spread(k)
                if k in (1, 3, 5):
                    sum_squares(k + 1)
                    spread(k + 1)

            def ffn(c, m, f):
                for first, runs, e, per, _ in ADA_RUNS[f]:
                    with pe.Fori(first, first + runs) as i:
                        for u in range(2):
                            for z in range(2 * u, 2 * u + 2):
                                pe.wait_ge(acc_free[(m + z) % 2], (m + z) // 2 + 2 * i)
                                slab(c + z, acc[(m + z) % 2][:], *of(hh, hl), 4, i,
                                     fresh=(h_done, KT * (0, 2, 3, 5)[f]) if z == 0 and first == 0 else None)
                            for piece, n in ada_pieces(first, e, per, u):
                                ada_columns(piece, n, i)
                out_tiles(c + 2 * FT, m + 2 * FT, 3, act_h, act_l, group_of("ffn", f), (prodlo, FT * f))

            def mix1(c, m, _):
                bank_free(m)
                slab(c, acc[m % 2][:], *of(hh, hl), fresh=(h_done, KT))
                tile_evacuated(pe, m)
                for h in range(HG):
                    MM((SC0, SC1, SC2, TP)[h][:], wa2[0:16, P * h:P * (h + 1)], nar[0:16, :], start=True, stop=True)\
                        .then_inc(la_ready, 1)
                c, m = c + 1, m + 1
                for u in range(2):
                    bank_free(m + u)
                    slab(c + u, acc[(m + u) % 2][:], *of(hh, hl))
                pe.wait_ge(la_x, HG)
                with pe.Fori(0, HG - 1) as i:
                    gla_head(c, m, i, 2)
                gla_head(c, m, HG - 1, 0)
                c, m = c + 6 * HG, m + 6 * HG
                for u in range(3):
                    bank_free(m + u)
                    slab(c + u, acc[(m + u) % 2][:], *of(hh, hl))
                with pe.Fori(0, FP // 2 - 1) as i:
                    for u in range(2):
                        fox_pair(c, m, 2 * i + u, u, 4)
                fox_pair(c, m, FP - 2, 0, 4)
                fox_pair(c, m, FP - 1, 1, 1)
                c, m = c + 4 * FP, m + 4 * FP
                with pe.Fori(0, KT) as i:
                    bank_free(m, 2, i)
                    slab(c, acc[m % 2][:], *of(hh, hl), 2, i)
                    bank_free(m + 1, 2, i)
                    slab(c + 1, acc[(m + 1) % 2][:], *of(oah, oal), 2, i)
                c, m = c + 2 * KT, m + 2 * KT
                with pe.Fori(0, KT // 2) as i:
                    for u in range(2):
                        bank_free(m + u, 2, i)
                        slab(c + u, acc[(m + u) % 2][:], *of(obh, obl), 2, i, fresh=None if u else (f_lo, 0))
                c, m = c + KT, m + KT
                out_tiles(c, m, 1, oah, oal, group_of("mix1", 0), (p_lo, 0))

            def gla_head(c, m, i, ahead):
                def project(u):
                    bank_free(m + u, 6, i)
                    slab(c + u, acc[(m + u) % 2][:], *of(hh, hl), 6, i)
                project(2)
                project(3)
                project(4)
                pe.wait_ge(g_read, 2 * i)
                for e in range(2):
                    tile_evacuated(pe, m + 2 + e, 6, i)
                    for t in range(TT):
                        ins = nc.tensor.transpose((TP, OV)[e][:, P * t:P * (t + 1)], vt[:, e, P * t:P * (t + 1)], ident[:])
                    ins.then_inc(g_vT, 1)
                filler = interleaved(c + 5, m + 5, 1, 6, i)
                pe.wait_ge(g_lev_ready, i + 1)
                pe.wait_ge(g_std, i)
                for l in range(len(LEVELS) + 1):
                    next(filler)
                    if l >= 2:
                        pe.wait_ge(g_picked, 8 * i + l - 1)
                    for t in range(TT):
                        s = slice(P * t, P * (t + 1))
                        a, b = (lev[:, l, s], lev[:, l, s]) if l < len(LEVELS) else (gk[:, s], gq[:, s])
                        ins = MM(SC[l % 2][:, s], a, b, start=True, stop=True)
                    ins.then_inc(g_scores, 1)
                    if l == 3:
                        pe.wait_ge(g_cross_ready, i + 1)
                        pe.wait_ge(g_cross_out, 2 * i)
                        MM(SC2[:, 0:P], kp[:, 0:P], qp[:, P:2 * P], start=True, stop=True)
                        MM(SC2[:, P:3 * P], k0[:], qc[:], start=True, stop=True)
                        MM(SC2[:, 3 * P:4 * P], kp[:, 2 * P:3 * P], qp[:, 3 * P:4 * P], start=True, stop=True).then_inc(g_cross, 1)
                        MM(ST[:, 0:2 * P], kp[:, P:2 * P], qc[:], start=True, stop=True).then_inc(g_cross, 1)
                filler = interleaved(c + 6, m + 6, ahead, 6, i)
                for _ in range(3):
                    next(filler, None)
                pe.wait_ge(g_vtok, 2 * i + 2)
                pe.wait_ge(g_picked, 8 * i + 8)
                pe.wait_ge(g_cross_out, 2 * i + 2)
                for e in range(2):
                    out = (OV, TP)[e]

                    def v(s):
                        return vtok[:, s, P * e:P * (e + 1)]
                    MM(out[:, 0:P], v(0), adiag[:, 0], start=True, stop=False, skip_group_check=True)
                    MM(out[:, P:4 * P], v(0), ac0[:, 0:3 * P], start=False, stop=False, skip_group_check=True)
                    MM(out[:, P:2 * P], v(1), adiag[:, 1], start=False, stop=False, skip_group_check=True)
                    MM(out[:, 2 * P:4 * P], v(1), ac1[:], start=False, stop=False, skip_group_check=True)
                    MM(out[:, 2 * P:3 * P], v(2), adiag[:, 2], start=False, stop=False, skip_group_check=True)
                    MM(out[:, 3 * P:4 * P], v(2), ac0[:, 3 * P:4 * P], start=False, stop=False, skip_group_check=True)
                    MM(out[:, 3 * P:4 * P], v(3), adiag[:, 3], start=False, stop=True, skip_group_check=True).then_inc(g_o, 1)
                for _ in range(10):
                    next(filler, None)
                pe.wait_ge(g_osum, i + 1)
                MM(SC0[:], ones[:], osum[:], start=True, stop=True).then_inc(g_ss, 1)
                for _ in range(3):
                    next(filler, None)

            def interleaved(c, m, count, per, i):
                for u in range(count):
                    bank_free(m + u, per, i)
                    for k in range(KT):
                        slab(c + u, acc[(m + u) % 2][:], *of(hh, hl), per, i, [k], k == 0, k == KT - 1,
                             slab_done if k == KT - 1 else None, k == 0)
                        yield

            def fox_pair(c, m, i, u, slabs):
                filler = interleaved(c + 3, m + 3, slabs, 4, i)
                pe.wait_ge(m1_in, 64)
                for n in range(8 + 2 + 2):
                    for _ in range(3):
                        next(filler, None)
                    if n == 1:
                        tile_evacuated(pe, m + 2, 4, i)
                        for t in range(TT):
                            ins = nc.tensor.transpose(SC2[:, P * t:P * (t + 1)], fv[:, P * t:P * (t + 1)], ident[:])
                        ins.then_inc(f_vT, 1)
                    if n < 8:
                        a, t = n // 4, n % 4
                        w = P * (t + 1)
                        h = slice(64 * a, 64 * (a + 1))
                        if n >= 2:
                            pe.wait_ge(f_sm, 8 * i + n - 1)
                        MM(SC[n % 2][:, 0:w], fq[h, u, P * t:w], fk[h, u, 0:w], start=True, stop=False)
                        MM(SC[n % 2][:, P * t:w], identb[:], trib[:], start=False, stop=True).then_inc(f_s, 1)
                    if 2 <= n < 10:
                        j = n - 2
                        t = j % 4
                        pe.wait_ge(f_p, 8 * i + j + 1)
                        if j >= 2:
                            pe.wait_ge(f_te, 8 * i + j - 1)
                        for k in range(t + 1):
                            ins = nc.tensor.transpose(TB[j % 2][:, P * k:P * (k + 1)], pb[:, j % 4, P * k:P * (k + 1)], ident[:])
                        ins.then_inc(f_t, 1)
                    if n in (7, 11):
                        a = (n - 7) // 4
                        pe.wait_ge(f_te, 8 * i + 4 * a + 4)
                        if a == 0:
                            pe.wait_ge(f_vtok, i + 1)
                            pe.wait_ge(f_lo, i)
                        for k in range(TT):
                            ins = MM(OV[64 * a:64 * (a + 1), P * k:T], fvtok[:, k, 64 * a:64 * (a + 1)], pt[:, a, k, P * k:T],
                                     start=k == 0, stop=k == TT - 1, skip_group_check=True)
                        if a == 1:
                            ins.then_inc(f_o, 1)

            def mix2(c, m, _):
                for u in range(7):
                    if u == 4:
                        for kv in range(2):
                            tile_evacuated(pe, m + kv)
                            for g in range(2):
                                ins = MM((OV, ST)[kv][64 * g:64 * (g + 1), :], ident[:, 64 * (1 - g):64 * (2 - g)], craw[:, kv],
                                         start=True, stop=True)
                            ins.then_inc(n_swap, 1)
                    bank_free(m + u)
                    slab(c + u, acc[(m + u) % 2][:], *of(hh, hl), fresh=None if u else (h_done, 4 * KT))
                pe.wait_ge(m2_in, 96)
                for kv in range(2):
                    pe.wait_ge(n_pe, 4 * (kv + 1))
                    for g in range(2):
                        for l in range(16):
                            ins = MM((SC0, SC1, SC2, TP)[2 * kv + g][:, 0:NC], w1[:, kv, l],
                                     cab[:, kv, g, l:l + 16 * (NC - 1) + 1:16], start=l == 0, stop=l == 15)
                        ins.then_inc(n_hid, 1)
                pe.wait_ge(n_act, 4)
                for g in range(2):
                    ins = MM(ST[64 * g:64 * (g + 1), 0:NC], w2[:, 0], chid[:, 0, g], start=True, stop=True)
                ins.then_inc(n_cw, 1)
                for g in range(2):
                    ins = MM(OV[0:NC, 64 * g:64 * (g + 1)], chid[:, 1, g], w2[:, 1], start=True, stop=True)
                ins.then_inc(n_cw, 1)
                tile_evacuated(pe, m + 5)
                tile_evacuated(pe, m + 6)
                for z in range(2):
                    for t in range(TT):
                        ins = nc.tensor.transpose(SC[z][:, P * t:P * (t + 1)], vst[:, z, P * t:P * (t + 1)], ident[:])
                    ins.then_inc(n_vT, 1)
                for t in range(TT):
                    ins = nc.tensor.transpose(SC2[:, 24 * t:24 * (t + 1)], gt24[:, P * t:P * (t + 1)], ident[0:24, 0:24])
                ins.then_inc(n_vT, 1)
                c, m = c + 7, m + 7
                pe.wait_ge(n_vtok, 3)
                pe.wait_ge(n_kc, 2)
                bank_free(m)
                slab(c, acc[m % 2][:], *of(hh, hl))
                with pe.Fori(0, NP - 1) as i:
                    nsa_pair(c, m, i, 4)
                nsa_pair(c, m, NP - 1, 3)
                c, m = c + 4 * NP, m + 4 * NP
                for u in range(3):
                    bank_free(m + u)
                    slab(c + u, acc[(m + u) % 2][:], *of(hh, hl))
                pe.wait_ge(r_in, 64)
                with pe.Fori(0, NP - 1) as i:
                    ret_pair(c, m, i, 4)
                ret_pair(c, m, NP - 1, 5)
                c, m = c + 4 * NP + 4, m + 4 * NP + 4
                with pe.Fori(0, KT // 2) as i:
                    for u in range(2):
                        t = m + 2 * u
                        bank_free(t, 4, i)
                        slab(c + u, acc[t % 2][:], *of(onh, onl), 2, i, range(NP), signal=q_half)
                        bank_free(t + 1, 4, i)
                        slab(c + u, acc[(t + 1) % 2][:], *of(orh, orl, -NP), 2, i, range(NP, 2 * NP), wait=False,
                             fresh=(r_lo, -NP))
                c, m = c + KT, m + 2 * KT
                out_tiles(c, m, 1, mh2, ml2, group_of("mix2", 0), (q_lo, 0))

            def nsa_pair(c, m, i, slabs):
                filler = interleaved(c + 1, m + 1, slabs, 4, i)

                def half(a):
                    return slice(64 * a, 64 * (a + 1))

                def cmp_scores(a):
                    for t in range(TT):
                        ins = MM(SC2[:, 32 * t:32 * t + NC], nq[half(a), P * t:P * (t + 1)], kct[half(a), 0:NC], start=True, stop=True)
                    ins.then_inc(n_cs, 1)

                def cmp_transpose(a):
                    pe.wait_ge(n_cp, 2 * i + a + 1)
                    for t in range(TT):
                        ins = nc.tensor.transpose(SC2[0:NC, P * t:P * (t + 1)], cb[:, t], ident[:])
                    ins.then_inc(n_ct, 1)

                def cmp_values(a):
                    pe.wait_ge(n_cte, 2 * i + a + 1)
                    if a == 0:
                        pe.wait_ge(n_lo, i)
                    MM(OV[half(a), :], vctok[:, a], ct[:], start=True, stop=False, skip_group_check=True)
                for n in range(16 + 4):
                    for _ in range(2 if n < 12 else 1):
                        next(filler, None)
                    if n == 0:
                        tile_evacuated(pe, m, 4, i)
                        cmp_scores(0)
                    if n < 16:
                        a, t = n // 8, n % 4
                        w = P * (t + 1)
                        if n >= 2:
                            pe.wait_ge(n_sm, 16 * i + n - 1)
                        MM(SC[n % 2][:, 0:w], nq[half(a), P * t:w], (ks, kw)[(n // 4) % 2][half(a), 0:w], start=True, stop=True)\
                            .then_inc(n_s, 1)
                    if 2 <= n < 18:
                        j = n - 2
                        t = j % 4
                        pe.wait_ge(n_p, 16 * i + j + 1)
                        if j >= 2:
                            pe.wait_ge(n_te, 16 * i + j - 1)
                        for k in range(t + 1):
                            ins = nc.tensor.transpose(TB[j % 2][:, P * k:P * (k + 1)], npb[:, j % 4, P * k:P * (k + 1)], ident[:])
                        ins.then_inc(n_t, 1)
                    if n == 4:
                        cmp_transpose(0)
                    if n == 6:
                        cmp_values(0)
                        cmp_scores(1)
                    if n == 10:
                        cmp_transpose(1)
                    if n == 12:
                        cmp_values(1)
                    if n % 4 == 3 and n >= 7:
                        g = (n - 7) // 4
                        a, br = g // 2, g % 2
                        pe.wait_ge(n_te, 16 * i + 4 * g + 4)
                        for k in range(TT):
                            ins = MM(OV[half(a), P * k:T], (vstok, vwtok)[br][:, k, half(a)], npt[:, g % 2, k, P * k:T],
                                     start=False, stop=br == 1 and k == TT - 1, skip_group_check=True)
                        if g == 3:
                            ins.then_inc(n_o, 1)

            def ret_pair(c, m, i, slabs):
                filler = interleaved(c + 3, m + 3, slabs, 4, i)

                def fill(n):
                    for _ in range(n):
                        next(filler, None)
                for z in range(2):
                    tile_evacuated(pe, m + z, 4, i)
                    MM(SC[z][:], rrot[:], rqr[:, z], start=True, stop=True).then_inc(r_rot, 1)
                    fill(3)
                tile_evacuated(pe, m + 2, 4, i)
                pe.wait_ge(r_cen, i)
                for t in range(TT):
                    ins = nc.tensor.transpose(SC2[:, P * t:P * (t + 1)], rvt[:, P * t:P * (t + 1)], ident[:])
                ins.then_inc(r_vT, 1)
                fill(4)
                pe.wait_ge(r_qk, 2 * i + 2)
                pe.wait_ge(r_vtok, i + 1)
                pe.wait_ge(r_ro, i)
                for n in range(8 + 2):
                    if n >= 2:
                        fill(1)
                    if n < 8:
                        a, s = n // 4, n % 4
                        h = slice(64 * a, 64 * (a + 1))
                        if n >= 2:
                            pe.wait_ge(r_ad, 8 * i + n - 1)
                        MM(SC[n % 2][:, 0:T - P * s], rqk[h, 1, P * s:P * (s + 1)], rqk[h, 0, P * s:T], start=True, stop=True)\
                            .then_inc(r_s, 1)
                    if n >= 2:
                        j = n - 2
                        a, s = j // 4, j % 4
                        h = slice(64 * a, 64 * (a + 1))
                        pe.wait_ge(r_ad, 8 * i + j + 1)
                        MM(OV[h, P * s:T], rvtok[:, s, h], rad[:, j % 4, 0:T - P * s], start=s == 0, stop=s == TT - 1,
                           skip_group_check=True).then_inc(r_pv, 1)
                fill(3)
                pe.wait_ge(r_ro, i + 1)
                MM(SC2[:], rblk[:], ro[:], start=True, stop=True).then_inc(r_mean, 1)
                fill(4)
                pe.wait_ge(r_sq, i + 1)
                MM(TP[:], rblk[:], rsq[:], start=True, stop=True).then_inc(r_var, 1)
                fill(8 * slabs)

            pe.wait_ge(ready, 1)
            pe.wait_ge(silu_c_done, 1)
            ada_rows(0)
            ada_rows(1)
            ada_rows(2)
            sum_squares(0)
            ada_rows(3)
            for z in range(ADA0 // 2):
                pe.wait_ge(ada0_row_out, z + 1)
                for j in range(TT):
                    ins = MM(TP[:, TT * z + j:TT * z + j + 1], ada_row[:, z, P * j:P * (j + 1)], ones[0:1, 0:1],
                             start=True, stop=True)
            ins.then_inc(ada0_cols, 1)
            spread(0)
            for kind, c, m, n in phases:
                {"ffn": ffn, "mix1": mix1, "mix2": mix2}[kind](c, m, n)


ADA0 = 8
ADA_RUNS = {
    0: [(0, 1, 0, 2, True), (1, 9, 4, 1, True), (10, 1, 22, 1, False)],
    1: [(0, 2, 24, 1, True), (2, 8, 28, 1, True), (10, 1, 44, 1, False)],
    2: [(0, 8, 46, 1, True), (8, 1, 62, 1, False), (9, 2, None, 0, False)],
    3: [(0, 11, None, 0, False)],
}


def ada_pieces(first, e, per, u):
    return [(e + per * u + v - 2 * per * first, 2 * per) for v in range(per)]


PRE_GROUP = [0, 2, 4, 6, 7, 8, 9]
PRE_MOD = [(0, 0), (0, 1), (0, 2), (1, 0), (1, 1), (1, 2)]
PRE_GAIN = [COLS["g_pre"], COLS["g_pre"] + 8, COLS["g_pre"] + 16, COLS["norm1"], COLS["norm2"], COLS["norm3"]]


def _tiles(w):
    rows, n = w.shape
    k = -(-rows // D)
    padded = np.zeros((k * D, n), np.float32)
    padded[:rows] = w
    return padded.reshape(k, KT, P, n // P, P).transpose(3, 0, 2, 1, 4).reshape(-1, P, KT, P)


def _ffn_slabs(w_gu, w_dn):
    gu = _tiles(w_gu)
    both = np.stack([gu[:FT], gu[FT:]], 1).reshape(-1, P, KT, P)
    return [both, _tiles(w_dn)]


def _interleave(*lists):
    runs = len(lists[0][0]) // lists[0][1]
    return np.concatenate([s[i * k:(i + 1) * k] for i in range(runs) for s, k in lists])


def _mix1_slabs(w_in, w_pa, w_pb, w_out):
    w = _split_cols(w_in, (512, 512, 1024, 16, 1024, 1024, 1024, 1024, 16, 1024, 1024))
    q_a, k_a, v_a, a_low, r_a, q_b, k_b, v_b, f_b, gate_a, gate_b = w
    narrow = np.zeros((D, P), np.float32)
    narrow[:, 0:16] = a_low
    narrow[:, 32:48] = f_b
    t = _tiles
    return [t(narrow),
            _interleave((t(q_a), 1), (t(k_a), 1), (t(v_a), 2), (t(r_a), 2)),
            _interleave((t(q_b), 1), (t(k_b), 1), (t(v_b), 1), (t(gate_b), 1)),
            _interleave((t(gate_a), 1), (t(w_pa), 1)),
            t(w_pb), t(w_out)]


def _split_cols(w, widths):
    return np.split(w, np.cumsum(widths)[:-1], axis=1)


def _mix2_slabs(w_in, w_nsa, w_ret, w_out):
    w = _split_cols(w_in, (512, 128, 128, 128, 128, 128, 128, 24, 512, 512, 512, 512, 1024, 1024))
    nq, kc, vc, ks, vs, kw, vw, gates, rq, rk, rv, rg, ga, gb = w
    pairs = [h for j in range(NP) for h in (j, NP + j)]
    nq = nq.reshape(D, 8, 64)[:, pairs].reshape(D, 512)
    w_nsa = w_nsa.reshape(8, 64, D)[pairs].reshape(512, D)
    narrow = np.zeros((D, P), np.float32)
    narrow[:, 0:24] = gates
    t = _tiles
    gb = t(gb)
    return [t(kc), t(vc), t(ks), t(vs), t(kw), t(vw), t(narrow),
            _interleave((t(nq), 1), (t(ga), 2), (gb[:4], 1)),
            _interleave((t(rq), 1), (t(rk), 1), (t(rv), 1), (t(rg), 1)),
            gb[4:], t(np.concatenate([w_nsa, w_ret])), t(w_out)]


def _ada_pieces(w):
    return w.reshape(KT, P, 36, 256).transpose(2, 1, 0, 3)


def _constants():
    f = np.float32
    c = {"ident": np.eye(P, dtype=f)}
    p, j = np.arange(P)[:, None], np.arange(P)[None, :]
    levels = [((p // b == j // b) & (p % b < b // 2) & (j % b >= b // 2)) for b in LEVELS] + [p == j]
    c["lmask"] = np.stack(levels, 1).astype(np.int32)
    c["segm"] = np.broadcast_to((np.arange(T) % P != 0).astype(f), (P, T)).copy()
    tri = np.where(j <= p, 0, NEG).astype(f)
    c["trib"] = tri.astype(mybir.dt.np(BF16))
    c["identb"] = c["ident"].astype(mybir.dt.np(BF16))
    c["causal"] = np.concatenate([np.zeros((P, T - P), f), tri], 1)
    t = np.arange(T).reshape(TT, P).T[:, :, None]
    end = (np.arange(NC) * 16 + 31)[None, None, :]
    c["cmask"] = np.where(end <= t, 0, NEG).astype(f)
    c["cvalid"] = (t[:, :, 0] >= 31).astype(f)
    inv = (f(10000.0) ** (-np.arange(32, dtype=f) / f(32))).astype(f)
    ang = (np.arange(T, dtype=f)[None, :] * np.tile(inv, 4)[:, None]).astype(f)
    c["rcos"], c["rsin"] = np.cos(ang).astype(f), np.sin(ang).astype(f)
    rot = np.zeros((P, P), f)
    for b in range(0, P, 64):
        for d in range(32):
            rot[b + 32 + d, b + d] = -1
            rot[b + d, b + 32 + d] = 1
    c["rrot"] = rot
    c["rblk"] = np.kron(np.eye(2), np.full((64, 64), 1 / 64)).astype(f)
    g = np.log1p(-2.0 ** (-5.0 - np.arange(8)))[:, None, None]
    diff = np.arange(T)[None, None, :] - np.arange(P)[None, :, None]
    c["rdec"] = np.where(diff >= 0, np.exp(g * np.maximum(diff, 0)), 0).astype(f)
    return c


def _layout(i):
    def c(v):
        return np.asarray(v, np.float32).reshape(-1, P).T
    b_f = np.zeros((P, 1), np.float32)
    b_f[32:48, 0] = i["b_f"][0]
    table = {"c1": c(i["c"]), "c2": c(i["c_2"]), "b_ada1": c(i["b_ada"]), "b_ada2": c(i["ada_b_2"]),
             "g_pre": c(i["g_pre"]), "g_post": c(i["g_post"]), "norm1": c(i["norm1_w_2"]), "norm2": c(i["norm2_w_2"]),
             "norm3": c(i["norm3_w_2"]), "final": c(i["final_norm_w_2"]), "b_a": c(i["b_a"]), "g_gla": c(i["g_gla"]),
             "b_f": b_f, "ret_norm": c(i["ret_norm_w_2"])}
    arrays = {"cols": np.concatenate([table[n] for n in COLS], 1)}
    slabs = (_ffn_slabs(i["w_gu1"][0], i["w_dn1"][0])
             + _mix1_slabs(i["w_in"][0], i["w_pa"][0], i["w_pb"][0], i["w_out"][0])
             + _ffn_slabs(i["w_gu2"][0], i["w_dn2"][0])
             + _ffn_slabs(i["ffn1_w_in_2"][0], i["ffn1_w_out_2"][0])
             + _mix2_slabs(i["w_in_2"][0], i["w_nsa_up_2"][0], i["w_ret_up_2"][0], i["w_out_2"][0])
             + _ffn_slabs(i["ffn2_w_in_2"][0], i["ffn2_w_out_2"][0]))
    arrays["slabs"] = np.concatenate(slabs)
    arrays["ada"] = np.concatenate([_ada_pieces(i["w_ada"][0]), _ada_pieces(i["ada_w_2"][0])])
    arrays["xt"] = i["x"][0].T.reshape(KT, P, T).transpose(1, 0, 2)
    arrays["w_a2"] = i["w_a2"][0]
    w1 = np.stack([i["cmp_k_w1_2"][0], i["cmp_v_w1_2"][0]]).reshape(2, 2, 16, 64, P)
    arrays["w1"] = w1.transpose(1, 3, 0, 2, 4).reshape(P, 2, 16, P)
    arrays["w2"] = np.stack([i["cmp_k_w2_2"][0], i["cmp_v_w2_2"][0]], 1)
    pe = np.stack([i["cmp_k_pe_2"][0].T, i["cmp_v_pe_2"][0].T], 1)
    arrays["cpe"] = np.concatenate([pe, pe])
    arrays.update(_constants())
    return {k: np.ascontiguousarray(v) for k, v in arrays.items()}


def kernel(**inputs):
    import concourse.bacc as bacc
    from concourse.bass_utils import run_bass_kernel_spmd

    arrays = _layout({k: np.asarray(v) for k, v in inputs.items()})
    nc = bacc.Bacc("TRN2", target_bir_lowering=False, num_devices=1)
    tensors = {k: nc.dram_tensor(k + "_dram", v.shape, mybir.dt.from_np(v.dtype), kind="ExternalInput").ap()
               for k, v in arrays.items()}
    tensors["out"] = nc.dram_tensor("out_dram", (P, KT, T), F32, kind="ExternalOutput").ap()
    tensors["fneg_dram"] = nc.dram_tensor("fneg_scratch", (16, T), F32, kind="Internal").ap()
    build(nc, tensors)
    r = run_bass_kernel_spmd(nc, [{k + "_dram": v for k, v in arrays.items()}], core_ids=[0])
    out = r.results[0]["out_dram"]
    return out.transpose(2, 1, 0).reshape(1, T, D)
```
